# Optimizing a Trainium2 kernel written in Bass

```python
import math
import jax
import jax.numpy as jnp
from jax import lax
import numpy as np

D_MODEL = 2048
BATCH = 1
SEQ = 256
DEPTH = 2

N_MIXERS = 2
N_ATT_LAYERS = (DEPTH + 1) // 2
N_REC_LAYERS = DEPTH // 2
NORM_EPS = 1e-6
MASK_VALUE = -1e30
LB_FLOOR = 1e-30

DILATED_GROUPS = ((128, 1), (512, 4), (2048, 16))
N_GROUPS = len(DILATED_GROUPS)
ATT_HEAD_DIM = 128
ATT_HEADS_PER_GROUP = D_MODEL // 256
ATT_BLOCK = 128
ROPE_THETA = 500000.0
ROPE_DIM = ATT_HEAD_DIM // 4
ATT_IN_WIDTH = N_GROUPS * 3 * ATT_HEADS_PER_GROUP * ATT_HEAD_DIM
ATT_OUT_WIDTH = ATT_HEADS_PER_GROUP * ATT_HEAD_DIM

HGRN_EXPAND = 128
HGRN_HEADS = D_MODEL // HGRN_EXPAND
HGRN_DK = HGRN_EXPAND
HGRN_DV = D_MODEL // HGRN_HEADS
HGRN_CHUNK = 16
HGRN_IN_WIDTH = 4 * D_MODEL

D_FF = 4 * D_MODEL

kernel_name = "hybrid_dilated_attn_hgrn2_trunk"

def rms_norm(x, g):
    xf = x.astype(jnp.float32)
    xf = xf * lax.rsqrt(jnp.mean(xf * xf, axis=-1, keepdims=True) + NORM_EPS)
    return xf.astype(x.dtype) * g

def partial_rope(x, positions):
    half = ROPE_DIM // 2
    inv_freq = ROPE_THETA ** (-jnp.arange(half, dtype=jnp.float32) / half)
    ang = positions.astype(jnp.float32)[..., None] * inv_freq
    cos = jnp.cos(ang)[:, :, None, :]
    sin = jnp.sin(ang)[:, :, None, :]
    xr = x[..., :ROPE_DIM].astype(jnp.float32)
    x1, x2 = xr[..., :half], xr[..., half:]
    rot = jnp.concatenate([x1 * cos - x2 * sin, x2 * cos + x1 * sin], axis=-1).astype(x.dtype)
    return jnp.concatenate([rot, x[..., ROPE_DIM:]], axis=-1)

def strided_window_attention(q, k, v, dilation, steps):
    B, S, H, dh = q.shape
    L = S // dilation
    N = B * dilation
    nb = -(-L // ATT_BLOCK)
    pad = nb * ATT_BLOCK - L

    def to_blocks(t):
        t = t.reshape(B, L, dilation, H, dh).transpose(0, 2, 1, 3, 4).reshape(N, L, H, dh)
        t = jnp.pad(t, ((0, 0), (0, pad), (0, 0), (0, 0)))
        return t.reshape(N, nb, ATT_BLOCK, H, dh)

    def with_prev(t):
        prev = jnp.concatenate([jnp.zeros_like(t[:, :1]), t[:, :-1]], axis=1)
        return jnp.concatenate([prev, t], axis=2)

    qb = to_blocks(q)
    kk = with_prev(to_blocks(k))
    vv = with_prev(to_blocks(v))

    scores = jnp.einsum('nbqhd,nbkhd->nbhqk', qb, kk).astype(jnp.float32) * (dh ** -0.5)
    blk = jnp.arange(nb)[:, None, None]
    qi = jnp.arange(ATT_BLOCK)[None, :, None] + ATT_BLOCK
    kj = jnp.arange(2 * ATT_BLOCK)[None, None, :]
    dist = qi - kj
    mask = (dist >= 0) & (dist <= steps) & ((blk > 0) | (kj >= ATT_BLOCK))
    scores = jnp.where(mask[None, :, None], scores, MASK_VALUE)
    m = jnp.max(scores, axis=-1, keepdims=True)
    p = jnp.exp(scores - m)
    l = jnp.sum(p, axis=-1, keepdims=True)
    out = jnp.einsum('nbhqk,nbkhd->nbqhd', (p / l).astype(v.dtype), vv)
    lse = (m + jnp.log(l))[..., 0]

    out = out.reshape(N, nb * ATT_BLOCK, H, dh)[:, :L]
    out = out.reshape(B, dilation, L, H, dh).transpose(0, 2, 1, 3, 4).reshape(B, S, H, dh)
    lse = lse.transpose(0, 1, 3, 2).reshape(N, nb * ATT_BLOCK, H)[:, :L]
    lse = lse.reshape(B, dilation, L, H).transpose(0, 2, 1, 3).reshape(B, S, H)
    return out, lse

def dilated_attention_mixer(u, positions, w_in, w_out):
    B, S, _ = u.shape
    proj = (u @ w_in).reshape(B, S, N_GROUPS, 3, ATT_HEADS_PER_GROUP, ATT_HEAD_DIM)
    outs, lses = [], []
    for g, (window, dilation) in enumerate(DILATED_GROUPS):
        q = partial_rope(proj[:, :, g, 0], positions)
        k = partial_rope(proj[:, :, g, 1], positions)
        v = proj[:, :, g, 2]
        o, lse = strided_window_attention(q, k, v, dilation, window // dilation)
        outs.append(o)
        lses.append(lse)
    w = jax.nn.softmax(jnp.stack(lses, axis=0), axis=0)
    o = jnp.sum(w[..., None] * jnp.stack(outs, axis=0).astype(jnp.float32), axis=0)
    return o.astype(u.dtype).reshape(B, S, ATT_OUT_WIDTH) @ w_out

def hgrn2_mixer(u, lower_bound, out_norm_g, w_in, w_out):
    B, S, _ = u.shape
    H, C = HGRN_HEADS, HGRN_CHUNK
    nC = S // C
    proj = (u @ w_in).reshape(B, S, 4, H, HGRN_DK)
    q, f_pre, i_val, gate = proj[:, :, 0], proj[:, :, 1], proj[:, :, 2], proj[:, :, 3]
    lb = lower_bound.astype(jnp.float32).reshape(H, HGRN_DK)
    log_f = jnp.logaddexp(jnp.log(jnp.maximum(lb, LB_FLOOR)),
                          jnp.log1p(-lb) + jax.nn.log_sigmoid(f_pre.astype(jnp.float32)))
    k = -jnp.expm1(log_f)

    def chunks(t):
        return t.astype(jnp.float32).reshape(B, nC, C, H, t.shape[-1]).transpose(1, 0, 3, 2, 4)

    causal = jnp.tril(jnp.ones((C, C), dtype=bool))[None, None, :, :, None]

    def step(state, inp):
        q_c, k_c, v_c, g_c = inp
        b = jnp.cumsum(g_c, axis=2)
        inter = jnp.einsum('bhtk,bhkv->bhtv', q_c * jnp.exp(b), state)
        diff = b[:, :, :, None, :] - b[:, :, None, :, :]
        decay = jnp.exp(jnp.where(causal, diff, MASK_VALUE))
        a = jnp.einsum('bhtk,bhsk,bhtsk->bhts', q_c, k_c, decay)
        intra = jnp.einsum('bhts,bhsv->bhtv', a, v_c)
        b_last = b[:, :, -1:, :]
        new_state = jnp.exp(b_last[:, :, 0, :])[..., None] * state + jnp.einsum(
            'bhsk,bhsv->bhkv', k_c * jnp.exp(b_last - b), v_c)
        return new_state, inter + intra

    state0 = jnp.zeros((B, H, HGRN_DK, HGRN_DV), jnp.float32)
    _, o = lax.scan(step, state0, (chunks(q), chunks(k), chunks(i_val), chunks(log_f)))
    o = o.transpose(1, 0, 3, 2, 4).reshape(B, S, H, HGRN_DV)
    o = rms_norm(o, out_norm_g) * jax.nn.silu(gate.astype(jnp.float32))
    return o.reshape(B, S, H * HGRN_DV).astype(u.dtype) @ w_out

def squared_relu_mlp(u, w1, w2):
    return jnp.square(jax.nn.relu(u @ w1)) @ w2

def setup_inputs(seed: int = 0) -> dict:
    key = jax.random.key(seed)
    ks = jax.random.split(key, 12)
    f32 = jnp.float32
    x = jax.random.normal(ks[0], (BATCH, SEQ, D_MODEL), f32)
    offsets = jax.random.randint(ks[1], (BATCH, 1), 0, 4096, dtype=jnp.int32)
    positions = offsets + jnp.arange(SEQ, dtype=jnp.int32)[None, :]
    norm_gains = 1.0 + 0.02 * jax.random.normal(ks[2], (DEPTH, 4, D_MODEL), f32)
    w_att_in = jax.random.normal(ks[3], (N_ATT_LAYERS, D_MODEL, ATT_IN_WIDTH), f32) * D_MODEL ** -0.5
    w_att_out = jax.random.normal(ks[4], (N_ATT_LAYERS, ATT_OUT_WIDTH, D_MODEL), f32) * ATT_OUT_WIDTH ** -0.5
    w_rec_in = jax.random.normal(ks[5], (N_REC_LAYERS, D_MODEL, HGRN_IN_WIDTH), f32) * D_MODEL ** -0.5
    rec_lower_bounds = 0.5 * jax.random.normal(ks[6], (N_REC_LAYERS, HGRN_HEADS * HGRN_DK), f32)
    rec_out_norm = 1.0 + 0.02 * jax.random.normal(ks[7], (N_REC_LAYERS, HGRN_DV), f32)
    w_rec_out = jax.random.normal(ks[8], (N_REC_LAYERS, HGRN_HEADS * HGRN_DV, D_MODEL), f32) * D_MODEL ** -0.5
    w_ff1 = jax.random.normal(ks[9], (DEPTH, D_MODEL, D_FF), f32) * D_MODEL ** -0.5
    w_ff2 = jax.random.normal(ks[10], (DEPTH, D_FF, D_MODEL), f32) * D_FF ** -0.5
    return {"x": x, "positions": positions, "norm_gains": norm_gains,
            "w_att_in": w_att_in, "w_att_out": w_att_out,
            "w_rec_in": w_rec_in, "rec_lower_bounds": rec_lower_bounds,
            "rec_out_norm": rec_out_norm, "w_rec_out": w_rec_out,
            "w_ff1": w_ff1, "w_ff2": w_ff2}

def reference(x, positions, norm_gains, w_att_in, w_att_out, w_rec_in, rec_lower_bounds,
              rec_out_norm, w_rec_out, w_ff1, w_ff2):
    lb = jax.nn.softmax(rec_lower_bounds.astype(jnp.float32), axis=0)
    lb = jnp.cumsum(lb, axis=0) - lb[0:1]
    h = x
    for layer in range(DEPTH):
        g = norm_gains[layer]
        u = rms_norm(h, g[0])
        j = layer // N_MIXERS
        if layer % N_MIXERS == 0:
            y = dilated_attention_mixer(u, positions, w_att_in[j], w_att_out[j])
        else:
            y = hgrn2_mixer(u, lb[j], rec_out_norm[j], w_rec_in[j], w_rec_out[j])
        h = h + rms_norm(y, g[1])
        u = rms_norm(h, g[2])
        h = h + rms_norm(squared_relu_mlp(u, w_ff1[layer], w_ff2[layer]), g[3])
    return h


_drawn_inputs = setup_inputs


def setup_inputs(seed=0):
    import zlib

    import numpy as np

    out = dict(_drawn_inputs(seed))
    spreads = {}
    factors = {}
    for name, (base, spread) in spreads.items():
        noise = np.random.default_rng([zlib.crc32(name.encode()), seed]).standard_normal(out[name].shape)
        drawn = base * np.exp(spread * noise) if base else spread * noise
        out[name] = jnp.asarray(drawn.astype(out[name].dtype))
    for name, factor in factors.items():
        out[name] = (out[name] * factor).astype(out[name].dtype)
    return out
```

```python
from contextlib import ExitStack

import numpy as np

import concourse.bass as bass
from concourse import mybir

F32 = mybir.dt.float32
F32R = mybir.dt.float32r
I32 = mybir.dt.int32
U32 = mybir.dt.uint32
ALU = mybir.AluOpType
ACT = mybir.ActivationFunctionType
AX = mybir.AxisListType

P = 128
TOK = 256
HALVES = TOK // P
D = 2048
KC = D // P
NB = 512
KK = 2
RAW = 8
SPLIT = 4
COLS = D // NB

ATT_HEADS = 8
GROUPS = 3
DILATION = (1, 4, 16)
WINDOW = (128, 512, 2048)
ATT_W = 3 * P
ATT_BLOCK_TILES = KC // KK
ATT_TILES = GROUPS * ATT_BLOCK_TILES
HALF_ROPE = 16
ROPE_THETA = 500000.0
MASKED = -1e30

REC_HEADS = 16
REC_TILES = KC // KK
LEVELS = 8
MASK_LEVELS = 5
SCORES = MASK_LEVELS * P // 2 + P
LB_FLOOR = 1e-30
EXP_CAP = 1e37

FF_BLOCKS = 16
FF_TILES = 8
EPS = 1e-6

AT_ATT = 0
AT_ATT_OUT = AT_ATT + ATT_HEADS * ATT_TILES
AT_FF0 = AT_ATT_OUT + ATT_HEADS // 4 * COLS * 2
AT_REC = AT_FF0 + FF_BLOCKS * 2 * FF_TILES
AT_REC_OUT = AT_REC + REC_HEADS * REC_TILES
AT_FF1 = AT_REC_OUT + REC_HEADS // 4 * COLS * 2
TILES = AT_FF1 + FF_BLOCKS * 2 * FF_TILES


class Steps:

    def __init__(self, eng, sem, base=0):
        self.eng, self.sem, self.base, self.count = eng, sem, base, 0

    def note(self, ins):
        ins.then_inc(self.sem, 1)
        self.count += 1
        return self.base + self.count

    def last(self):
        self.eng.wait_ge(self.sem, self.base + self.count)

    def link(self, ins):
        self.note(ins)
        self.last()


def hybrid_trunk(nc, x, positions, norm_gains, lower_bound, rec_gain, s_att_in, s_att_out,
                 s_rec_in, s_rec_out, s_up, s_down, out):
    with ExitStack() as ctx:
        def sb(name, shape, dt=F32):
            return ctx.enter_context(nc.sbuf_tensor(name, shape, dt))

        def psum(name, shape):
            return ctx.enter_context(nc.psum_tensor(name, shape, F32))

        def sem(name):
            return ctx.enter_context(nc.semaphore(name))

        raw = sb("raw", [P, RAW, KK * NB])
        w_hi = sb("w_hi", [P, SPLIT, KK * NB], F32R)
        w_lo = sb("w_lo", [P, SPLIT, KK * NB], F32R)
        u_hi = sb("u_hi", [P, KC, TOK], F32R)
        u_lo = sb("u_lo", [P, KC, TOK], F32R)
        c_hi = sb("c_hi", [P, REC_HEADS, TOK], F32R)
        c_lo = sb("c_lo", [P, REC_HEADS, TOK], F32R)
        h = sb("h", [P, HALVES, D])
        y = sb("y", [P, HALVES, D])
        gain_post = sb("gain_post", [P, D])
        gain_pre = sb("gain_pre", [P, D])
        ident = sb("ident", [P, P])
        junk = sb("junk", [P, NB], mybir.dt.bfloat16)
        stat = sb("stat", [P, 64])
        mix = sb("mix", [P, 7168])
        rope = sb("rope", [P, 2, HALVES, HALF_ROPE])
        pos_i = sb("pos_i", [P, HALVES], I32)
        bounds = sb("bounds", [P, 5, REC_HEADS])
        rgain = sb("rgain", [P, P])

        def carve(at, *shape):
            n = int(np.prod(shape))
            v = mix[:, at:at + n]
            if len(shape) == 2:
                v = v.rearrange("p (a b) -> p a b", a=shape[0])
            if len(shape) == 3:
                v = v.rearrange("p (a b c) -> p a b c", a=shape[0], b=shape[1])
            return v

        ssq_y = stat[:, 0:8].rearrange("p (m c) -> p m c", m=HALVES)
        ssq_h = stat[:, 8:16].rearrange("p (m c) -> p m c", m=HALVES)
        mean_y = stat[:, 16:18]
        rstd_y = stat[:, 18:20]
        mean_h = stat[:, 20:22]
        rstd_u = stat[:, 22:24]
        eps_col = stat[:, 24:25]

        az = carve(0, HALVES, 9, P)
        a_qkT = carve(2304, GROUPS, NB)
        a_v = carve(3840, HALVES, GROUPS, P)
        a_p = carve(4608, 768)
        a_pT = carve(5376, 768)
        a_o = carve(6144, HALVES, P)
        a_cosx = carve(4608, 9 * 32)
        a_sinx = carve(4896, 9 * 32)
        amask = carve(6400, GROUPS, TOK)
        a_max = stat[:, 26:28]
        a_sum = stat[:, 28:30]
        a_rsum = stat[:, 30:32]

        rz = carve(0, HALVES, NB)
        r_q = carve(1024, TOK)
        r_e = carve(1280, TOK)
        r_d = carve(1536, TOK)
        r_f = carve(1792, TOK)
        r_R = carve(2048, LEVELS, P)
        r_K = carve(3072, LEVELS, TOK)
        r_tot = carve(5120, 2 * TOK)
        r_A = carve(5632, GROUPS * P)
        r_eg = carve(6016, HALVES, P)
        r_G = carve(6272, HALVES, P)
        r_o = carve(6528, HALVES, P)
        rmask = sb("rmask", [P, SCORES], mybir.dt.bfloat16)
        r_prod = carve(2048, HALVES, SCORES)
        r_ms = stat[:, 32:34]
        r_ln = stat[:, 34:36]
        r_rs = stat[:, 36:38]
        r_x = stat[:, 38:40]
        r_t = stat[:, 40:42]

        m_h = carve(0, HALVES, NB)
        hid_hi, hid_lo = c_hi[:, 0:4, :], c_lo[:, 0:4, :]

        pairA = psum("pairA", [P, HALVES, NB])
        pairB = psum("pairB", [P, HALVES, NB])
        pairS = psum("pairS", [P, HALVES, NB])
        bankX = psum("bankX", [P, NB])
        bankO = psum("bankO", [P, NB])
        turn_bank = [bankX[:], bankO[:], pairS[:, 0], pairS[:, 1]]

        landed = [sem(f"landed{s}") for s in range(RAW)]
        hi_made, lo_made, tiles_used = sem("hi_made"), sem("lo_made"), sem("tiles_used")
        x_in, pos_in, bound_in, rgain_in = sem("x_in"), sem("pos_in"), sem("bound_in"), sem("rgain_in")
        pre_in, post_in = sem("pre_in"), sem("post_in")
        out_sent = sem("out_sent")
        ident_ready, masks_ready, pool_steps = sem("ident_ready"), sem("masks_ready"), sem("pool_steps")
        v_setup, act_setup = sem("v_setup"), sem("act_setup")
        amask_ready, angle_ready, sines_ready, rope_ready = (
            sem("amask_ready"), sem("angle_ready"), sem("sines_ready"), sem("rope_ready"))
        bexp_in, bexp_out = sem("bexp_in"), sem("bexp_out")
        zmem = sem("zmem")

        def norm_sems(b):
            names = ("ssq_y_made", "mean_y_made", "root_y_made", "h_new", "hg_made", "turned", "u_hi_made",
                     "u_lo_made", "ssq_h_made", "mean_h_made", "root_h_made", "rstd_u_made", "steps")
            return {n: sem(f"n{b}_{n}") for n in names}

        NORM = [norm_sems(b) for b in range(5)]

        a_half = sem("a_half")
        a_evac = sem("a_evac")
        a_rot = sem("a_rot")
        a_vcopied = sem("a_vcopied")
        a_turned = sem("a_turned")
        a_qk = sem("a_qk")
        a_scored = sem("a_scored")
        a_maxed = sem("a_maxed")
        a_probs = sem("a_probs")
        a_rs = sem("a_rs")
        a_pturned = sem("a_pturned")
        a_pt = sem("a_pt")
        a_pv = sem("a_pv")
        a_out = sem("a_out")
        a_oturned = sem("a_oturned")
        a_ohi = sem("a_ohi")
        a_olo = sem("a_olo")
        a_steps = sem("a_steps")

        r_half, r_evac, r_qfT, r_exp, r_qcopied, r_expg = (
            sem("r_half"), sem("r_evac"), sem("r_qfT"), sem("r_exp"), sem("r_qcopied"), sem("r_expg"))
        r_levels, r_scored, r_att, r_across = sem("r_levels"), sem("r_scored"), sem("r_att"), sem("r_across")
        r_pv, r_ssq, r_logged, r_root, r_out = (
            sem("r_pv"), sem("r_ssq"), sem("r_logged"), sem("r_root"), sem("r_out"))
        r_oturned, r_ohi, r_olo, r_steps = sem("r_oturned"), sem("r_ohi"), sem("r_olo"), sem("r_steps")
        r_gate = sem("r_gate")

        y_add = [sem(f"y_add{b}") for b in range(4)]
        f_half = [sem(f"f_half{b}") for b in range(2)]
        f_relu = [sem(f"f_relu{b}") for b in range(2)]
        f_hid = [sem(f"f_hid{b}") for b in range(2)]
        f_turned = [sem(f"f_turned{b}") for b in range(2)]
        f_hi = [sem(f"f_hi{b}") for b in range(2)]
        f_lo = [sem(f"f_lo{b}") for b in range(2)]

        block = ctx.enter_context(nc.Block())

        @block.sync
        def _(sp):
            def load(stream, width, index, base, i, per, t):
                slot = (base + t) % RAW
                at = index if isinstance(index, int) else sp.snap(index)
                if base + t >= RAW or not isinstance(i, int) or i:
                    sp.wait_ge(lo_made, i * per + (base + t - RAW + 1))
                src = stream[at] if isinstance(at, int) else stream[bass.ds(at, 1)].squeeze(0)
                sp.dma_start(raw[:, slot, 0:width], src).then_inc(landed[slot], 16)

            def gains(b, post, pre):
                if b > 0:
                    sp.wait_ge(NORM[b - 1]["hg_made"], COLS * HALVES)
                if post is not None:
                    sp.dma_start(gain_post[:], post.partition_broadcast(P)).then_inc(post_in, 16)
                if pre is not None:
                    sp.dma_start(gain_pre[:], pre.partition_broadcast(P)).then_inc(pre_in, 16)

            def mlp_loads(layer, base):
                for t in range(FF_TILES):
                    load(s_up, KK * NB, layer * P + t, base, 0, 0, t)
                gains(2 + 2 * layer, norm_gains[layer, 3], norm_gains[1, 0] if layer == 0 else None)
                with sp.Fori(0, FF_BLOCKS - 1) as i:
                    for t in range(FF_TILES):
                        load(s_up, KK * NB, i * FF_TILES + (layer * P + FF_TILES + t),
                             base + FF_TILES, i, 2 * FF_TILES, t)
                    for t in range(FF_TILES):
                        load(s_down, KK * NB, i * FF_TILES + (layer * P + t),
                             base + 2 * FF_TILES, i, 2 * FF_TILES, t)
                for t in range(FF_TILES):
                    load(s_down, KK * NB, layer * P + (FF_BLOCKS - 1) * FF_TILES + t,
                         base + (2 * FF_BLOCKS - 1) * FF_TILES, 0, 0, t)

            for m in range(HALVES):
                sp.dma_start(h[:, m, :], x[m * P:(m + 1) * P, :]).then_inc(x_in, 16)
            gains(0, None, norm_gains[0, 0])
            for t in range(RAW):
                load(s_att_in, KK * ATT_W, t, AT_ATT, 0, 0, t)
            sp.dma_start(pos_i[:], positions).then_inc(pos_in, 16)
            sp.dma_start(bounds[:, 0, :], lower_bound).then_inc(bound_in, 16)
            sp.dma_start(rgain[:], rec_gain[0].partition_broadcast(P)).then_inc(rgain_in, 16)
            gains(1, norm_gains[0, 1], norm_gains[0, 2])
            for t in range(RAW, ATT_TILES):
                load(s_att_in, KK * ATT_W, t, AT_ATT, 0, 0, t)
            with sp.Fori(1, ATT_HEADS) as hd:
                for t in range(ATT_TILES):
                    load(s_att_in, KK * ATT_W, hd * ATT_TILES + t, AT_ATT, hd, ATT_TILES, t)
            for t in range(AT_FF0 - AT_ATT_OUT):
                load(s_att_out, KK * NB, t, AT_ATT_OUT, 0, 0, t)
            mlp_loads(0, AT_FF0)
            for t in range(REC_TILES):
                load(s_rec_in, KK * NB, t, AT_REC, 0, 0, t)
            gains(3, norm_gains[1, 1], norm_gains[1, 2])
            with sp.Fori(1, REC_HEADS) as hd:
                for t in range(REC_TILES):
                    load(s_rec_in, KK * NB, hd * REC_TILES + t, AT_REC, hd, REC_TILES, t)
            for t in range(AT_FF1 - AT_REC_OUT):
                load(s_rec_out, KK * NB, t, AT_REC_OUT, 0, 0, t)
            mlp_loads(1, AT_FF1)
            for c in range(COLS):
                sp.wait_ge(NORM[4]["h_new"], HALVES * (c + 1))
                sp.dma_start(out.rearrange("(m p) d -> p m d", p=P)[:, :, c * NB:(c + 1) * NB],
                             h[:, :, c * NB:(c + 1) * NB]).then_inc(out_sent, 16)
            sp.wait_ge(out_sent, 16 * COLS)

        @block.gpsimd
        def _(pool):
            pool_s = Steps(pool, pool_steps)
            pool_s.note(nc.gpsimd.memset(ident[:], 0.0))
            pool_s.note(nc.gpsimd.memset(amask, 0.0))
            pool_s.note(nc.gpsimd.memset(rmask[:], 1.0))
            pool_s.last()
            nc.gpsimd.affine_select(out=ident[:], in_=ident[:], compare_op=ALU.not_equal, fill=1.0, base=0,
                                    pattern=[[-1, P]], channel_multiplier=1).then_inc(ident_ready, 1)
            pool_s.link(nc.gpsimd.affine_select(out=amask, in_=amask, compare_op=ALU.is_ge, fill=MASKED,
                                                base=P, pattern=[[0, GROUPS], [-1, TOK]], channel_multiplier=1))
            for g in range(GROUPS):
                if WINDOW[g] < TOK:
                    pool_s.link(nc.gpsimd.affine_select(
                        out=amask[:, g, :], in_=amask[:, g, :], compare_op=ALU.is_ge, fill=MASKED,
                        base=WINDOW[g] - P, pattern=[[1, TOK]], channel_multiplier=-1))
            for j in range(MASK_LEVELS):
                w = 1 << j
                view = rmask[:, j * 64:(j + 1) * 64].rearrange("p (b w) -> p b w", w=w)
                pool_s.link(nc.gpsimd.affine_select(out=view, in_=view, compare_op=ALU.is_ge, fill=0.0, base=0,
                                                    pattern=[[-2 * w, P // 2 // w], [0, w]], channel_multiplier=1))
                pool_s.link(nc.gpsimd.affine_select(out=view, in_=view, compare_op=ALU.is_ge, fill=0.0, base=w - 1,
                                                    pattern=[[2 * w, P // 2 // w], [0, w]], channel_multiplier=-1))
            pool_s.link(nc.gpsimd.affine_select(out=rmask[:, SCORES - P:SCORES], in_=rmask[:, SCORES - P:SCORES],
                                                compare_op=ALU.is_equal, fill=0.0, base=0,
                                                pattern=[[-1, P]], channel_multiplier=1))
            nc.gpsimd.memset(eps_col, EPS).then_inc(masks_ready, 1)
            for layer in range(2):
                pool.wait_ge(NORM[1 + 2 * layer]["u_lo_made"], COLS * HALVES)
                for m in range(HALVES):
                    nc.gpsimd.memset(y[:, m, :], 0.0).then_inc(y_add[1 + 2 * layer], 1)

        @block.tensor
        def _(pe):
            def three_pass(dst, s_hi, s_lo, slot, kk, width, first, last):
                wh = w_hi[:, slot, kk * width:(kk + 1) * width]
                wl = w_lo[:, slot, kk * width:(kk + 1) * width]
                pe.matmul(dst, s_hi, wh, start=first, stop=False)
                pe.matmul(dst, s_hi, wl, start=False, stop=False)
                return pe.matmul(dst, s_lo, wh, start=False, stop=last)

            def tile(pair, s_hi, s_lo, chunk0, at, i, per, width, first, last, half_sem=None, free=None):
                slot = at % SPLIT
                pe.wait_ge(lo_made, i * per + (at + 1))
                for m in range(HALVES):
                    if first and free is not None:
                        free(m)
                    for kk in range(KK):
                        k = chunk0 + kk
                        mm = three_pass(pair[:, m, 0:width], s_hi[:, k, m * P:(m + 1) * P],
                                        s_lo[:, k, m * P:(m + 1) * P], slot, kk, width,
                                        first and kk == 0, last and kk == KK - 1)
                    if m == 0 and last and half_sem is not None:
                        mm.then_inc(half_sem, 1)
                mm.then_inc(tiles_used, 1)

            def turn_boundary(b):
                n = NORM[b]
                if b == 0:
                    pe.wait_ge(ident_ready, 1)
                for c in range(COLS):
                    for m in range(HALVES):
                        q = c * HALVES + m
                        pe.wait_ge(n["hg_made"], q + 1)
                        if q >= 4:
                            pe.wait_ge(n["u_lo_made"], q - 3)
                        for j in range(4):
                            t = pe.transpose(turn_bank[q % 4][:, j * P:(j + 1) * P],
                                             y[:, m, c * NB + j * P:c * NB + (j + 1) * P], ident[:])
                        t.then_inc(n["turned"], 1)

            def wait_u(b, t):
                pe.wait_ge(NORM[b]["u_lo_made"], HALVES * (t * KK // 4 + 1))

            def att_turn(hp, g):
                if g == 0:
                    pe.wait_ge(a_rot, hp + 1)
                if g == 2:
                    pe.wait_ge(a_qk, hp * 3 + 1)
                bank = bankO if g == 1 else bankX
                for j in range(4):
                    src = az[:, j % 2, 3 * g + j // 2, :]
                    t = pe.transpose(bank[:, j * P:(j + 1) * P], src, ident[:])
                t.then_inc(a_turned, 1)

            def att_scores(hp, m):
                if m == 1:
                    pe.wait_ge(a_qk, hp * 3 + 3)
                keys = (m + 1) * P
                flat = pairS[:].rearrange("p m n -> p (m n)")
                for g in range(GROUPS):
                    mm = pe.matmul(flat[:, g * keys:(g + 1) * keys], a_qkT[:, g, m * P:(m + 1) * P],
                                   a_qkT[:, g, TOK:TOK + keys], start=True, stop=True)
                mm.then_inc(a_scored, 1)

            def att_turn_probs(hp, m):
                pe.wait_ge(a_probs, hp * 2 + (2 - m))
                flat = pairS[:].rearrange("p m n -> p (m n)")
                for j in range(GROUPS * (m + 1)):
                    t = pe.transpose(flat[:, j * P:(j + 1) * P], a_p[:, j * P:(j + 1) * P], ident[:])
                t.then_inc(a_pturned, 1)

            def att_pv(hp, m):
                pe.wait_ge(a_pt, hp * 2 + (2 - m))
                pe.wait_ge(a_vcopied, hp + 1)
                if m == 0:
                    pe.wait_ge(a_out, hp * 2 + 1)
                n = GROUPS * (m + 1)
                for j in range(n):
                    mm = pe.matmul(bankO[:, m * P:(m + 1) * P], a_pT[:, j * P:(j + 1) * P],
                                   a_v[:, j % (m + 1), j // (m + 1), :], start=(j == 0), stop=(j == n - 1))
                mm.then_inc(a_pv, 1)

            def att_turn_out(hp):
                pe.wait_ge(a_out, hp * 2 + 2)
                for m in range(HALVES):
                    t = pe.transpose(bankX[:, m * P:(m + 1) * P], a_o[:, m, :], ident[:])
                t.then_inc(a_oturned, 1)

            def att_block_free(hd, g):
                def free(m):
                    back = {0: 1, 1: 3, 2: 2}[g]
                    if not isinstance(hd, int) or hd * 3 + g - back >= 0:
                        pe.wait_ge(a_evac, hd * 6 + ((g - back) * 2 + 1 + m))
                return free

            def att_project(hd, prev):
                for t in range(ATT_TILES):
                    g, tb = divmod(t, ATT_BLOCK_TILES)
                    if isinstance(hd, int) and hd == 0 and g == 0:
                        wait_u(0, tb)
                    tile(pairB if g == 1 else pairA, u_hi, u_lo, tb * KK, AT_ATT + t, hd, ATT_TILES, ATT_W,
                         tb == 0, tb == ATT_BLOCK_TILES - 1, a_half, att_block_free(hd, g))
                    if prev is None:
                        continue
                    if t == 2:
                        att_turn(prev, 0)
                        att_turn(prev, 1)
                    if t == 3:
                        att_turn(prev, 2)
                    if t == 5:
                        att_scores(prev, 1)
                    if t == 7:
                        att_turn_probs(prev, 1)
                    if t == 9:
                        att_pv(prev, 1)
                        att_scores(prev, 0)
                    if t == 12:
                        att_turn_probs(prev, 0)
                    if t == 14:
                        att_pv(prev, 0)
                    if t == 16:
                        att_turn_out(prev)

            def out_tile(t, base, b, after_free):
                kq, c, pr = t // 8, t // 2 % 4, t % 2
                n = t // 2
                pair = pairA if kq == 0 or n % 2 == 0 else pairB

                def free(m):
                    if n == 0:
                        after_free(m)
                    elif n < 4:
                        pe.wait_ge(y_add[b], n)
                    elif n == 4:
                        pe.wait_ge(y_add[b], 4)
                    else:
                        pe.wait_ge(y_add[b], n - 1)

                tile(pair, c_hi, c_lo, kq * 4 + pr * KK, base + t, 0, 0, NB, pr == 0, pr == 1, None, free)

            turn_boundary(0)
            att_project(0, None)
            with pe.Fori(1, ATT_HEADS) as hd:
                att_project(hd, hd - 1)
            hp = ATT_HEADS - 1
            for t in range(8):
                if t == 0:
                    pe.wait_ge(a_olo, 4)
                out_tile(t, AT_ATT_OUT, 0, lambda m: pe.wait_ge(a_evac, 6 * ATT_HEADS - 1 + m))
                if t == 0:
                    att_turn(hp, 0)
                    att_turn(hp, 1)
                if t == 1:
                    att_turn(hp, 2)
                    att_scores(hp, 1)
                if t == 2:
                    att_turn_probs(hp, 1)
                if t == 3:
                    att_pv(hp, 1)
                    att_scores(hp, 0)
                if t == 5:
                    att_turn_probs(hp, 0)
                if t == 6:
                    att_pv(hp, 0)
                if t == 7:
                    att_turn_out(hp)
            pe.wait_ge(a_olo, ATT_HEADS)
            for t in range(8, 16):
                out_tile(t, AT_ATT_OUT, 0, None)

            def up(layer, base, i, t, first_block):
                if first_block:
                    wait_u(1 + 2 * layer, t)

                def free(m):
                    if not first_block:
                        pe.wait_ge(f_relu[layer], i * 2 + (1 + m))

                tile(pairA, u_hi, u_lo, t * KK, base + t, i, 2 * FF_TILES, NB, t == 0, t == FF_TILES - 1,
                     f_half[layer], free)

            def turn_hidden(layer, i):
                for m in range(HALVES):
                    pe.wait_ge(f_hid[layer], i * 2 + (1 + m))
                    bank = bankO if m else bankX
                    for j in range(4):
                        t = pe.transpose(bank[:, j * P:(j + 1) * P], m_h[:, m, j * P:(j + 1) * P], ident[:])
                    t.then_inc(f_turned[layer], 1)

            def down(layer, base, i, t):
                c, pr = divmod(t, 2)
                if t == 0:
                    pe.wait_ge(f_lo[layer], i * 2 + 2)

                def free(m):
                    pe.wait_ge(y_add[1 + 2 * layer], i * 4 + (c + 1))

                tile(pairS if c % 2 else pairB, hid_hi, hid_lo, pr * KK, base + t, i, 2 * FF_TILES, NB,
                     pr == 0, pr == 1, None, free)

            def mlp(layer, base):
                turn_boundary(1 + 2 * layer)
                for t in range(FF_TILES):
                    up(layer, base, 0, t, True)
                with pe.Fori(0, FF_BLOCKS - 1) as i:
                    for t in range(FF_TILES):
                        up(layer, base + FF_TILES, i, t, False)
                        if t == 1:
                            turn_hidden(layer, i)
                    for t in range(FF_TILES):
                        down(layer, base + 2 * FF_TILES, i, t)
                last = FF_BLOCKS - 1
                turn_hidden(layer, last)
                for t in range(FF_TILES):
                    down(layer, base + FF_TILES, last, t)

            mlp(0, AT_FF0)

            def rec_turn(hp):
                pe.wait_ge(r_evac, hp * 2 + 2)
                pe.wait_ge(r_olo, hp + 1)
                for j in range(4):
                    t = pe.transpose(bankX[:, j * P:(j + 1) * P], rz[:, j % 2, (j // 2) * P:(j // 2 + 1) * P],
                                     ident[:])
                t.then_inc(r_qfT, 1)

            def rec_scores(hp):
                pe.wait_ge(r_levels, hp + 1)
                for m in range(HALVES):
                    half, right = m * P, m * P // 2
                    for j in range(MASK_LEVELS):
                        pe.matmul(pairS[:, m, j * 64:(j + 1) * 64], r_K[:, j, half:half + P],
                                  r_R[:, j, right:right + 64], start=True, stop=True)
                    pe.matmul(pairS[:, m, 320:448], r_K[:, 0, half:half + P], r_q[:, half:half + P],
                              start=True, stop=True)
                    for b in range(2):
                        pe.matmul(pairB[64 * b:64 * b + 32, 0, half + 64 * b + 32:half + 64 * b + 64],
                                  r_K[:, 5, half + 64 * b:half + 64 * b + 32],
                                  r_R[:, 5, right + 32 * b:right + 32 * b + 32], start=True, stop=True)
                    pe.matmul(pairB[0:64, 0, half + 64:half + P], r_K[:, 6, half:half + 64],
                              r_R[:, 6, right:right + 64], start=True, stop=True)
                pe.matmul(pairB[:, 0, 2 * P:3 * P], r_K[:, 7, 0:P], r_R[:, 7, :], start=True,
                          stop=True).then_inc(r_scored, 1)

            def rec_pv(hp):
                pe.wait_ge(r_att, hp + 1)
                pe.wait_ge(r_across, hp + 1)
                v = [rz[:, m, 2 * P:3 * P] for m in range(HALVES)]
                pe.matmul(bankO[:, 0:P], r_A[:, 0:P], v[0], start=True, stop=True)
                pe.matmul(bankO[:, P:2 * P], r_A[:, P:2 * P], v[1], start=True, stop=False)
                pe.matmul(bankO[:, P:2 * P], r_A[:, 2 * P:3 * P], v[0], start=False, stop=True).then_inc(r_pv, 1)

            def rec_turn_out(hp):
                pe.wait_ge(r_out, hp + 1)
                for m in range(HALVES):
                    t = pe.transpose(bankX[:, m * P:(m + 1) * P], r_o[:, m, :], ident[:])
                t.then_inc(r_oturned, 1)

            def rec_mix(t, hp):
                if t == 0:
                    rec_turn(hp)
                if t == 4:
                    rec_scores(hp)
                if t == 5:
                    rec_pv(hp)
                if t == 7:
                    rec_turn_out(hp)

            turn_boundary(2)
            for t in range(REC_TILES):
                wait_u(2, t)
                tile(pairA, u_hi, u_lo, t * KK, AT_REC + t, 0, 0, NB, t == 0, t == REC_TILES - 1, r_half)
            with pe.Fori(1, REC_HEADS) as hd:
                for t in range(REC_TILES):
                    tile(pairA, u_hi, u_lo, t * KK, AT_REC + t, hd, REC_TILES, NB, t == 0, t == REC_TILES - 1,
                         r_half, lambda m: pe.wait_ge(r_evac, hd * 2 + (m - 1)))
                    rec_mix(t, hd - 1)
            for t in range(8):
                if t == 0:
                    pe.wait_ge(r_olo, 5)
                out_tile(t, AT_REC_OUT, 2, lambda m: pe.wait_ge(r_evac, 2 * REC_HEADS - 1 + m))
                rec_mix(t, REC_HEADS - 1)
            for t in range(8, 32):
                if t == 24:
                    pe.wait_ge(r_olo, REC_HEADS + 1)
                out_tile(t, AT_REC_OUT, 2, None)

            mlp(1, AT_FF1)

        @block.scalar
        def _(act):
            def high(at, i, per, width=KK * NB):
                if isinstance(i, int) and i * per + at >= TILES:
                    return
                slot, rounds = at % RAW, per // RAW
                act.wait_ge(landed[slot], i * (16 * rounds) + 16 * (at // RAW + 1))
                if at >= SPLIT or not isinstance(i, int):
                    act.wait_ge(tiles_used, i * per + (at - SPLIT + 1))
                nc.scalar.activation(w_hi[:, at % SPLIT, 0:width], raw[:, slot, 0:width],
                                     ACT.Copy).then_inc(hi_made, 1)

            def boundary(b, y_from=None):
                n = NORM[b]
                if b > 0:
                    for c in range(COLS):
                        act.wait_ge(y_add[b - 1], y_from + c + 1)
                        for m in range(HALVES):
                            if c or m:
                                act.wait_ge(n["ssq_y_made"], c * HALVES + m)
                            nc.scalar.activation(junk[:], y[:, m, c * NB:(c + 1) * NB], ACT.Square,
                                                 accum_out=ssq_y[:, m, c:c + 1]).then_inc(n["ssq_y_made"], 1)
                    act.wait_ge(n["mean_y_made"], 1)
                    nc.scalar.activation(rstd_y, mean_y, ACT.Sqrt).then_inc(n["root_y_made"], 1)
                if b == 4:
                    return
                for c in range(COLS):
                    for m in range(HALVES):
                        q = c * HALVES + m
                        if b == 0:
                            if c == 0:
                                act.wait_ge(x_in, 16 * HALVES)
                        else:
                            act.wait_ge(n["h_new"], q + 1)
                        if q:
                            act.wait_ge(n["ssq_h_made"], q)
                        else:
                            if b:
                                act.wait_ge(n["ssq_y_made"], COLS * HALVES)
                        nc.scalar.activation(junk[:], h[:, m, c * NB:(c + 1) * NB], ACT.Square,
                                             accum_out=ssq_h[:, m, c:c + 1]).then_inc(n["ssq_h_made"], 1)
                        act.wait_ge(n["turned"], q + 1)
                        nc.scalar.activation(u_hi[:, 4 * c:4 * c + 4, m * P:(m + 1) * P],
                                             turn_bank[q % 4].rearrange("p (k t) -> p k t", k=4),
                                             ACT.Copy).then_inc(n["u_hi_made"], 1)
                act.wait_ge(n["mean_h_made"], 1)
                nc.scalar.activation(rstd_u, mean_h, ACT.Sqrt).then_inc(n["root_h_made"], 1)

            def att_evacuate(hd, g):
                pair = pairB if g == 1 else pairA
                for m in range(HALVES):
                    if m == 0:
                        act.wait_ge(a_half, hd * 3 + (g + 1))
                    else:
                        act.wait_ge(tiles_used, hd * ATT_TILES + (AT_ATT + (g + 1) * ATT_BLOCK_TILES))
                    nc.scalar.activation(az[:, m, 3 * g:3 * g + 3, :],
                                         pair[:, m, 0:ATT_W].rearrange("p (s n) -> p s n", s=3), ACT.Copy,
                                         scale=rstd_u[:, m:m + 1]).then_inc(a_evac, 1)

            def att_copy_v(hp):
                act.wait_ge(a_evac, hp * 6 + 6)
                for m in range(HALVES):
                    ins = nc.scalar.activation(a_v[:, m, :, :], az[:, m, 2:9:3, :], ACT.Copy)
                ins.then_inc(a_vcopied, 1)

            def att_copy_qk(hp, g):
                act.wait_ge(a_turned, hp * 3 + (g + 1))
                bank = bankO if g == 1 else bankX
                nc.scalar.activation(a_qkT[:, g, :], bank[:], ACT.Copy).then_inc(a_qk, 1)

            def att_exp(hp, m):
                act.wait_ge(a_maxed, hp * 2 + (2 - m))
                n = GROUPS * (m + 1) * P
                nc.scalar.activation(a_p[:, 0:n], a_p[:, 0:n], ACT.Exp, bias=a_max[:, m:m + 1],
                                     accum_out=a_sum[:, m:m + 1]).then_inc(a_probs, 1)

            def att_copy_pt(hp, m):
                act.wait_ge(a_pturned, hp * 2 + (2 - m))
                n = GROUPS * (m + 1) * P
                flat = pairS[:].rearrange("p m n -> p (m n)")
                nc.scalar.activation(a_pT[:, 0:n], flat[:, 0:n], ACT.Copy).then_inc(a_pt, 1)

            def att_output(hp, m):
                act.wait_ge(a_pv, hp * 2 + (2 - m))
                act.wait_ge(a_rs, hp * 2 + (2 - m))
                nc.scalar.activation(a_o[:, m, :], bankO[:, m * P:(m + 1) * P], ACT.Copy,
                                     scale=a_rsum[:, m:m + 1]).then_inc(a_out, 1)

            def att_high(hp):
                act.wait_ge(a_oturned, hp + 1)
                dst = c_hi[:, hp, :] if isinstance(hp, int) else c_hi[:, bass.ds(hp, 1), :].squeeze(1)
                nc.scalar.activation(dst, bankX[:, 0:TOK], ACT.Copy).then_inc(a_ohi, 1)

            def att_head(hd, prev, last=False):
                for t in range(ATT_TILES):
                    if prev is not None:
                        if t == 0:
                            att_copy_v(prev)
                        if t == 2:
                            att_copy_qk(prev, 0)
                            att_copy_qk(prev, 1)
                        if t == 3:
                            att_copy_qk(prev, 2)
                        if t == 6:
                            att_exp(prev, 1)
                        if t == 8:
                            att_copy_pt(prev, 1)
                        if t == 10:
                            att_output(prev, 1)
                        if t == 11:
                            att_exp(prev, 0)
                        if t == 13:
                            att_copy_pt(prev, 0)
                        if t == 15:
                            att_output(prev, 0)
                        if t == 17:
                            att_high(prev)
                    if t % ATT_BLOCK_TILES == ATT_BLOCK_TILES - 1:
                        att_evacuate(hd, t // ATT_BLOCK_TILES)
                    into_next = last and t + SPLIT >= ATT_TILES
                    high(AT_ATT + t + SPLIT, hd, ATT_TILES, KK * (NB if into_next else ATT_W))

            for t in range(SPLIT):
                high(t, 0, 0, KK * ATT_W)
            boundary(0)
            act.wait_ge(angle_ready, 1)
            nc.scalar.activation(rope[:, 0, :, :], rope[:, 0, :, :], ACT.Sin)
            nc.scalar.activation(rope[:, 1, :, :], rope[:, 1, :, :], ACT.Sin).then_inc(sines_ready, 1)
            act.wait_ge(bexp_in, 1)
            nc.scalar.activation(bounds[:, 1, :], bounds[:, 1, :], ACT.Exp).then_inc(bexp_out, 1)
            act.wait_ge(NORM[0]["rstd_u_made"], 1)
            att_head(0, None)
            with act.Fori(1, ATT_HEADS - 1) as hd:
                att_head(hd, hd - 1)
            att_head(ATT_HEADS - 1, ATT_HEADS - 2, last=True)
            hp = ATT_HEADS - 1
            for t in range(16):
                if t == 0:
                    att_copy_v(hp)
                    att_copy_qk(hp, 0)
                    att_copy_qk(hp, 1)
                if t == 1:
                    att_copy_qk(hp, 2)
                    att_exp(hp, 1)
                if t == 2:
                    att_copy_pt(hp, 1)
                if t == 3:
                    att_output(hp, 1)
                if t == 4:
                    att_exp(hp, 0)
                if t == 5:
                    att_copy_pt(hp, 0)
                if t == 6:
                    att_output(hp, 0)
                if t == 7:
                    att_high(hp)
                high(AT_ATT_OUT + t + SPLIT, 0, 0)

            def hidden(layer, i, used):
                for m in range(HALVES):
                    if m == 0:
                        act.wait_ge(f_half[layer], i + 1)
                    else:
                        act.wait_ge(tiles_used, used)
                    nc.scalar.activation(m_h[:, m, :], pairA[:, m, :], ACT.Relu,
                                         scale=rstd_u[:, m:m + 1]).then_inc(f_relu[layer], 1)
                for m in range(HALVES):
                    act.wait_ge(f_relu[layer], i * 2 + (1 + m))
                    nc.scalar.activation(m_h[:, m, :], m_h[:, m, :], ACT.Square).then_inc(f_hid[layer], 1)

            def hidden_high(layer, i):
                for m in range(HALVES):
                    act.wait_ge(f_turned[layer], i * 2 + (1 + m))
                    bank = bankO if m else bankX
                    nc.scalar.activation(hid_hi[:, :, m * P:(m + 1) * P],
                                         bank[:].rearrange("p (k t) -> p k t", k=4),
                                         ACT.Copy).then_inc(f_hi[layer], 1)

            def mlp(layer, base):
                for t in range(FF_TILES):
                    if t == FF_TILES - 1:
                        hidden(layer, 0, base + FF_TILES)
                    high(base + t + SPLIT, 0, 0)
                with act.Fori(0, FF_BLOCKS - 1) as i:
                    for t in range(2 * FF_TILES):
                        if t == 1:
                            hidden_high(layer, i)
                        if t == FF_TILES - 1:
                            hidden(layer, i + 1, i * (2 * FF_TILES) + (base + 2 * FF_TILES))
                        high(base + FF_TILES + t + SPLIT, i, 2 * FF_TILES)
                last = base + (2 * FF_BLOCKS - 1) * FF_TILES
                for t in range(FF_TILES):
                    if t == 0:
                        hidden_high(layer, FF_BLOCKS - 1)
                    high(last + t + SPLIT, 0, 0)

            boundary(1, 4)
            act.wait_ge(NORM[1]["rstd_u_made"], 1)
            mlp(0, AT_FF0)
            boundary(2, 2 + 4 * (FF_BLOCKS - 1))
            act.wait_ge(NORM[2]["rstd_u_made"], 1)

            def rec_evacuate(hd):
                for m in range(HALVES):
                    if m == 0:
                        act.wait_ge(r_half, hd + 1)
                        act.wait_ge(r_gate, hd + 1)
                    else:
                        act.wait_ge(tiles_used, hd * REC_TILES + (AT_REC + REC_TILES))
                    nc.scalar.activation(rz[:, m, :], pairA[:, m, :], ACT.Copy,
                                         scale=rstd_u[:, m:m + 1]).then_inc(r_evac, 1)

            def rec_exps(hp):
                act.wait_ge(r_qfT, hp + 1)
                nc.scalar.activation(r_e, bankX[:, TOK:2 * TOK], ACT.Exp, scale=-1.0).then_inc(r_exp, 1)
                nc.scalar.activation(r_q, bankX[:, 0:TOK], ACT.Copy).then_inc(r_qcopied, 1)
                act.wait_ge(r_evac, hp * 2 + 2)
                nc.scalar.activation(r_eg, rz[:, :, 3 * P:4 * P], ACT.Exp, scale=-1.0).then_inc(r_expg, 1)

            def rec_across(hp):
                act.wait_ge(r_scored, hp + 1)
                nc.scalar.activation(r_A[:, TOK:3 * P], pairB[:, 0, TOK:3 * P], ACT.Copy).then_inc(r_across, 1)

            def rec_norm(hp):
                act.wait_ge(r_pv, hp + 1)
                for m in range(HALVES):
                    if m:
                        act.wait_ge(r_ssq, hp * 2 + 1)
                    nc.scalar.activation(junk[:, 0:P], bankO[:, m * P:(m + 1) * P], ACT.Square,
                                         accum_out=r_ms[:, m:m + 1]).then_inc(r_ssq, 1)
                act.wait_ge(r_ssq, hp * 2 + 2)
                nc.scalar.activation(r_ln, r_ms, ACT.Ln, bias=eps_col, scale=1.0 / P).then_inc(r_logged, 1)
                act.wait_ge(r_logged, hp + 1)
                nc.scalar.activation(r_rs, r_ln, ACT.Exp, scale=-0.5).then_inc(r_root, 1)

            def rec_high(hp):
                act.wait_ge(r_oturned, hp + 1)
                dst = c_hi[:, hp, :] if isinstance(hp, int) else c_hi[:, bass.ds(hp, 1), :].squeeze(1)
                nc.scalar.activation(dst, bankX[:, 0:TOK], ACT.Copy).then_inc(r_ohi, 1)

            def rec_mix(t, hp):
                if t == 0:
                    rec_exps(hp)
                if t == 4:
                    rec_across(hp)
                if t == 6:
                    rec_norm(hp)

            for t in range(REC_TILES):
                if t == REC_TILES - 1:
                    rec_evacuate(0)
                high(AT_REC + t + SPLIT, 0, 0)
            with act.Fori(1, REC_HEADS) as hd:
                for t in range(REC_TILES):
                    rec_mix(t, hd - 1)
                    if t == REC_TILES - 1:
                        rec_evacuate(hd)
                    high(AT_REC + t + SPLIT, hd, REC_TILES)
                    if t == REC_TILES - 1:
                        rec_high(hd - 1)
            for t in range(32):
                if t < 8:
                    rec_mix(t, REC_HEADS - 1)
                high(AT_REC_OUT + t + SPLIT, 0, 0)
                if t == 7:
                    rec_high(REC_HEADS - 1)

            boundary(3, 12)
            act.wait_ge(NORM[3]["rstd_u_made"], 1)
            mlp(1, AT_FF1)
            boundary(4, 2 + 4 * (FF_BLOCKS - 1))

        @block.vector
        def _(dve):
            V = nc.vector

            def low(at, i, per, width=KK * NB):
                if isinstance(i, int) and i * per + at >= TILES:
                    return
                dve.wait_ge(hi_made, i * per + (at + 1))
                V.tensor_tensor(w_lo[:, at % SPLIT, 0:width], raw[:, at % RAW, 0:width],
                                w_hi[:, at % SPLIT, 0:width].bitcast(F32), ALU.subtract).then_inc(lo_made, 1)

            def boundary(b):
                n = NORM[b]
                s = Steps(dve, n["steps"])
                pre_count = [0, 1, 2, 3, None][b]
                if b > 0:
                    dve.wait_ge(n["ssq_y_made"], COLS * HALVES)
                    s.link(V.tensor_reduce(mean_y, ssq_y, AX.X, ALU.add))
                    V.tensor_scalar(mean_y, mean_y, 1.0 / D, EPS, ALU.mult, ALU.add).then_inc(n["mean_y_made"], 1)
                    dve.wait_ge(n["root_y_made"], 1)
                    s.link(V.reciprocal(rstd_y, rstd_y))
                    dve.wait_ge(post_in, 16 * b)
                if b < 4:
                    dve.wait_ge(pre_in, 16 * (pre_count + 1))
                if b == 0:
                    dve.wait_ge(x_in, 16 * HALVES)

                def gained(c):
                    cols = slice(c * NB, (c + 1) * NB)
                    if b > 0:
                        for m in range(HALVES):
                            s.note(V.scalar_tensor_tensor(out=y[:, m, cols], in0=y[:, m, cols],
                                                          scalar=rstd_y[:, m:m + 1], in1=gain_post[:, cols],
                                                          op0=ALU.mult, op1=ALU.mult))
                        s.last()
                        for m in range(HALVES):
                            V.tensor_tensor(h[:, m, cols], h[:, m, cols], y[:, m, cols],
                                            ALU.add).then_inc(n["h_new"], 1)
                        dve.wait_ge(n["h_new"], HALVES * (c + 1))
                    if b < 4:
                        for m in range(HALVES):
                            V.tensor_tensor(y[:, m, cols], h[:, m, cols], gain_pre[:, cols],
                                            ALU.mult).then_inc(n["hg_made"], 1)

                def low_u(c):
                    for m in range(HALVES):
                        q = c * HALVES + m
                        dve.wait_ge(n["u_hi_made"], q + 1)
                        V.tensor_tensor(u_lo[:, 4 * c:4 * c + 4, m * P:(m + 1) * P],
                                        turn_bank[q % 4].rearrange("p (k t) -> p k t", k=4),
                                        u_hi[:, 4 * c:4 * c + 4, m * P:(m + 1) * P].bitcast(F32),
                                        ALU.subtract).then_inc(n["u_lo_made"], 1)

                for c in range(COLS):
                    gained(c)
                    if c and b < 4:
                        low_u(c - 1)
                if b == 4:
                    return
                low_u(COLS - 1)
                dve.wait_ge(n["ssq_h_made"], COLS * HALVES)
                s.link(V.tensor_reduce(mean_h, ssq_h, AX.X, ALU.add))
                V.tensor_scalar(mean_h, mean_h, 1.0 / D, EPS, ALU.mult, ALU.add).then_inc(n["mean_h_made"], 1)
                dve.wait_ge(n["root_h_made"], 1)
                V.reciprocal(rstd_u, rstd_u).then_inc(n["rstd_u_made"], 1)

            def setup_attention():
                s = Steps(dve, v_setup)
                dve.wait_ge(masks_ready, 1)
                dve.wait_ge(ident_ready, 1)
                onehot = carve(0, 32)
                for g in range(GROUPS):
                    d = DILATION[g]
                    if d == 1:
                        continue
                    s.link(V.tensor_reduce(onehot[:, 0:d], ident[:].rearrange("p (b r) -> p r b", r=d),
                                           AX.X, ALU.add))
                    s.link(V.tensor_scalar(onehot[:, 0:d], onehot[:, 0:d], 1.0, -MASKED, ALU.subtract, ALU.mult))
                    view = amask[:, g, :].rearrange("p (b r) -> p b r", r=d)
                    s.link(V.tensor_tensor(view, view, onehot[:, None, 0:d].broadcast_to([P, TOK // d, d]),
                                           ALU.add))
                inv = carve(32, HALF_ROPE)
                posf = carve(64, HALVES)
                ang = carve(96, HALVES, HALF_ROPE)
                turns = carve(128, HALVES, HALF_ROPE)
                half = HALF_ROPE
                freq = np.float32(ROPE_THETA) ** (-np.arange(half, dtype=np.float32) / np.float32(half))
                dve.wait_ge(pos_in, 16)
                s.note(V.tensor_copy(posf, pos_i[:]))
                for j in range(half):
                    s.note(V.memset(inv[:, j:j + 1], float(freq[j])))
                s.last()
                for m in range(HALVES):
                    s.note(V.tensor_scalar(ang[:, m, :], inv, posf[:, m:m + 1], None, ALU.mult))
                s.last()
                two_pi = 2 * np.pi
                part1 = 6.28125
                part2 = float(np.float32(np.round((two_pi - part1) * 2 ** 21) / 2 ** 21))
                part3 = float(np.float32(two_pi - part1 - part2))
                magic = 1.5 * 2 ** 23
                s.link(V.tensor_scalar(turns, ang, float(np.float32(1 / two_pi)), None, ALU.mult))
                s.link(V.tensor_scalar(turns, turns, magic, None, ALU.add))
                s.link(V.tensor_scalar(turns, turns, magic, None, ALU.subtract))
                for part in (part1, part2, part3):
                    s.link(V.scalar_tensor_tensor(out=ang, in0=turns, scalar=-part, in1=ang,
                                                  op0=ALU.mult, op1=ALU.add))
                pi = 3.1415925
                s.link(V.tensor_scalar(ang, ang, pi, -pi, ALU.min, ALU.max))
                s.note(V.tensor_scalar(rope[:, 0, :, :], ang, 0.5, None, ALU.mult))
                V.tensor_copy(rope[:, 1, :, :], ang).then_inc(angle_ready, 1)
                dve.wait_ge(bound_in, 16)
                V.tensor_tensor(bounds[:, 1, :], bounds[:, 0, :], bounds[:, 0, :],
                                ALU.subtract).then_inc(bexp_in, 1)
                dve.wait_ge(sines_ready, 1)
                s.link(V.tensor_tensor(rope[:, 0, :, :], rope[:, 0, :, :], rope[:, 0, :, :], ALU.mult))
                V.tensor_scalar(rope[:, 0, :, :], rope[:, 0, :, :], -2.0, 1.0, ALU.mult,
                                ALU.add).then_inc(rope_ready, 1)
                dve.wait_ge(bexp_out, 1)
                s.link(V.reciprocal(bounds[:, 2, :], bounds[:, 1, :]))
                s.link(V.tensor_tensor(bounds[:, 1, :], bounds[:, 1, :], bounds[:, 2, :], ALU.mult))
                s.link(V.tensor_tensor(bounds[:, 1, :], bounds[:, 1, :], bounds[:, 1, :], ALU.subtract))
                s.note(V.tensor_scalar(bounds[:, 2, :], bounds[:, 1, :], LB_FLOOR, None, ALU.max))
                s.link(V.tensor_scalar(bounds[:, 3, :], bounds[:, 1, :], -1.0, 1.0, ALU.mult, ALU.add))
                s.link(V.tensor_tensor(bounds[:, 4, :], bounds[:, 2, :], bounds[:, 1, :], ALU.subtract))
                dve.wait_ge(rope_ready, 1)

            def att_rotate(hp, s):
                dve.wait_ge(a_evac, hp * 6 + 6)
                cosx = a_cosx.rearrange("p (s j i) -> p s j i", s=9, j=2)
                sinx = a_sinx.rearrange("p (s j i) -> p s j i", s=9, j=2)
                for m in range(HALVES):
                    src = az[:, m, :, 0:32].rearrange("p s (j i) -> p s j i", j=2)
                    cos = rope[:, 0, m, :][:, None, None, :].broadcast_to([P, 9, 2, HALF_ROPE])
                    sin = rope[:, 1, m, :][:, None, None, :].broadcast_to([P, 9, 2, HALF_ROPE])
                    s.note(V.tensor_tensor(cosx, src, cos, ALU.mult))
                    s.note(V.tensor_tensor(sinx, src, sin, ALU.mult))
                    s.last()

                    def qk(view):
                        return view.rearrange("p (g s) i -> p g s i", g=GROUPS)[:, :, 0:2, :]

                    s.note(V.tensor_tensor(qk(az[:, m, :, 0:16]), qk(cosx[:, :, 0, :]), qk(sinx[:, :, 1, :]),
                                           ALU.subtract))
                    ins = V.tensor_tensor(qk(az[:, m, :, 16:32]), qk(cosx[:, :, 1, :]), qk(sinx[:, :, 0, :]),
                                          ALU.add)
                    if m == 0:
                        s.link(ins)
                    else:
                        ins.then_inc(a_rot, 1)

            def att_mask(hp, m, s):
                dve.wait_ge(a_scored, hp * 2 + (2 - m))
                n = (m + 1) * P
                flat = pairS[:].rearrange("p m n -> p (m n)")[:, 0:GROUPS * n]
                s.link(V.scalar_tensor_tensor(
                    out=a_p[:, 0:GROUPS * n].rearrange("p (g n) -> p g n", g=GROUPS),
                    in0=flat.rearrange("p (g n) -> p g n", g=GROUPS), scalar=float(P) ** -0.5,
                    in1=amask[:, :, TOK - n:TOK], op0=ALU.mult, op1=ALU.add))
                s.link(V.tensor_reduce(a_max[:, m:m + 1], a_p[:, 0:GROUPS * n], AX.X, ALU.max))
                V.tensor_scalar(a_max[:, m:m + 1], a_max[:, m:m + 1], -1.0, None,
                                ALU.mult).then_inc(a_maxed, 1)

            def att_rsum(hp, m):
                dve.wait_ge(a_probs, hp * 2 + (2 - m))
                V.reciprocal(a_rsum[:, m:m + 1], a_sum[:, m:m + 1]).then_inc(a_rs, 1)

            def att_low(hp):
                dve.wait_ge(a_ohi, hp + 1)
                if isinstance(hp, int):
                    hi, lo = c_hi[:, hp, :], c_lo[:, hp, :]
                else:
                    hi, lo = c_hi[:, bass.ds(hp, 1), :].squeeze(1), c_lo[:, bass.ds(hp, 1), :].squeeze(1)
                V.tensor_tensor(lo, bankX[:, 0:TOK], hi.bitcast(F32), ALU.subtract).then_inc(a_olo, 1)

            ATT_STEPS = 11

            def att_head(hd, prev, last=False):
                s = Steps(dve, a_steps, None if prev is None else prev * ATT_STEPS)
                for t in range(ATT_TILES):
                    if prev is not None:
                        if t == 0:
                            att_rotate(prev, s)
                        if t == 5:
                            att_mask(prev, 1, s)
                        if t == 7:
                            att_rsum(prev, 1)
                        if t == 10:
                            att_mask(prev, 0, s)
                        if t == 12:
                            att_rsum(prev, 0)
                        if t == 17:
                            att_low(prev)
                    into_next = last and t + SPLIT >= ATT_TILES
                    low(AT_ATT + t + SPLIT, hd, ATT_TILES, KK * (NB if into_next else ATT_W))
                assert prev is None or s.count == ATT_STEPS, s.count

            def add_y(b, n, c, pair, used, fresh, before):
                dve.wait_ge(tiles_used, used)
                if before is not None:
                    dve.wait_ge(y_add[b], before)
                dst = y[:, :, c * NB:(c + 1) * NB]
                if fresh:
                    V.tensor_copy(dst, pair[:]).then_inc(y_add[b], 1)
                else:
                    V.tensor_tensor(dst, dst, pair[:], ALU.add).then_inc(y_add[b], 1)

            def out_add(b, base, t):
                if t % 2:
                    n = t // 2
                    pair = pairA if n < 4 or n % 2 == 0 else pairB
                    add_y(b, n, n % 4, pair, base + t + 1, n < 4, n if n >= 4 else None)

            for t in range(SPLIT):
                low(t, 0, 0, KK * ATT_W)
            boundary(0)
            setup_attention()
            att_head(0, None)
            with dve.Fori(1, ATT_HEADS - 1) as hd:
                att_head(hd, hd - 1)
            att_head(ATT_HEADS - 1, ATT_HEADS - 2, last=True)
            hp = ATT_HEADS - 1
            s = Steps(dve, a_steps, hp * ATT_STEPS)
            for t in range(16):
                if t == 0:
                    att_rotate(hp, s)
                if t == 1:
                    att_mask(hp, 1, s)
                if t == 2:
                    att_rsum(hp, 1)
                if t == 3:
                    att_mask(hp, 0, s)
                if t == 4:
                    att_rsum(hp, 0)
                if t == 7:
                    att_low(hp)
                low(AT_ATT_OUT + t + SPLIT, 0, 0)
                out_add(0, AT_ATT_OUT, t)

            def hidden_low(layer, i):
                for m in range(HALVES):
                    dve.wait_ge(f_hi[layer], i * 2 + (1 + m))
                    bank = bankO if m else bankX
                    V.tensor_tensor(hid_lo[:, :, m * P:(m + 1) * P], bank[:].rearrange("p (k t) -> p k t", k=4),
                                    hid_hi[:, :, m * P:(m + 1) * P].bitcast(F32),
                                    ALU.subtract).then_inc(f_lo[layer], 1)

            def mlp(layer, base):
                b = 1 + 2 * layer
                for t in range(FF_TILES):
                    low(base + t + SPLIT, 0, 0)
                with dve.Fori(0, FF_BLOCKS - 1) as i:
                    for t in range(2 * FF_TILES):
                        if t == 1:
                            hidden_low(layer, i)
                        low(base + FF_TILES + t + SPLIT, i, 2 * FF_TILES)
                        if t >= FF_TILES and t % 2:
                            c = (t - FF_TILES) // 2
                            add_y(b, None, c, pairS if c % 2 else pairB,
                                  i * (2 * FF_TILES) + (base + FF_TILES + t + 1), False, i * 4 + (c + 2))
                last = base + (2 * FF_BLOCKS - 1) * FF_TILES
                hidden_low(layer, FF_BLOCKS - 1)
                for t in range(FF_TILES):
                    low(last + t + SPLIT, 0, 0)
                    if t % 2:
                        c = t // 2
                        add_y(b, None, c, pairS if c % 2 else pairB, last + t + 1, False,
                              4 * (FF_BLOCKS - 1) + c + 2)

            boundary(1)
            mlp(0, AT_FF0)
            boundary(2)

            REC_STEPS = 6 + 5 * (LEVELS - 1) + 2 + 2 * MASK_LEVELS - 1 + 3 + 5

            def rec_gates(hp, s):
                def col(row):
                    return bounds[:, row, hp:hp + 1] if isinstance(hp, int) else bounds[:, row, bass.ds(hp, 1)]
                dve.wait_ge(r_exp, hp + 1)
                s.link(V.tensor_scalar(r_d, r_e, EXP_CAP, 1.0, ALU.min, ALU.add))
                s.link(V.reciprocal(r_d, r_d))
                s.note(V.tensor_scalar(r_f, r_d, col(3), col(2), ALU.mult, ALU.add))
                s.link(V.scalar_tensor_tensor(out=r_e, in0=r_e, scalar=EXP_CAP, in1=r_d,
                                              op0=ALU.min, op1=ALU.mult))
                s.note(V.tensor_scalar(r_K[:, 0, :], r_e, col(3), col(4), ALU.mult, ALU.subtract))
                s.link(V.tensor_copy(r_tot[:, 0:TOK], r_f))

            def rec_levels_(hp, s):
                dve.wait_ge(r_qcopied, hp + 1)
                at = 0
                for j in range(LEVELS):
                    w, nb = 1 << j, TOK >> (j + 1)
                    def halves(v):
                        return v.rearrange("p (b two w) -> p b two w", two=2, w=w)
                    tot = r_tot[:, at:at + 2 * nb].rearrange("p (b two) -> p b two", two=2)
                    last = j == LEVELS - 1
                    ins = V.tensor_tensor(r_R[:, j, :].rearrange("p (b w) -> p b w", w=w),
                                          halves(r_q)[:, :, 1, :], halves(r_f)[:, :, 1, :], ALU.mult)
                    if last:
                        ins.then_inc(r_levels, 1)
                        break
                    s.note(ins)
                    s.note(V.tensor_tensor(halves(r_K[:, j + 1, :])[:, :, 0, :], halves(r_K[:, j, :])[:, :, 0, :],
                                           tot[:, :, 1:2].broadcast_to([P, nb, w]), ALU.mult))
                    s.note(V.tensor_copy(halves(r_K[:, j + 1, :])[:, :, 1, :], halves(r_K[:, j, :])[:, :, 1, :]))
                    s.note(V.tensor_tensor(r_tot[:, at + 2 * nb:at + 3 * nb], tot[:, :, 0], tot[:, :, 1], ALU.mult))
                    s.link(V.tensor_tensor(halves(r_f)[:, :, 1, :], halves(r_f)[:, :, 1, :],
                                           tot[:, :, 0:1].broadcast_to([P, nb, w]), ALU.mult))
                    at += 2 * nb

            def rec_assemble(hp, s):
                dve.wait_ge(r_scored, hp + 1)
                s.link(V.tensor_tensor(r_prod, pairS[:, :, 0:SCORES],
                                       rmask[:, None, :].broadcast_to([P, HALVES, SCORES]), ALU.mult))
                rows = r_A[:, 0:TOK]
                dve.wait_ge(r_across, hp + 1)
                s.link(V.tensor_tensor(rows.rearrange("p (m t) -> p m t", m=HALVES),
                                       pairB[:, 0, 0:TOK].rearrange("p (m t) -> p m t", m=HALVES),
                                       r_prod[:, :, SCORES - P:SCORES], ALU.add))
                for j in range(MASK_LEVELS):
                    w = 1 << j
                    dst = rows.rearrange("p (n two w) -> p n two w", two=2, w=w)[:, :, 1, :]
                    for m in range(HALVES):
                        part = dst[:, m * 64 // w:(m + 1) * 64 // w, :]
                        ins = V.tensor_tensor(part, part, r_prod[:, m, j * 64:(j + 1) * 64].rearrange(
                            "p (b w) -> p b w", w=w), ALU.add)
                        if m == 0:
                            s.note(ins)
                    if j < MASK_LEVELS - 1:
                        s.link(ins)
                ins.then_inc(r_att, 1)

            def rec_gate_out(hp, s):
                dve.wait_ge(r_expg, hp + 1)
                s.link(V.tensor_scalar(r_G, r_eg, EXP_CAP, 1.0, ALU.min, ALU.add))
                s.link(V.reciprocal(r_G, r_G))
                s.link(V.tensor_tensor(r_G, r_G, rz[:, :, 3 * P:4 * P], ALU.mult))
                V.tensor_tensor(r_G, r_G, rgain[:, None, :].broadcast_to([P, HALVES, P]),
                                ALU.mult).then_inc(r_gate, 1)

            def rec_output(hp, s):
                dve.wait_ge(r_ssq, hp * 2 + 2)
                s.note(V.tensor_scalar(r_x, r_ms, 1.0 / P, EPS, ALU.mult, ALU.add))
                dve.wait_ge(r_root, hp + 1)
                s.link(V.tensor_tensor(r_t, r_rs, r_rs, ALU.mult))
                s.link(V.tensor_tensor(r_t, r_t, r_x, ALU.mult))
                s.link(V.tensor_scalar(r_t, r_t, -0.5, 1.5, ALU.mult, ALU.add))
                s.link(V.tensor_tensor(r_rs, r_rs, r_t, ALU.mult))
                dve.wait_ge(r_gate, hp + 2)
                for m in range(HALVES):
                    ins = V.scalar_tensor_tensor(out=r_o[:, m, :], in0=bankO[:, m * P:(m + 1) * P],
                                                 scalar=r_rs[:, m:m + 1], in1=r_G[:, m, :],
                                                 op0=ALU.mult, op1=ALU.mult)
                ins.then_inc(r_out, 1)

            def rec_low(hp):
                dve.wait_ge(r_ohi, hp + 1)
                if isinstance(hp, int):
                    hi, lo = c_hi[:, hp, :], c_lo[:, hp, :]
                else:
                    hi, lo = c_hi[:, bass.ds(hp, 1), :].squeeze(1), c_lo[:, bass.ds(hp, 1), :].squeeze(1)
                V.tensor_tensor(lo, bankX[:, 0:TOK], hi.bitcast(F32), ALU.subtract).then_inc(r_olo, 1)

            def rec_mix(t, hp, s):
                if t == 0:
                    rec_gates(hp, s)
                if t == 1:
                    rec_levels_(hp, s)
                if t == 3:
                    rec_gate_out(hp, s)
                if t == 4:
                    rec_assemble(hp, s)
                if t == 6:
                    rec_output(hp, s)

            dve.wait_ge(y_add[1], 2 + 4 * FF_BLOCKS)
            V.memset(pairB[:, 0, :], 0.0).then_inc(zmem, 1)
            dve.wait_ge(zmem, 1)
            V.memset(r_A, 0.0).then_inc(r_olo, 1)
            dve.wait_ge(rgain_in, 16)
            V.memset(r_x, 0.0).then_inc(r_gate, 1)
            for t in range(REC_TILES):
                low(AT_REC + t + SPLIT, 0, 0)
            with dve.Fori(1, REC_HEADS) as hd:
                s = Steps(dve, r_steps, (hd - 1) * REC_STEPS)
                for t in range(REC_TILES):
                    rec_mix(t, hd - 1, s)
                    low(AT_REC + t + SPLIT, hd, REC_TILES)
                    if t == REC_TILES - 1:
                        rec_low(hd - 1)
                assert s.count == REC_STEPS, s.count
            s = Steps(dve, r_steps, (REC_HEADS - 1) * REC_STEPS)
            for t in range(32):
                if t < 8:
                    rec_mix(t, REC_HEADS - 1, s)
                low(AT_REC_OUT + t + SPLIT, 0, 0)
                out_add(2, AT_REC_OUT, t)
                if t == 7:
                    rec_low(REC_HEADS - 1)

            boundary(3)
            mlp(1, AT_FF1)
            boundary(4)


def _tiles_by_head(w, groups, parts, heads):
    a = w.reshape(KC // KK, KK, P, groups, parts, heads, P)
    a = a.transpose(5, 3, 0, 2, 1, 4, 6)
    return np.ascontiguousarray(a).reshape(heads * groups * (KC // KK), P, KK * parts * P)


def _tiles_up(w):
    a = w.reshape(2, KC // KK, KK, P, FF_BLOCKS, NB).transpose(0, 4, 1, 3, 2, 5)
    return np.ascontiguousarray(a).reshape(-1, P, KK * NB)


def _tiles_down(w):
    a = w.reshape(-1, 2, KK, P, COLS, NB).transpose(0, 4, 1, 3, 2, 5)
    return np.ascontiguousarray(a).reshape(-1, P, KK * NB)


def kernel(**inputs):
    import concourse.bacc as _bacc
    from concourse.bass_utils import run_bass_kernel_spmd as _run

    a = {k: np.asarray(v) for k, v in inputs.items()}
    arrays = {
        "x": a["x"][0],
        "positions": np.ascontiguousarray(a["positions"].reshape(HALVES, P).T),
        "norm_gains": a["norm_gains"],
        "lower_bound": np.ascontiguousarray(a["rec_lower_bounds"].reshape(REC_HEADS, P).T),
        "rec_gain": a["rec_out_norm"],
        "s_att_in": _tiles_by_head(a["w_att_in"][0], GROUPS, 3, ATT_HEADS),
        "s_att_out": _tiles_down(a["w_att_out"]),
        "s_rec_in": _tiles_by_head(a["w_rec_in"][0], 1, 4, REC_HEADS),
        "s_rec_out": _tiles_down(a["w_rec_out"]),
        "s_up": _tiles_up(a["w_ff1"]),
        "s_down": _tiles_down(a["w_ff2"]),
    }
    nc = _bacc.Bacc("TRN2", target_bir_lowering=False, num_devices=1)
    args = [nc.dram_tensor("in_" + k, v.shape, mybir.dt.from_np(v.dtype), kind="ExternalInput").ap()
            for k, v in arrays.items()]
    out = nc.dram_tensor("out_h", (TOK, D), F32, kind="ExternalOutput").ap()
    hybrid_trunk(nc, *args, out)
    r = _run(nc, [{"in_" + k: np.ascontiguousarray(v) for k, v in arrays.items()}], core_ids=[0])
    return r.results[0]["out_h"].reshape(1, TOK, D)
```

```python
from contextlib import ExitStack

import numpy as np

import concourse.bass as bass
from concourse import mybir

F32 = mybir.dt.float32
F32R = mybir.dt.float32r
I32 = mybir.dt.int32
U32 = mybir.dt.uint32
ALU = mybir.AluOpType
ACT = mybir.ActivationFunctionType
AX = mybir.AxisListType

P = 128
TOK = 256
HALVES = TOK // P
D = 2048
KC = D // P
NB = 512
KK = 2
RAW = 8
SPLIT = 4
COLS = D // NB

ATT_HEADS = 8
GROUPS = 3
DILATION = (1, 4, 16)
WINDOW = (128, 512, 2048)
ATT_W = 3 * P
ATT_BLOCK_TILES = KC // KK
ATT_TILES = GROUPS * ATT_BLOCK_TILES
HALF_ROPE = 16
ROPE_THETA = 500000.0
MASKED = -1e30

REC_HEADS = 16
REC_TILES = KC // KK
LEVELS = 8
MASK_LEVELS = 5
SCORES = MASK_LEVELS * P // 2 + P
LB_FLOOR = 1e-30

FF_BLOCKS = 16
FF_TILES = 8
EPS = 1e-6

AT_ATT = 0
AT_ATT_OUT = AT_ATT + ATT_HEADS * ATT_TILES
AT_FF0 = AT_ATT_OUT + ATT_HEADS // 4 * COLS * 2
AT_REC = AT_FF0 + FF_BLOCKS * 2 * FF_TILES
AT_REC_OUT = AT_REC + REC_HEADS * REC_TILES
AT_FF1 = AT_REC_OUT + REC_HEADS // 4 * COLS * 2
TILES = AT_FF1 + FF_BLOCKS * 2 * FF_TILES


class Steps:

    def __init__(self, eng, sem, base=0):
        self.eng, self.sem, self.base, self.count = eng, sem, base, 0

    def note(self, ins):
        ins.then_inc(self.sem, 1)
        self.count += 1
        return self.base + self.count

    def last(self):
        self.eng.wait_ge(self.sem, self.base + self.count)

    def reach(self, count):
        self.eng.wait_ge(self.sem, self.base + count)

    def link(self, ins):
        self.note(ins)
        self.last()


def hybrid_trunk(nc, x, positions, norm_gains, lower_bound, rec_gain, s_att_in, s_att_out,
                 s_rec_in, s_rec_out, s_up, s_down, out):
    with ExitStack() as ctx:
        def sb(name, shape, dt=F32):
            return ctx.enter_context(nc.sbuf_tensor(name, shape, dt))

        def psum(name, shape):
            return ctx.enter_context(nc.psum_tensor(name, shape, F32))

        def sem(name):
            return ctx.enter_context(nc.semaphore(name))

        raw = sb("raw", [P, RAW, KK * NB])
        w_hi = sb("w_hi", [P, SPLIT, KK * NB], F32R)
        w_lo = sb("w_lo", [P, SPLIT, KK * NB], F32R)
        u_hi = sb("u_hi", [P, KC, TOK], F32R)
        u_lo = sb("u_lo", [P, KC, TOK], F32R)
        c_hi = sb("c_hi", [P, REC_HEADS, TOK], F32R)
        c_lo = sb("c_lo", [P, REC_HEADS, TOK], F32R)
        h = sb("h", [P, HALVES, D])
        y = sb("y", [P, HALVES, D])
        gain_post = sb("gain_post", [P, D])
        gain_pre = sb("gain_pre", [P, D])
        ident = sb("ident", [P, P])
        junk = sb("junk", [P, NB], mybir.dt.bfloat16)
        stat = sb("stat", [P, 64])
        mix = sb("mix", [P, 7168])
        rope = sb("rope", [P, 2, HALVES, HALF_ROPE])
        pos_i = sb("pos_i", [P, HALVES], I32)
        bounds = sb("bounds", [P, 5, REC_HEADS])
        rgain = sb("rgain", [P, 1])

        def carve(at, *shape):
            n = int(np.prod(shape))
            v = mix[:, at:at + n]
            if len(shape) == 2:
                v = v.rearrange("p (a b) -> p a b", a=shape[0])
            if len(shape) == 3:
                v = v.rearrange("p (a b c) -> p a b c", a=shape[0], b=shape[1])
            return v

        ssq_y = stat[:, 0:8].rearrange("p (m c) -> p m c", m=HALVES)
        ssq_h = stat[:, 8:16].rearrange("p (m c) -> p m c", m=HALVES)
        mean_y = stat[:, 16:18]
        rstd_y = stat[:, 18:20]
        mean_h = stat[:, 20:22]
        rstd_u = stat[:, 22:24]
        eps_col = stat[:, 24:25]

        az = carve(0, HALVES, 9, P)
        a_qkT = carve(2304, GROUPS, NB)
        a_v = carve(3840, HALVES, GROUPS, P)
        a_p = carve(4608, 768)
        a_pT = carve(5376, 768)
        a_o = carve(6144, HALVES, P)
        a_cosx = carve(4608, 9 * 32)
        a_sinx = carve(4896, 9 * 32)
        amask = carve(6400, GROUPS, TOK)
        a_max = stat[:, 26:28]
        a_sum = stat[:, 28:30]
        a_rsum = stat[:, 30:32]

        rz = carve(0, HALVES, NB)
        r_q = carve(1024, TOK)
        r_neg = carve(1280, TOK)
        r_sig = carve(1536, TOK)
        r_f = carve(1792, TOK)
        r_R = carve(2048, LEVELS, P)
        r_K = carve(3072, LEVELS, TOK)
        r_tot = carve(5120, 2 * TOK)
        r_A = carve(5632, GROUPS * P)
        r_sgate = carve(6016, HALVES, P)
        r_G = carve(6272, HALVES, P)
        r_o = carve(6528, HALVES, P)
        r_v = carve(6784, HALVES, P)
        rmask = sb("rmask", [P, SCORES], mybir.dt.bfloat16)
        r_prod = carve(2048, HALVES, SCORES)
        r_ms = stat[:, 32:34]
        r_rs = stat[:, 36:38]
        r_x = stat[:, 38:40]
        r_t = stat[:, 40:42]

        m_h = carve(0, HALVES, NB)
        hid_hi, hid_lo = c_hi[:, 0:8, :], c_lo[:, 0:8, :]

        pairA = psum("pairA", [P, HALVES, NB])
        pairB = psum("pairB", [P, HALVES, NB])
        pairS = psum("pairS", [P, HALVES, NB])
        bankX = psum("bankX", [P, NB])
        bankO = psum("bankO", [P, NB])
        turn_bank = [bankX[:], bankO[:], pairS[:, 0], pairS[:, 1]]

        def out_pair(b, n):
            if b == 0:
                return pairA if n % 2 else pairB
            if n < 4:
                return pairS if n == 1 else pairA
            return pairB if n % 2 else pairA

        landed = [sem(f"landed{s}") for s in range(RAW)]
        hi_made, lo_made, tiles_used = sem("hi_made"), sem("lo_made"), sem("tiles_used")
        x_in = [sem(f"x_in{c}") for c in range(COLS)]
        pos_in, bound_in, rgain_in = sem("pos_in"), sem("bound_in"), sem("rgain_in")
        gain0_in = [sem(f"gain0_in{c}") for c in range(COLS)]
        pre_in, post_in = sem("pre_in"), sem("post_in")
        out_sent = sem("out_sent")
        ident_ready, masks_ready, pool_steps = sem("ident_ready"), sem("masks_ready"), sem("pool_steps")
        v_setup, act_setup = sem("v_setup"), sem("act_setup")
        amask_ready, angle_ready, sines_ready, rope_ready = (
            sem("amask_ready"), sem("angle_ready"), sem("sines_ready"), sem("rope_ready"))
        bexp_in, bexp_out = sem("bexp_in"), sem("bexp_out")
        zmem = sem("zmem")

        def norm_sems(b):
            names = ["steps"]
            if b > 0:
                names += ["ssq_y_made", "gained", "mean_y_made", "root_y_made", "h_new"]
            if b < 4:
                names += ["hg_made", "turned", "u_hi_made", "u_lo_made", "ssq_h_made", "mean_h_made",
                          "root_h_made", "rstd_u_made"]
            return {n: sem(f"n{b}_{n}") for n in names}

        NORM = [norm_sems(b) for b in range(5)]

        a_half = sem("a_half")
        a_evac = sem("a_evac")
        a_rot = sem("a_rot")
        a_vcopied = sem("a_vcopied")
        a_turned = sem("a_turned")
        a_qk = sem("a_qk")
        a_scored = sem("a_scored")
        a_maxed = sem("a_maxed")
        a_probs = sem("a_probs")
        a_rs = sem("a_rs")
        a_pturned = sem("a_pturned")
        a_pt = sem("a_pt")
        a_pv = sem("a_pv")
        a_out = sem("a_out")
        a_oturned = sem("a_oturned")
        a_ohi = sem("a_ohi")
        a_olo = sem("a_olo")
        a_steps = sem("a_steps")

        r_half, r_evac, r_qfT, r_sigs, r_qcopied, r_sgated, r_vcopied = (
            sem("r_half"), sem("r_evac"), sem("r_qfT"), sem("r_sigs"), sem("r_qcopied"), sem("r_sgated"),
            sem("r_vcopied"))
        r_levels, r_scored, r_att, r_across = sem("r_levels"), sem("r_scored"), sem("r_att"), sem("r_across")
        r_pv, r_ssq, r_out, r_gate = sem("r_pv"), sem("r_ssq"), sem("r_out"), sem("r_gate")
        r_oturned, r_ohi, r_olo = sem("r_oturned"), sem("r_ohi"), sem("r_olo")
        r_front_steps, r_back_steps = sem("r_front_steps"), sem("r_back_steps")

        y_add = [sem(f"y_add{b}") for b in range(4)]
        f_half = [sem(f"f_half{b}") for b in range(2)]
        f_relu = [sem(f"f_relu{b}") for b in range(2)]
        f_hid = [sem(f"f_hid{b}") for b in range(2)]
        f_turned = [sem(f"f_turned{b}") for b in range(2)]
        f_hi = [sem(f"f_hi{b}") for b in range(2)]
        f_lo = [sem(f"f_lo{b}") for b in range(2)]

        block = ctx.enter_context(nc.Block())

        @block.sync
        def _(sp):
            def load(stream, width, index, base, i, per, t):
                slot = (base + t) % RAW
                at = index if isinstance(index, int) else sp.snap(index)
                if base + t >= RAW or not isinstance(i, int) or i:
                    sp.wait_ge(lo_made, i * per + (base + t - RAW + 1))
                src = stream[at] if isinstance(at, int) else stream[bass.ds(at, 1)].squeeze(0)
                sp.dma_start(raw[:, slot, 0:width], src).then_inc(landed[slot], 16)

            def mlp_loads(layer, base):
                for t in range(FF_TILES):
                    load(s_up, KK * NB, layer * P + t, base, 0, 0, t)
                with sp.Fori(0, FF_BLOCKS - 1) as i:
                    for t in range(FF_TILES):
                        load(s_up, KK * NB, i * FF_TILES + (layer * P + FF_TILES + t),
                             base + FF_TILES, i, 2 * FF_TILES, t)
                    for t in range(FF_TILES):
                        load(s_down, KK * NB, i * FF_TILES + (layer * P + t),
                             base + 2 * FF_TILES, i, 2 * FF_TILES, t)
                for t in range(FF_TILES):
                    load(s_down, KK * NB, layer * P + (FF_BLOCKS - 1) * FF_TILES + t,
                         base + (2 * FF_BLOCKS - 1) * FF_TILES, 0, 0, t)

            for c in range(COLS):
                cols = slice(c * NB, (c + 1) * NB)
                sp.dma_start(h[:, :, cols],
                             x.rearrange("(m p) d -> p m d", p=P)[:, :, cols]).then_inc(x_in[c], 16)
                sp.dma_start(gain_pre[:, cols],
                             norm_gains[0, 0, cols].partition_broadcast(P)).then_inc(gain0_in[c], 16)
                for t in (2 * c, 2 * c + 1):
                    load(s_att_in, KK * ATT_W, t, AT_ATT, 0, 0, t)
            sp.dma_start(pos_i[:], positions).then_inc(pos_in, 16)
            sp.dma_start(bounds[:, 0, :], lower_bound).then_inc(bound_in, 16)
            sp.dma_start(rgain[:], rec_gain).then_inc(rgain_in, 16)
            for t in range(RAW, ATT_TILES):
                load(s_att_in, KK * ATT_W, t, AT_ATT, 0, 0, t)
            with sp.Fori(1, ATT_HEADS) as hd:
                for t in range(ATT_TILES):
                    load(s_att_in, KK * ATT_W, hd * ATT_TILES + t, AT_ATT, hd, ATT_TILES, t)
            for t in range(AT_FF0 - AT_ATT_OUT):
                load(s_att_out, KK * NB, t, AT_ATT_OUT, 0, 0, t)
            mlp_loads(0, AT_FF0)
            for t in range(REC_TILES):
                load(s_rec_in, KK * NB, t, AT_REC, 0, 0, t)
            with sp.Fori(1, REC_HEADS) as hd:
                for t in range(REC_TILES):
                    load(s_rec_in, KK * NB, hd * REC_TILES + t, AT_REC, hd, REC_TILES, t)
            for t in range(AT_FF1 - AT_REC_OUT):
                load(s_rec_out, KK * NB, t, AT_REC_OUT, 0, 0, t)
            mlp_loads(1, AT_FF1)
            for c in range(COLS):
                sp.wait_ge(NORM[4]["h_new"], HALVES * (c + 1))
                sp.dma_start(out.rearrange("(m p) d -> p m d", p=P)[:, :, c * NB:(c + 1) * NB],
                             h[:, :, c * NB:(c + 1) * NB]).then_inc(out_sent, 16)
            sp.wait_ge(out_sent, 16 * COLS)

        @block.gpsimd
        def _(pool):
            pool_s = Steps(pool, pool_steps)
            pool_s.note(nc.gpsimd.memset(ident[:], 0.0))
            pool_s.note(nc.gpsimd.memset(amask, 0.0))
            pool_s.note(nc.gpsimd.memset(rmask[:], 1.0))
            pool_s.last()
            nc.gpsimd.affine_select(out=ident[:], in_=ident[:], compare_op=ALU.not_equal, fill=1.0, base=0,
                                    pattern=[[-1, P]], channel_multiplier=1).then_inc(ident_ready, 1)
            pool_s.link(nc.gpsimd.affine_select(out=amask, in_=amask, compare_op=ALU.is_ge, fill=MASKED,
                                                base=P, pattern=[[0, GROUPS], [-1, TOK]], channel_multiplier=1))
            for g in range(GROUPS):
                if WINDOW[g] < TOK:
                    pool_s.link(nc.gpsimd.affine_select(
                        out=amask[:, g, :], in_=amask[:, g, :], compare_op=ALU.is_ge, fill=MASKED,
                        base=WINDOW[g] - P, pattern=[[1, TOK]], channel_multiplier=-1))
            for j in range(MASK_LEVELS):
                w = 1 << j
                view = rmask[:, j * 64:(j + 1) * 64].rearrange("p (b w) -> p b w", w=w)
                pool_s.link(nc.gpsimd.affine_select(out=view, in_=view, compare_op=ALU.is_ge, fill=0.0, base=0,
                                                    pattern=[[-2 * w, P // 2 // w], [0, w]], channel_multiplier=1))
                pool_s.link(nc.gpsimd.affine_select(out=view, in_=view, compare_op=ALU.is_ge, fill=0.0, base=w - 1,
                                                    pattern=[[2 * w, P // 2 // w], [0, w]], channel_multiplier=-1))
            pool_s.link(nc.gpsimd.affine_select(out=rmask[:, SCORES - P:SCORES], in_=rmask[:, SCORES - P:SCORES],
                                                compare_op=ALU.is_equal, fill=0.0, base=0,
                                                pattern=[[-1, P]], channel_multiplier=1))
            nc.gpsimd.memset(eps_col, EPS).then_inc(masks_ready, 1)
            for layer in range(2):
                pool.wait_ge(NORM[1 + 2 * layer]["u_lo_made"], COLS * HALVES)
                for m in range(HALVES):
                    nc.gpsimd.memset(y[:, m, :], 0.0).then_inc(y_add[1 + 2 * layer], 1)

        @block.tensor
        def _(pe):
            def three_pass(dst, s_hi, s_lo, slot, kk, width, first, last):
                wh = w_hi[:, slot, kk * width:(kk + 1) * width]
                wl = w_lo[:, slot, kk * width:(kk + 1) * width]
                pe.matmul(dst, s_hi, wh, start=first, stop=False)
                pe.matmul(dst, s_hi, wl, start=False, stop=False)
                return pe.matmul(dst, s_lo, wh, start=False, stop=last)

            def tile(pair, s_hi, s_lo, chunk0, at, i, per, width, first, last, half_sem=None, free=None,
                     ready=None):
                slot = at % SPLIT
                pe.wait_ge(lo_made, i * per + (at + 1))
                for m in range(HALVES):
                    if first and free is not None:
                        free(m)
                    if ready is not None:
                        ready(m)
                    for kk in range(KK):
                        k = chunk0 + kk
                        mm = three_pass(pair[:, m, 0:width], s_hi[:, k, m * P:(m + 1) * P],
                                        s_lo[:, k, m * P:(m + 1) * P], slot, kk, width,
                                        first and kk == 0, last and kk == KK - 1)
                    if m == 0 and last and half_sem is not None:
                        mm.then_inc(half_sem, 1)
                mm.then_inc(tiles_used, 1)

            def turn_block(b, c):
                n = NORM[b]
                for m in range(HALVES):
                    q = c * HALVES + m
                    pe.wait_ge(n["hg_made"], q + 1)
                    if q >= 4:
                        pe.wait_ge(n["u_lo_made"], q - 3)
                    for j in range(4):
                        t = pe.transpose(turn_bank[q % 4][:, j * P:(j + 1) * P],
                                         y[:, m, c * NB + j * P:c * NB + (j + 1) * P], ident[:])
                    t.then_inc(n["turned"], 1)

            def wait_u(b, t, m):
                pe.wait_ge(NORM[b]["u_lo_made"], HALVES * (t * KK // 4) + m + 1)

            def turn_next(b, t):
                if t % 2 == 0 and t // 2 + 1 < COLS:
                    turn_block(b, t // 2 + 1)

            def att_turn(hp, g):
                if g == 0:
                    pe.wait_ge(a_rot, hp + 1)
                if g == 2:
                    pe.wait_ge(a_qk, hp * 3 + 1)
                bank = bankO if g == 1 else bankX
                for j in range(4):
                    src = az[:, j % 2, 3 * g + j // 2, :]
                    t = pe.transpose(bank[:, j * P:(j + 1) * P], src, ident[:])
                t.then_inc(a_turned, 1)

            def att_scores(hp, m):
                if m == 1:
                    pe.wait_ge(a_qk, hp * 3 + 3)
                keys = (m + 1) * P
                flat = pairS[:].rearrange("p m n -> p (m n)")
                for g in range(GROUPS):
                    mm = pe.matmul(flat[:, g * keys:(g + 1) * keys], a_qkT[:, g, m * P:(m + 1) * P],
                                   a_qkT[:, g, TOK:TOK + keys], start=True, stop=True)
                mm.then_inc(a_scored, 1)

            def att_turn_probs(hp, m):
                pe.wait_ge(a_probs, hp * 2 + (2 - m))
                flat = pairS[:].rearrange("p m n -> p (m n)")
                for j in range(GROUPS * (m + 1)):
                    t = pe.transpose(flat[:, j * P:(j + 1) * P], a_p[:, j * P:(j + 1) * P], ident[:])
                t.then_inc(a_pturned, 1)

            def att_pv(hp, m):
                pe.wait_ge(a_pt, hp * 2 + (2 - m))
                pe.wait_ge(a_vcopied, hp + 1)
                if m == 0:
                    pe.wait_ge(a_out, hp * 2 + 1)
                n = GROUPS * (m + 1)
                for j in range(n):
                    mm = pe.matmul(bankO[:, m * P:(m + 1) * P], a_pT[:, j * P:(j + 1) * P],
                                   a_v[:, j % (m + 1), j // (m + 1), :], start=(j == 0), stop=(j == n - 1))
                mm.then_inc(a_pv, 1)

            def att_turn_out(hp):
                pe.wait_ge(a_out, hp * 2 + 2)
                for m in range(HALVES):
                    t = pe.transpose(bankX[:, m * P:(m + 1) * P], a_o[:, m, :], ident[:])
                t.then_inc(a_oturned, 1)

            def att_block_free(hd, g):
                def free(m):
                    back = {0: 1, 1: 3, 2: 2}[g]
                    if not isinstance(hd, int) or hd * 3 + g - back >= 0:
                        pe.wait_ge(a_evac, hd * 6 + ((g - back) * 2 + 1 + m))
                return free

            def att_project(hd, prev):
                for t in range(ATT_TILES):
                    g, tb = divmod(t, ATT_BLOCK_TILES)
                    first_block = isinstance(hd, int) and hd == 0 and g == 0
                    tile(pairB if g == 1 else pairA, u_hi, u_lo, tb * KK, AT_ATT + t, hd, ATT_TILES, ATT_W,
                         tb == 0, tb == ATT_BLOCK_TILES - 1, a_half, att_block_free(hd, g),
                         (lambda m: wait_u(0, tb, m)) if first_block else None)
                    if first_block:
                        turn_next(0, tb)
                    if prev is None:
                        continue
                    if t == 2:
                        att_turn(prev, 0)
                        att_turn(prev, 1)
                    if t == 3:
                        att_turn(prev, 2)
                    if t == 5:
                        att_scores(prev, 1)
                    if t == 7:
                        att_turn_probs(prev, 1)
                    if t == 9:
                        att_pv(prev, 1)
                        att_scores(prev, 0)
                    if t == 12:
                        att_turn_probs(prev, 0)
                    if t == 14:
                        att_pv(prev, 0)
                    if t == 16:
                        att_turn_out(prev)

            def out_tile(t, base, b, evac_sem, half_sem):
                kq, c, pr = t // 8, t // 2 % 4, t % 2
                n = t // 2

                def free(m):
                    if b == 0 and n < 2:
                        pe.wait_ge(evac_sem, 6 * ATT_HEADS - 3 + 2 * n + m)
                    elif b == 0:
                        pe.wait_ge(y_add[b], n - 1)
                    elif n == 0:
                        pe.wait_ge(evac_sem, 2 * REC_HEADS - 1 + m)
                    elif n != 1:
                        pe.wait_ge(y_add[b], {2: 1, 3: 3, 4: 4}.get(n, n - 1))

                tile(out_pair(b, n), c_hi, c_lo, kq * 4 + pr * KK, base + t, 0, 0, NB, pr == 0, pr == 1,
                     half_sem, free)

            pe.wait_ge(ident_ready, 1)
            turn_block(0, 0)
            att_project(0, None)
            with pe.Fori(1, ATT_HEADS) as hd:
                att_project(hd, hd - 1)
            hp = ATT_HEADS - 1
            for t in range(16):
                if t == 0:
                    pe.wait_ge(a_olo, 4)
                if t == 8:
                    pe.wait_ge(a_olo, 6)
                if t == 9:
                    pe.wait_ge(a_olo, ATT_HEADS)
                out_tile(t, AT_ATT_OUT, 0, a_evac, a_half if t == 15 else None)
                if t == 0:
                    att_turn(hp, 0)
                    att_turn(hp, 1)
                if t == 1:
                    att_turn(hp, 2)
                    att_scores(hp, 1)
                if t == 2:
                    att_turn_probs(hp, 1)
                if t == 3:
                    att_pv(hp, 1)
                    att_scores(hp, 0)
                if t == 5:
                    att_turn_probs(hp, 0)
                if t == 6:
                    att_pv(hp, 0)
                if t == 7:
                    att_turn_out(hp)

            def up(layer, base, i, t, first_block):
                def free(m):
                    if not first_block:
                        pe.wait_ge(f_relu[layer], i * 2 + (1 + m))

                tile(pairA, u_hi, u_lo, t * KK, base + t, 0 if isinstance(i, int) else i, 2 * FF_TILES, NB,
                     t == 0, t == FF_TILES - 1, f_half[layer], free,
                     (lambda m: wait_u(1 + 2 * layer, t, m)) if first_block else None)
                if first_block:
                    turn_next(1 + 2 * layer, t)

            def turn_hidden(layer, i):
                for m in range(HALVES):
                    pe.wait_ge(f_hid[layer], i * 2 + (1 + m))
                    bank = bankO if m else bankX
                    for j in range(4):
                        t = pe.transpose(bank[:, j * P:(j + 1) * P], m_h[:, m, j * P:(j + 1) * P], ident[:])
                    t.then_inc(f_turned[layer], 1)

            def down(layer, base, i, t):
                c, pr = divmod(t, 2)
                if t == 0:
                    pe.wait_ge(f_lo[layer], i * 2 + 2)

                def free(m):
                    pe.wait_ge(y_add[1 + 2 * layer], i * 4 + (c + 1))

                last = isinstance(i, int) and i == FF_BLOCKS - 1
                tile(pairS if c % 2 else pairB, hid_hi, hid_lo, 4 * last + pr * KK, base + t,
                     0 if isinstance(i, int) else i, 2 * FF_TILES, NB, pr == 0, pr == 1,
                     f_half[layer] if last and t == FF_TILES - 1 else None, free)

            def mlp(layer, base):
                turn_block(1 + 2 * layer, 0)
                for t in range(FF_TILES):
                    up(layer, base, 0, t, True)
                with pe.Fori(0, FF_BLOCKS - 2) as i:
                    for t in range(FF_TILES):
                        up(layer, base + FF_TILES, i, t, False)
                        if t == 1:
                            turn_hidden(layer, i)
                    for t in range(FF_TILES):
                        down(layer, base + 2 * FF_TILES, i, t)
                last = FF_BLOCKS - 1
                at = base + (2 * last - 1) * FF_TILES
                for t in range(FF_TILES):
                    up(layer, at, last - 1, t, False)
                    if t == 1:
                        turn_hidden(layer, last - 1)
                for t in range(FF_TILES):
                    down(layer, at + FF_TILES, last - 1, t)
                    if t == 3:
                        turn_hidden(layer, last)
                for t in range(FF_TILES):
                    down(layer, at + 2 * FF_TILES, last, t)

            mlp(0, AT_FF0)

            def rec_turn(hp):
                pe.wait_ge(r_evac, hp * 2 + 2)
                if not isinstance(hp, int) or hp > 0:
                    pe.wait_ge(r_olo, hp)
                for j in range(4):
                    t = pe.transpose(bankX[:, j * P:(j + 1) * P], rz[:, j % 2, (j // 2) * P:(j // 2 + 1) * P],
                                     ident[:])
                t.then_inc(r_qfT, 1)

            def rec_scores(hp):
                pe.wait_ge(r_levels, hp + 1)
                for m in range(HALVES):
                    half, right = m * P, m * P // 2
                    for j in range(MASK_LEVELS):
                        pe.matmul(pairS[:, m, j * 64:(j + 1) * 64], r_K[:, j, half:half + P],
                                  r_R[:, j, right:right + 64], start=True, stop=True)
                    pe.matmul(pairS[:, m, 320:448], r_K[:, 0, half:half + P], r_q[:, half:half + P],
                              start=True, stop=True)
                    for b in range(2):
                        pe.matmul(pairB[64 * b:64 * b + 32, 0, half + 64 * b + 32:half + 64 * b + 64],
                                  r_K[:, 5, half + 64 * b:half + 64 * b + 32],
                                  r_R[:, 5, right + 32 * b:right + 32 * b + 32], start=True, stop=True)
                    pe.matmul(pairB[0:64, 0, half + 64:half + P], r_K[:, 6, half:half + 64],
                              r_R[:, 6, right:right + 64], start=True, stop=True)
                pe.matmul(pairB[:, 0, 2 * P:3 * P], r_K[:, 7, 0:P], r_R[:, 7, :], start=True,
                          stop=True).then_inc(r_scored, 1)

            def rec_pv(hp):
                pe.wait_ge(r_att, hp + 1)
                pe.wait_ge(r_across, hp + 1)
                pe.wait_ge(r_vcopied, hp + 1)
                v = [r_v[:, m, :] for m in range(HALVES)]
                pe.matmul(bankO[:, 0:P], r_A[:, 0:P], v[0], start=True, stop=True)
                pe.matmul(bankO[:, P:2 * P], r_A[:, P:2 * P], v[1], start=True, stop=False)
                pe.matmul(bankO[:, P:2 * P], r_A[:, 2 * P:3 * P], v[0], start=False, stop=True).then_inc(r_pv, 1)

            def rec_turn_out(hp, last=False):
                pe.wait_ge(r_out, hp + 1)
                pe.wait_ge(r_qcopied, hp + 1 if last else hp + 2)
                for m in range(HALVES):
                    t = pe.transpose(bankX[:, m * P:(m + 1) * P], r_o[:, m, :], ident[:])
                t.then_inc(r_oturned, 1)

            def rec_mix(t, front, back):
                if t == 0 and front is not None:
                    rec_turn(front)
                if t == 0 and back is not None:
                    rec_pv(back)
                if t == 3 and back is not None:
                    rec_turn_out(back, last=front is None)
                if t == 5 and front is not None:
                    rec_scores(front)

            turn_block(2, 0)
            for t in range(REC_TILES):
                tile(pairA, u_hi, u_lo, t * KK, AT_REC + t, 0, 0, NB, t == 0, t == REC_TILES - 1, r_half, None,
                     lambda m: wait_u(2, t, m))
                turn_next(2, t)

            def rec_project(hd, front, back):
                for t in range(REC_TILES):
                    tile(pairA, u_hi, u_lo, t * KK, AT_REC + t, hd, REC_TILES, NB, t == 0, t == REC_TILES - 1,
                         r_half, lambda m: pe.wait_ge(r_evac, hd * 2 + (m - 1)))
                    rec_mix(t, front, back)

            rec_project(1, 0, None)
            with pe.Fori(2, REC_HEADS) as hd:
                rec_project(hd, hd - 1, hd - 2)
            for t in range(32):
                if t == 0:
                    pe.wait_ge(r_olo, 5)
                if t == 24:
                    pe.wait_ge(r_olo, REC_HEADS + 1)
                out_tile(t, AT_REC_OUT, 2, r_evac, r_half if t == 31 else None)
                if t == 5:
                    pe.wait_ge(y_add[2], 2)
                if t < 8:
                    rec_mix(t, REC_HEADS - 1, REC_HEADS - 2)
                elif t < 16:
                    rec_mix(t - 8, None, REC_HEADS - 1)

            mlp(1, AT_FF1)

        @block.scalar
        def _(act):
            def high(at, i, per, width=KK * NB):
                if isinstance(i, int) and i * per + at >= TILES:
                    return
                slot, rounds = at % RAW, per // RAW
                act.wait_ge(landed[slot], i * (16 * rounds) + 16 * (at // RAW + 1))
                if at >= SPLIT or not isinstance(i, int):
                    act.wait_ge(tiles_used, i * per + (at - SPLIT + 1))
                nc.scalar.activation(w_hi[:, at % SPLIT, 0:width], raw[:, slot, 0:width],
                                     ACT.Copy).then_inc(hi_made, 1)

            def square_y(b, c, count):
                n = NORM[b]
                if c == 0:
                    nc.scalar.activation(stat[:, 44 + b:45 + b], eps_col, ACT.Sqrt)
                act.wait_ge(y_add[b - 1], count)
                for m in range(HALVES):
                    if c == COLS - 1 and m:
                        act.wait_ge(y_add[b - 1], count + 1)
                    if c or m:
                        act.wait_ge(n["ssq_y_made"], c * HALVES + m)
                    nc.scalar.activation(junk[:], y[:, m, c * NB:(c + 1) * NB], ACT.Square,
                                         accum_out=ssq_y[:, m, c:c + 1]).then_inc(n["ssq_y_made"], 1)

            def root_y(b):
                act.wait_ge(NORM[b]["mean_y_made"], 1)
                nc.scalar.activation(rstd_y, mean_y, ACT.Sqrt).then_inc(NORM[b]["root_y_made"], 1)

            def high_u(b, c):
                n = NORM[b]
                for m in range(HALVES):
                    q = c * HALVES + m
                    act.wait_ge(n["turned"], q + 1)
                    nc.scalar.activation(u_hi[:, 4 * c:4 * c + 4, m * P:(m + 1) * P],
                                         turn_bank[q % 4].rearrange("p (k t) -> p k t", k=4),
                                         ACT.Copy).then_inc(n["u_hi_made"], 1)

            def square_h(b, c):
                n = NORM[b]
                for m in range(HALVES):
                    q = c * HALVES + m
                    if b:
                        act.wait_ge(n["h_new"], q + 1)
                    else:
                        act.wait_ge(x_in[c], 16)
                    if q:
                        act.wait_ge(n["ssq_h_made"], q)
                    elif b:
                        act.wait_ge(n["ssq_y_made"], COLS * HALVES)
                    nc.scalar.activation(junk[:], h[:, m, c * NB:(c + 1) * NB], ACT.Square,
                                         accum_out=ssq_h[:, m, c:c + 1]).then_inc(n["ssq_h_made"], 1)

            def first_before(b, t):
                if t % 2 == 0 and t // 2 + 1 < COLS:
                    high_u(b, t // 2 + 1)
                if t == 7:
                    act.wait_ge(NORM[b]["rstd_u_made"], 1)

            def first_after(b, t, post, pre):
                if t in (0, 1, 2, 4):
                    square_h(b, {0: 0, 1: 1, 2: 2, 4: 3}[t])
                if t == 5:
                    act.wait_ge(NORM[b]["mean_h_made"], 1)
                    nc.scalar.activation(rstd_u, mean_h, ACT.Sqrt).then_inc(NORM[b]["root_h_made"], 1)
                    act.wait_ge(NORM[b]["hg_made"], COLS * HALVES)
                    act.dma_start(gain_post[:], post.partition_broadcast(P)).then_inc(post_in, 16)
                    if pre is not None:
                        act.dma_start(gain_pre[:], pre.partition_broadcast(P)).then_inc(pre_in, 16)

            def att_evacuate(hd, g):
                pair = pairB if g == 1 else pairA
                for m in range(HALVES):
                    if m == 0:
                        act.wait_ge(a_half, hd * 3 + (g + 1))
                    else:
                        act.wait_ge(tiles_used, hd * ATT_TILES + (AT_ATT + (g + 1) * ATT_BLOCK_TILES))
                    nc.scalar.activation(az[:, m, 3 * g:3 * g + 3, :],
                                         pair[:, m, 0:ATT_W].rearrange("p (s n) -> p s n", s=3), ACT.Copy,
                                         scale=rstd_u[:, m:m + 1]).then_inc(a_evac, 1)

            def att_copy_v(hp):
                act.wait_ge(a_evac, hp * 6 + 6)
                for m in range(HALVES):
                    ins = nc.scalar.activation(a_v[:, m, :, :], az[:, m, 2:9:3, :], ACT.Copy)
                ins.then_inc(a_vcopied, 1)

            def att_copy_qk(hp, g):
                act.wait_ge(a_turned, hp * 3 + (g + 1))
                bank = bankO if g == 1 else bankX
                nc.scalar.activation(a_qkT[:, g, :], bank[:], ACT.Copy).then_inc(a_qk, 1)

            def att_exp(hp, m):
                act.wait_ge(a_maxed, hp * 2 + (2 - m))
                n = GROUPS * (m + 1) * P
                nc.scalar.activation(a_p[:, 0:n], a_p[:, 0:n], ACT.Exp, bias=a_max[:, m:m + 1],
                                     accum_out=a_sum[:, m:m + 1]).then_inc(a_probs, 1)

            def att_copy_pt(hp, m):
                act.wait_ge(a_pturned, hp * 2 + (2 - m))
                n = GROUPS * (m + 1) * P
                flat = pairS[:].rearrange("p m n -> p (m n)")
                nc.scalar.activation(a_pT[:, 0:n], flat[:, 0:n], ACT.Copy).then_inc(a_pt, 1)

            def att_output(hp, m):
                act.wait_ge(a_pv, hp * 2 + (2 - m))
                act.wait_ge(a_rs, hp * 2 + (2 - m))
                nc.scalar.activation(a_o[:, m, :], bankO[:, m * P:(m + 1) * P], ACT.Copy,
                                     scale=a_rsum[:, m:m + 1]).then_inc(a_out, 1)

            def att_high(hp):
                act.wait_ge(a_oturned, hp + 1)
                dst = c_hi[:, hp, :] if isinstance(hp, int) else c_hi[:, bass.ds(hp, 1), :].squeeze(1)
                nc.scalar.activation(dst, bankX[:, 0:TOK], ACT.Copy).then_inc(a_ohi, 1)

            def att_head(hd, prev, last=False):
                for t in range(ATT_TILES):
                    if prev is not None:
                        if t == 0:
                            att_copy_v(prev)
                        if t == 2:
                            att_copy_qk(prev, 0)
                            att_copy_qk(prev, 1)
                        if t == 3:
                            att_copy_qk(prev, 2)
                        if t == 6:
                            att_exp(prev, 1)
                        if t == 8:
                            att_copy_pt(prev, 1)
                        if t == 10:
                            att_output(prev, 1)
                        if t == 11:
                            att_exp(prev, 0)
                        if t == 13:
                            att_copy_pt(prev, 0)
                        if t == 15:
                            att_output(prev, 0)
                        if t == 17:
                            att_high(prev)
                    first_block = prev is None and t < ATT_BLOCK_TILES
                    if first_block:
                        first_before(0, t)
                    if prev is None and t == 13:
                        act.wait_ge(angle_ready, 1)
                        nc.scalar.activation(rope[:, 0, :, :], rope[:, 0, :, :], ACT.Sin)
                        nc.scalar.activation(rope[:, 1, :, :], rope[:, 1, :, :], ACT.Sin).then_inc(sines_ready, 1)
                    if prev is None and t == 14:
                        act.wait_ge(bexp_in, 1)
                        nc.scalar.activation(bounds[:, 1, :], bounds[:, 1, :], ACT.Exp).then_inc(bexp_out, 1)
                    if t % ATT_BLOCK_TILES == ATT_BLOCK_TILES - 1:
                        att_evacuate(hd, t // ATT_BLOCK_TILES)
                    into_next = last and t + SPLIT >= ATT_TILES
                    high(AT_ATT + t + SPLIT, hd, ATT_TILES, KK * (NB if into_next else ATT_W))
                    if first_block:
                        first_after(0, t, norm_gains[0, 1], norm_gains[0, 2])

            high(0, 0, 0, KK * ATT_W)
            high_u(0, 0)
            for t in range(1, SPLIT):
                high(t, 0, 0, KK * ATT_W)
            att_head(0, None)
            with act.Fori(1, ATT_HEADS - 1) as hd:
                att_head(hd, hd - 1)
            att_head(ATT_HEADS - 1, ATT_HEADS - 2, last=True)
            hp = ATT_HEADS - 1
            for t in range(16):
                if t == 0:
                    att_copy_v(hp)
                    att_copy_qk(hp, 0)
                    att_copy_qk(hp, 1)
                if t == 1:
                    att_copy_qk(hp, 2)
                    att_exp(hp, 1)
                if t == 2:
                    att_copy_pt(hp, 1)
                if t == 3:
                    att_output(hp, 1)
                if t == 4:
                    att_exp(hp, 0)
                if t == 5:
                    att_copy_pt(hp, 0)
                if t == 6:
                    att_output(hp, 0)
                if t == 7:
                    att_high(hp)
                if t >= 10 and t % 2 == 0:
                    square_y(1, (t - 10) // 2, 4 + (t - 8) // 2)
                if t < 15:
                    high(AT_ATT_OUT + t + SPLIT, 0, 0)
            square_y(1, COLS - 1, 8)

            def hidden(layer, i, used):
                for m in range(HALVES):
                    if m == 0:
                        act.wait_ge(f_half[layer], i + 1)
                    else:
                        act.wait_ge(tiles_used, used)
                    nc.scalar.activation(m_h[:, m, :], pairA[:, m, :], ACT.Relu,
                                         scale=rstd_u[:, m:m + 1]).then_inc(f_relu[layer], 1)
                for m in range(HALVES):
                    act.wait_ge(f_relu[layer], i * 2 + (1 + m))
                    nc.scalar.activation(m_h[:, m, :], m_h[:, m, :], ACT.Square).then_inc(f_hid[layer], 1)

            def hidden_high(layer, i):
                for m in range(HALVES):
                    act.wait_ge(f_turned[layer], i * 2 + (1 + m))
                    bank = bankO if m else bankX
                    at = 4 * (isinstance(i, int) and i == FF_BLOCKS - 1)
                    nc.scalar.activation(hid_hi[:, at:at + 4, m * P:(m + 1) * P],
                                         bank[:].rearrange("p (k t) -> p k t", k=4),
                                         ACT.Copy).then_inc(f_hi[layer], 1)

            def mlp(layer, base):
                b = 1 + 2 * layer
                root_y(b)
                high_u(b, 0)
                high(base + SPLIT - 1, 0, 0)
                for t in range(FF_TILES):
                    first_before(b, t)
                    if t == FF_TILES - 1:
                        hidden(layer, 0, base + FF_TILES)
                    high(base + t + SPLIT, 0, 0)
                    first_after(b, t, norm_gains[layer, 3], None if layer else norm_gains[1, 0])
                with act.Fori(0, FF_BLOCKS - 2) as i:
                    for t in range(2 * FF_TILES):
                        if t == 1:
                            hidden_high(layer, i)
                        if t == FF_TILES - 1:
                            hidden(layer, i + 1, i * (2 * FF_TILES) + (base + 2 * FF_TILES))
                        high(base + FF_TILES + t + SPLIT, i, 2 * FF_TILES)
                last = FF_BLOCKS - 1
                at = base + (2 * last - 1) * FF_TILES
                for t in range(2 * FF_TILES):
                    if t == 1:
                        hidden_high(layer, last - 1)
                    if t == FF_TILES - 1:
                        hidden(layer, last, at + FF_TILES)
                    if t == FF_TILES + 4:
                        hidden_high(layer, last)
                    high(at + t + SPLIT, 0, 0)
                for t in range(FF_TILES):
                    if t and t % 2 == 0:
                        square_y(b + 1, t // 2 - 1, 2 + 4 * last + t // 2)
                    if t < FF_TILES - 1:
                        high(at + 2 * FF_TILES + t + SPLIT, 0, 0)
                square_y(b + 1, COLS - 1, 2 + 4 * FF_BLOCKS)

            mlp(0, AT_FF0)

            def rec_evacuate(hd):
                for m in range(HALVES):
                    if m == 0:
                        act.wait_ge(r_half, hd + 1)
                        if not isinstance(hd, int) or hd > 0:
                            act.wait_ge(r_gate, hd)
                    else:
                        act.wait_ge(tiles_used, hd * REC_TILES + (AT_REC + REC_TILES))
                    nc.scalar.activation(rz[:, m, :], pairA[:, m, :], ACT.Copy,
                                         scale=rstd_u[:, m:m + 1]).then_inc(r_evac, 1)

            def rec_sigmoids(hp):
                act.wait_ge(r_qfT, hp + 1)
                nc.scalar.activation(r_sig, bankX[:, TOK:2 * TOK], ACT.Sigmoid).then_inc(r_sigs, 1)
                nc.scalar.activation(r_neg, bankX[:, TOK:2 * TOK], ACT.Sigmoid, scale=-1.0).then_inc(r_sigs, 1)
                nc.scalar.activation(r_q, bankX[:, 0:TOK], ACT.Copy).then_inc(r_qcopied, 1)

            def rec_values(hp):
                act.wait_ge(r_evac, hp * 2 + 2)
                if not isinstance(hp, int) or hp > 0:
                    act.wait_ge(r_pv, hp)
                nc.scalar.activation(r_v, rz[:, :, 2 * P:3 * P], ACT.Copy).then_inc(r_vcopied, 1)
                nc.scalar.activation(r_sgate, rz[:, :, 3 * P:4 * P], ACT.Sigmoid).then_inc(r_sgated, 1)

            def rec_across(hp):
                act.wait_ge(r_scored, hp + 1)
                nc.scalar.activation(r_A[:, TOK:3 * P], pairB[:, 0, TOK:3 * P], ACT.Copy).then_inc(r_across, 1)

            def rec_squares(hp):
                act.wait_ge(r_pv, hp + 1)
                for m in range(HALVES):
                    if m or not isinstance(hp, int) or hp > 0:
                        act.wait_ge(r_ssq, hp * 2 + m)
                    nc.scalar.activation(junk[:, 0:P], bankO[:, m * P:(m + 1) * P], ACT.Square,
                                         accum_out=r_ms[:, m:m + 1]).then_inc(r_ssq, 1)

            def rec_high(hp):
                act.wait_ge(r_oturned, hp + 1)
                dst = c_hi[:, hp, :] if isinstance(hp, int) else c_hi[:, bass.ds(hp, 1), :].squeeze(1)
                nc.scalar.activation(dst, bankX[:, 0:TOK], ACT.Copy, scale=rgain[:, 0:1]).then_inc(r_ohi, 1)

            def rec_mix(t, front, back):
                if t == 0 and front is not None:
                    rec_sigmoids(front)
                if t == 1 and back is not None:
                    rec_squares(back)
                if t == 3 and front is not None:
                    rec_values(front)
                if t == 4 and back is not None:
                    rec_high(back)
                if t == 6 and front is not None:
                    rec_across(front)

            def rec_head(hd, front, back):
                for t in range(REC_TILES):
                    first_block = isinstance(hd, int) and hd == 0
                    if first_block:
                        first_before(2, t)
                    rec_mix(t, front, back)
                    if t == REC_TILES - 1:
                        rec_evacuate(hd)
                    high(AT_REC + t + SPLIT, hd, REC_TILES)
                    if first_block:
                        first_after(2, t, norm_gains[1, 1], norm_gains[1, 2])

            root_y(2)
            high_u(2, 0)
            high(AT_REC + SPLIT - 1, 0, 0)
            act.wait_ge(rgain_in, 16)
            rec_head(0, None, None)
            rec_head(1, 0, None)
            with act.Fori(2, REC_HEADS) as hd:
                rec_head(hd, hd - 1, hd - 2)
            for t in range(32):
                if t < 8:
                    rec_mix(t, REC_HEADS - 1, REC_HEADS - 2)
                elif t < 16:
                    rec_mix(t - 8, None, REC_HEADS - 1)
                if t >= 26 and t % 2 == 0:
                    square_y(3, (t - 26) // 2, 12 + (t - 24) // 2)
                if t < 31:
                    high(AT_REC_OUT + t + SPLIT, 0, 0)
            square_y(3, COLS - 1, 16)

            mlp(1, AT_FF1)
            root_y(4)

        @block.vector
        def _(dve):
            V = nc.vector

            def low(at, i, per, width=KK * NB):
                if isinstance(i, int) and i * per + at >= TILES:
                    return
                dve.wait_ge(hi_made, i * per + (at + 1))
                V.tensor_tensor(w_lo[:, at % SPLIT, 0:width], raw[:, at % RAW, 0:width],
                                w_hi[:, at % SPLIT, 0:width].bitcast(F32), ALU.subtract).then_inc(lo_made, 1)

            def gain_y(b, c):
                n = NORM[b]
                cols = slice(c * NB, (c + 1) * NB)
                if c == 0:
                    dve.wait_ge(post_in, 16 * b)
                dve.wait_ge(n["ssq_y_made"], HALVES * (c + 1))
                V.tensor_tensor(y[:, :, cols], y[:, :, cols],
                                gain_post[:, None, cols].broadcast_to([P, HALVES, NB]),
                                ALU.mult).then_inc(n["gained"], 1)

            def root_y(b):
                n = NORM[b]
                s = Steps(dve, n["steps"])
                dve.wait_ge(n["ssq_y_made"], COLS * HALVES)
                s.link(V.tensor_reduce(mean_y, ssq_y, AX.X, ALU.add))
                V.tensor_scalar(mean_y, mean_y, 1.0 / D, EPS, ALU.mult, ALU.add).then_inc(n["mean_y_made"], 1)
                dve.wait_ge(n["root_y_made"], 1)
                s.link(V.reciprocal(rstd_y, rstd_y))

            def renew(b, c):
                n = NORM[b]
                cols = slice(c * NB, (c + 1) * NB)
                if b == 0:
                    dve.wait_ge(x_in[c], 16)
                    dve.wait_ge(gain0_in[c], 16)
                else:
                    if c == COLS - 1:
                        gain_y(b, c)
                    dve.wait_ge(n["gained"], c + 1)
                    if c == 0 and b < 4:
                        dve.wait_ge(pre_in, 16 * b)
                for m in range(HALVES):
                    if b > 0:
                        V.scalar_tensor_tensor(out=h[:, m, cols], in0=y[:, m, cols],
                                               scalar=rstd_y[:, m:m + 1], in1=h[:, m, cols],
                                               op0=ALU.mult, op1=ALU.add).then_inc(n["h_new"], 1)
                    if 0 < b < 4:
                        dve.wait_ge(n["h_new"], HALVES * c + m + 1)
                    if b < 4:
                        V.tensor_tensor(y[:, m, cols], h[:, m, cols], gain_pre[:, cols],
                                        ALU.mult).then_inc(n["hg_made"], 1)

            def low_u(b, c):
                n = NORM[b]
                for m in range(HALVES):
                    q = c * HALVES + m
                    dve.wait_ge(n["u_hi_made"], q + 1)
                    V.tensor_tensor(u_lo[:, 4 * c:4 * c + 4, m * P:(m + 1) * P],
                                    turn_bank[q % 4].rearrange("p (k t) -> p k t", k=4),
                                    u_hi[:, 4 * c:4 * c + 4, m * P:(m + 1) * P].bitcast(F32),
                                    ALU.subtract).then_inc(n["u_lo_made"], 1)

            def first_before(b, t):
                n = NORM[b]
                if t % 2 == 0 and t // 2 + 1 < COLS:
                    renew(b, t // 2 + 1)
                    low_u(b, t // 2 + 1)
                if t == 5:
                    s = Steps(dve, n["steps"], 2 if b else 0)
                    dve.wait_ge(n["ssq_h_made"], COLS * HALVES)
                    s.link(V.tensor_reduce(mean_h, ssq_h, AX.X, ALU.add))
                    V.tensor_scalar(mean_h, mean_h, 1.0 / D, EPS, ALU.mult, ALU.add).then_inc(n["mean_h_made"], 1)
                if t == 6:
                    dve.wait_ge(n["root_h_made"], 1)
                    V.reciprocal(rstd_u, rstd_u).then_inc(n["rstd_u_made"], 1)

            def setup_masks(s):
                dve.wait_ge(masks_ready, 1)
                dve.wait_ge(ident_ready, 1)
                onehot = carve(4608, 32)
                for g in range(GROUPS):
                    d = DILATION[g]
                    if d == 1:
                        continue
                    s.link(V.tensor_reduce(onehot[:, 0:d], ident[:].rearrange("p (b r) -> p r b", r=d),
                                           AX.X, ALU.add))
                    s.link(V.tensor_scalar(onehot[:, 0:d], onehot[:, 0:d], 1.0, -MASKED, ALU.subtract, ALU.mult))
                    view = amask[:, g, :].rearrange("p (b r) -> p b r", r=d)
                    s.link(V.tensor_tensor(view, view, onehot[:, None, 0:d].broadcast_to([P, TOK // d, d]),
                                           ALU.add))

            inv = carve(4640, HALF_ROPE)
            posf = carve(4672, HALVES)
            ang = carve(4704, HALVES, HALF_ROPE)
            turns = carve(4736, HALVES, HALF_ROPE)

            def setup_angles(s):
                half = HALF_ROPE
                freq = np.float32(ROPE_THETA) ** (-np.arange(half, dtype=np.float32) / np.float32(half))
                dve.wait_ge(pos_in, 16)
                s.note(V.tensor_copy(posf, pos_i[:]))
                for j in range(half):
                    s.note(V.memset(inv[:, j:j + 1], float(freq[j])))
                s.last()
                for m in range(HALVES):
                    s.note(V.tensor_scalar(ang[:, m, :], inv, posf[:, m:m + 1], None, ALU.mult))
                s.last()

            def setup_range(s):
                two_pi = 2 * np.pi
                part1 = 6.28125
                part2 = float(np.float32(np.round((two_pi - part1) * 2 ** 21) / 2 ** 21))
                part3 = float(np.float32(two_pi - part1 - part2))
                magic = 1.5 * 2 ** 23
                s.link(V.tensor_scalar(turns, ang, float(np.float32(1 / two_pi)), None, ALU.mult))
                s.link(V.tensor_scalar(turns, turns, magic, None, ALU.add))
                s.link(V.tensor_scalar(turns, turns, magic, None, ALU.subtract))
                for part in (part1, part2, part3):
                    s.link(V.scalar_tensor_tensor(out=ang, in0=turns, scalar=-part, in1=ang,
                                                  op0=ALU.mult, op1=ALU.add))
                pi = 3.1415925
                s.link(V.tensor_scalar(ang, ang, pi, -pi, ALU.min, ALU.max))
                s.note(V.tensor_scalar(rope[:, 0, :, :], ang, 0.5, None, ALU.mult))
                V.tensor_copy(rope[:, 1, :, :], ang).then_inc(angle_ready, 1)
                dve.wait_ge(bound_in, 16)
                V.tensor_tensor(bounds[:, 1, :], bounds[:, 0, :], bounds[:, 0, :],
                                ALU.subtract).then_inc(bexp_in, 1)

            def setup_cosines(s):
                dve.wait_ge(sines_ready, 1)
                s.link(V.tensor_tensor(rope[:, 0, :, :], rope[:, 0, :, :], rope[:, 0, :, :], ALU.mult))
                V.tensor_scalar(rope[:, 0, :, :], rope[:, 0, :, :], -2.0, 1.0, ALU.mult,
                                ALU.add).then_inc(rope_ready, 1)
                dve.wait_ge(rope_ready, 1)

            def setup_bounds(s):
                dve.wait_ge(bexp_out, 1)
                s.link(V.reciprocal(bounds[:, 2, :], bounds[:, 1, :]))
                s.link(V.tensor_tensor(bounds[:, 1, :], bounds[:, 1, :], bounds[:, 2, :], ALU.mult))
                s.link(V.tensor_tensor(bounds[:, 1, :], bounds[:, 1, :], bounds[:, 1, :], ALU.subtract))
                s.note(V.tensor_scalar(bounds[:, 2, :], bounds[:, 1, :], LB_FLOOR, None, ALU.max))
                s.link(V.tensor_scalar(bounds[:, 3, :], bounds[:, 1, :], -1.0, 1.0, ALU.mult, ALU.add))
                s.link(V.tensor_tensor(bounds[:, 4, :], bounds[:, 2, :], bounds[:, 1, :], ALU.subtract))

            def att_rotate(hp, s):
                dve.wait_ge(a_evac, hp * 6 + 6)
                cosx = a_cosx.rearrange("p (s j i) -> p s j i", s=9, j=2)
                sinx = a_sinx.rearrange("p (s j i) -> p s j i", s=9, j=2)
                for m in range(HALVES):
                    src = az[:, m, :, 0:32].rearrange("p s (j i) -> p s j i", j=2)
                    cos = rope[:, 0, m, :][:, None, None, :].broadcast_to([P, 9, 2, HALF_ROPE])
                    sin = rope[:, 1, m, :][:, None, None, :].broadcast_to([P, 9, 2, HALF_ROPE])
                    s.note(V.tensor_tensor(cosx, src, cos, ALU.mult))
                    s.note(V.tensor_tensor(sinx, src, sin, ALU.mult))
                    s.last()

                    def qk(view):
                        return view.rearrange("p (g s) i -> p g s i", g=GROUPS)[:, :, 0:2, :]

                    s.note(V.tensor_tensor(qk(az[:, m, :, 0:16]), qk(cosx[:, :, 0, :]), qk(sinx[:, :, 1, :]),
                                           ALU.subtract))
                    ins = V.tensor_tensor(qk(az[:, m, :, 16:32]), qk(cosx[:, :, 1, :]), qk(sinx[:, :, 0, :]),
                                          ALU.add)
                    if m == 0:
                        s.link(ins)
                    else:
                        ins.then_inc(a_rot, 1)

            def att_mask(hp, m, s):
                dve.wait_ge(a_scored, hp * 2 + (2 - m))
                n = (m + 1) * P
                flat = pairS[:].rearrange("p m n -> p (m n)")[:, 0:GROUPS * n]
                s.link(V.scalar_tensor_tensor(
                    out=a_p[:, 0:GROUPS * n].rearrange("p (g n) -> p g n", g=GROUPS),
                    in0=flat.rearrange("p (g n) -> p g n", g=GROUPS), scalar=float(P) ** -0.5,
                    in1=amask[:, :, TOK - n:TOK], op0=ALU.mult, op1=ALU.add))
                s.link(V.tensor_reduce(a_max[:, m:m + 1], a_p[:, 0:GROUPS * n], AX.X, ALU.max))
                V.tensor_scalar(a_max[:, m:m + 1], a_max[:, m:m + 1], -1.0, None,
                                ALU.mult).then_inc(a_maxed, 1)

            def att_rsum(hp, m):
                dve.wait_ge(a_probs, hp * 2 + (2 - m))
                V.reciprocal(a_rsum[:, m:m + 1], a_sum[:, m:m + 1]).then_inc(a_rs, 1)

            def att_low(hp):
                dve.wait_ge(a_ohi, hp + 1)
                if isinstance(hp, int):
                    hi, lo = c_hi[:, hp, :], c_lo[:, hp, :]
                else:
                    hi, lo = c_hi[:, bass.ds(hp, 1), :].squeeze(1), c_lo[:, bass.ds(hp, 1), :].squeeze(1)
                V.tensor_tensor(lo, bankX[:, 0:TOK], hi.bitcast(F32), ALU.subtract).then_inc(a_olo, 1)

            ATT_STEPS = 11

            def att_head(hd, prev, last=False):
                s = Steps(dve, a_steps, None if prev is None else prev * ATT_STEPS)
                setup = Steps(dve, v_setup)
                for t in range(ATT_TILES):
                    if prev is None and t < ATT_BLOCK_TILES:
                        first_before(0, t)
                    if prev is None and 9 <= t < 17 and t != 12 and t != 13 and t != 14:
                        {9: setup_masks, 10: setup_angles, 11: setup_range, 15: setup_cosines,
                         16: setup_bounds}[t](setup)
                    if prev is not None:
                        if t == 0:
                            att_rotate(prev, s)
                        if t == 5:
                            att_mask(prev, 1, s)
                        if t == 7:
                            att_rsum(prev, 1)
                        if t == 10:
                            att_mask(prev, 0, s)
                        if t == 12:
                            att_rsum(prev, 0)
                        if t == 17:
                            att_low(prev)
                    into_next = last and t + SPLIT >= ATT_TILES
                    low(AT_ATT + t + SPLIT, hd, ATT_TILES, KK * (NB if into_next else ATT_W))
                assert prev is None or s.count == ATT_STEPS, s.count

            def add_y(b, c, pair, used, fresh, before, half=None):
                dst = y[:, :, c * NB:(c + 1) * NB]
                if before is not None:
                    dve.wait_ge(y_add[b], before)
                if half is not None:
                    dve.wait_ge(*half)
                    V.tensor_tensor(dst[:, 0, :], dst[:, 0, :], pair[:, 0, :], ALU.add).then_inc(y_add[b], 1)
                    dve.wait_ge(tiles_used, used)
                    V.tensor_tensor(dst[:, 1, :], dst[:, 1, :], pair[:, 1, :], ALU.add).then_inc(y_add[b], 1)
                    return
                dve.wait_ge(tiles_used, used)
                if fresh:
                    V.tensor_copy(dst, pair[:]).then_inc(y_add[b], 1)
                else:
                    V.tensor_tensor(dst, dst, pair[:], ALU.add).then_inc(y_add[b], 1)

            def out_add(b, base, t, half=None):
                if t % 2:
                    n = t // 2
                    add_y(b, n % 4, out_pair(b, n), base + t + 1, n < 4, n if n >= 4 else None, half)

            renew(0, 0)
            low(0, 0, 0, KK * ATT_W)
            low_u(0, 0)
            for t in range(1, SPLIT):
                low(t, 0, 0, KK * ATT_W)
            att_head(0, None)
            with dve.Fori(1, ATT_HEADS - 1) as hd:
                att_head(hd, hd - 1)
            att_head(ATT_HEADS - 1, ATT_HEADS - 2, last=True)
            hp = ATT_HEADS - 1
            s = Steps(dve, a_steps, hp * ATT_STEPS)
            for t in range(16):
                if t == 0:
                    att_rotate(hp, s)
                if t == 1:
                    att_mask(hp, 1, s)
                if t == 2:
                    att_rsum(hp, 1)
                if t == 3:
                    att_mask(hp, 0, s)
                if t == 4:
                    att_rsum(hp, 0)
                if t == 7:
                    att_low(hp)
                if t < 15:
                    low(AT_ATT_OUT + t + SPLIT, 0, 0)
                else:
                    gain_y(1, 2)
                out_add(0, AT_ATT_OUT, t, (a_half, 3 * ATT_HEADS + 1) if t == 15 else None)
                if t in (11, 13):
                    gain_y(1, (t - 11) // 2)

            def hidden_low(layer, i):
                for m in range(HALVES):
                    dve.wait_ge(f_hi[layer], i * 2 + (1 + m))
                    bank = bankO if m else bankX
                    at = 4 * (isinstance(i, int) and i == FF_BLOCKS - 1)
                    V.tensor_tensor(hid_lo[:, at:at + 4, m * P:(m + 1) * P],
                                    bank[:].rearrange("p (k t) -> p k t", k=4),
                                    hid_hi[:, at:at + 4, m * P:(m + 1) * P].bitcast(F32),
                                    ALU.subtract).then_inc(f_lo[layer], 1)

            def mlp(layer, base):
                b = 1 + 2 * layer
                root_y(b)
                renew(b, 0)
                low_u(b, 0)
                low(base + SPLIT - 1, 0, 0)
                for t in range(FF_TILES):
                    first_before(b, t)
                    low(base + t + SPLIT, 0, 0)
                with dve.Fori(0, FF_BLOCKS - 2) as i:
                    for t in range(2 * FF_TILES):
                        if t == 1:
                            hidden_low(layer, i)
                        low(base + FF_TILES + t + SPLIT, i, 2 * FF_TILES)
                        if t >= FF_TILES and t % 2:
                            c = (t - FF_TILES) // 2
                            add_y(b, c, pairS if c % 2 else pairB,
                                  i * (2 * FF_TILES) + (base + FF_TILES + t + 1), False, i * 4 + (c + 2))
                last = FF_BLOCKS - 1
                at = base + (2 * last - 1) * FF_TILES
                for t in range(2 * FF_TILES):
                    if t == 1:
                        hidden_low(layer, last - 1)
                    if t == FF_TILES + 4:
                        hidden_low(layer, last)
                    low(at + t + SPLIT, 0, 0)
                    if t >= FF_TILES and t % 2:
                        c = (t - FF_TILES) // 2
                        add_y(b, c, pairS if c % 2 else pairB, at + t + 1, False, (last - 1) * 4 + c + 2)
                at += 2 * FF_TILES
                for t in range(FF_TILES):
                    if t < FF_TILES - 1:
                        low(at + t + SPLIT, 0, 0)
                    else:
                        gain_y(b + 1, 2)
                    if t % 2:
                        c = t // 2
                        add_y(b, c, pairS if c % 2 else pairB, at + t + 1, False, 4 * last + c + 2,
                              (f_half[layer], FF_BLOCKS + 1) if t == FF_TILES - 1 else None)
                        if 0 < c < COLS - 1:
                            gain_y(b + 1, c - 1)

            mlp(0, AT_FF0)

            REC_FRONT_STEPS = 2 + 5 * (LEVELS - 1) + 2 + MASK_LEVELS - 1
            ROOT_OPS = 3 + 3 * 3
            REC_BACK_STEPS = ROOT_OPS

            def rec_gates(hp, s):
                def col(row):
                    return bounds[:, row, hp:hp + 1] if isinstance(hp, int) else bounds[:, row, bass.ds(hp, 1)]
                dve.wait_ge(r_sigs, hp * 2 + 1)
                s.note(V.tensor_scalar(r_f, r_sig, col(3), col(2), ALU.mult, ALU.add))
                dve.wait_ge(r_sigs, hp * 2 + 2)
                s.note(V.tensor_scalar(r_K[:, 0, :], r_neg, col(3), col(4), ALU.mult, ALU.subtract))

            def rec_level(hp, s, j, root_op):
                if j == 0:
                    s.last()
                else:
                    s.reach(s.count - 2)
                w, nb = 1 << j, TOK >> (j + 1)

                def halves(v):
                    return v.rearrange("p (b two w) -> p b two w", two=2, w=w)

                def decayed_queries():
                    return V.tensor_tensor(r_R[:, j, :].rearrange("p (b w) -> p b w", w=w),
                                           halves(r_q)[:, :, 1, :], f[:, :, 1, :], ALU.mult)

                f, k = halves(r_f), halves(r_K[:, j, :])
                if j == LEVELS - 1:
                    s.last()
                    decayed_queries().then_inc(r_levels, 1)
                    return
                at = 0 if j == 0 else TOK - (TOK >> (j - 1))
                tot = (r_f if j == 0 else r_tot[:, at:at + 2 * nb]).rearrange("p (b two) -> p b two", two=2)
                k_next = halves(r_K[:, j + 1, :])
                root_op(0)
                s.note(V.tensor_tensor(k_next[:, :, 0, :], k[:, :, 0, :],
                                       tot[:, :, 1:2].broadcast_to([P, nb, w]), ALU.mult))
                root_op(1)
                s.note(V.tensor_copy(k_next[:, :, 1, :], k[:, :, 1, :]))
                root_op(2)
                at_next = TOK - (TOK >> j)
                s.note(V.tensor_tensor(r_tot[:, at_next:at_next + nb], tot[:, :, 0], tot[:, :, 1], ALU.mult))
                root_op(3)
                if j == 0:
                    dve.wait_ge(r_qcopied, hp + 1)
                else:
                    s.reach(s.count - 3)
                s.note(decayed_queries())
                root_op(4)
                s.note(V.tensor_tensor(f[:, :, 1, :], f[:, :, 1, :],
                                       tot[:, :, 0:1].broadcast_to([P, nb, w]), ALU.mult))
                root_op(5)

            def rec_assemble(hp, s):
                dve.wait_ge(r_scored, hp + 1)
                s.link(V.tensor_tensor(r_prod, pairS[:, :, 0:SCORES],
                                       rmask[:, None, :].broadcast_to([P, HALVES, SCORES]), ALU.mult))
                rows = r_A[:, 0:TOK]
                dve.wait_ge(r_across, hp + 1)
                s.link(V.tensor_tensor(rows.rearrange("p (m t) -> p m t", m=HALVES),
                                       pairB[:, 0, 0:TOK].rearrange("p (m t) -> p m t", m=HALVES),
                                       r_prod[:, :, SCORES - P:SCORES], ALU.add))
                for j in range(MASK_LEVELS):
                    w = 1 << j
                    dst = rows.rearrange("p (m b two w) -> p m b two w", m=HALVES, two=2, w=w)[:, :, :, 1, :]
                    ins = V.tensor_tensor(dst, dst, r_prod[:, :, j * 64:(j + 1) * 64].rearrange(
                        "p m (b w) -> p m b w", w=w), ALU.add)
                    if j < MASK_LEVELS - 1:
                        s.link(ins)
                ins.then_inc(r_att, 1)

            def rec_gate_out(hp):
                dve.wait_ge(r_sgated, hp + 1)
                V.tensor_tensor(r_G, r_sgate, rz[:, :, 3 * P:4 * P], ALU.mult).then_inc(r_gate, 1)

            def rec_root(hp, s, op):
                if op == 0:
                    dve.wait_ge(r_ssq, hp * 2 + 2)
                    s.note(V.tensor_scalar(r_x, r_ms, 1.0 / P, EPS, ALU.mult, ALU.add))
                    return
                s.last()
                if op == 1:
                    s.note(V.tensor_scalar(r_t.bitcast(I32), r_x.bitcast(I32), 1, None, ALU.logical_shift_right))
                elif op == 2:
                    s.note(V.tensor_scalar(r_rs.bitcast(I32), r_t.bitcast(I32), -1.0, float(0x5F3759DF),
                                           ALU.mult, ALU.add))
                elif op % 3 == 0:
                    s.note(V.scalar_tensor_tensor(out=r_t, in0=r_rs, scalar=-0.5, in1=r_x,
                                                  op0=ALU.mult, op1=ALU.mult))
                elif op % 3 == 1:
                    s.note(V.tensor_tensor(r_t, r_t, r_rs, ALU.mult))
                else:
                    s.note(V.scalar_tensor_tensor(out=r_rs, in0=r_t, scalar=1.5, in1=r_rs,
                                                  op0=ALU.add, op1=ALU.mult))

            def rec_output(hp, s):
                s.last()
                dve.wait_ge(r_gate, hp + 1)
                for m in range(HALVES):
                    ins = V.scalar_tensor_tensor(out=r_o[:, m, :], in0=bankO[:, m * P:(m + 1) * P],
                                                 scalar=r_rs[:, m:m + 1], in1=r_G[:, m, :],
                                                 op0=ALU.mult, op1=ALU.mult)
                ins.then_inc(r_out, 1)

            def rec_low(hp):
                dve.wait_ge(r_ohi, hp + 1)
                if isinstance(hp, int):
                    hi, lo = c_hi[:, hp, :], c_lo[:, hp, :]
                else:
                    hi, lo = c_hi[:, bass.ds(hp, 1), :].squeeze(1), c_lo[:, bass.ds(hp, 1), :].squeeze(1)
                V.scalar_tensor_tensor(out=lo, in0=bankX[:, 0:TOK], scalar=rgain[:, 0:1], in1=hi.bitcast(F32),
                                       op0=ALU.mult, op1=ALU.subtract).then_inc(r_olo, 1)

            def rec_mix(t, front, back, sf, sb_):
                if t == 0 and front is not None:
                    rec_gates(front, sf)
                if 1 <= t <= 4 and front is not None:
                    for j in (2 * t - 2, 2 * t - 1):
                        rec_level(front, sf, j, lambda k: rec_root(back, sb_, 6 * j + k)
                                  if t == 1 and back is not None else None)
                elif t == 1 and back is not None:
                    for op in range(ROOT_OPS):
                        rec_root(back, sb_, op)
                if t == 1 and back is not None:
                    rec_output(back, sb_)
                if t == 5 and front is not None:
                    rec_gate_out(front)
                if t == 5 and back is not None:
                    rec_low(back)
                if t == 6 and front is not None:
                    rec_assemble(front, sf)

            def rec_head(hd, front, back):
                sf = Steps(dve, r_front_steps, None if front is None else front * REC_FRONT_STEPS)
                sb_ = Steps(dve, r_back_steps, None if back is None else back * REC_BACK_STEPS)
                for t in range(REC_TILES):
                    if isinstance(hd, int) and hd == 0:
                        first_before(2, t)
                    if isinstance(hd, int) and hd == 0 and t == 7:
                        V.memset(pairB[:, 0, :], 0.0).then_inc(zmem, 1)
                        dve.wait_ge(zmem, 1)
                        V.memset(r_A, 0.0).then_inc(r_olo, 1)
                    rec_mix(t, front, back, sf, sb_)
                    low(AT_REC + t + SPLIT, hd, REC_TILES)
                assert front is None or sf.count == REC_FRONT_STEPS, sf.count
                assert back is None or sb_.count == REC_BACK_STEPS, sb_.count

            root_y(2)
            renew(2, 0)
            low_u(2, 0)
            low(AT_REC + SPLIT - 1, 0, 0)
            dve.wait_ge(rgain_in, 16)
            rec_head(0, None, None)
            rec_head(1, 0, None)
            with dve.Fori(2, REC_HEADS) as hd:
                rec_head(hd, hd - 1, hd - 2)
            last_head = REC_HEADS - 1
            sf = Steps(dve, r_front_steps, last_head * REC_FRONT_STEPS)
            for t in range(32):
                if t == 0:
                    sb_ = Steps(dve, r_back_steps, (last_head - 1) * REC_BACK_STEPS)
                if t == 8:
                    sb_ = Steps(dve, r_back_steps, last_head * REC_BACK_STEPS)
                if t < 8:
                    rec_mix(t, last_head, last_head - 1, sf, sb_)
                elif t < 16:
                    rec_mix(t - 8, None, last_head, None, sb_)
                if t < 31:
                    low(AT_REC_OUT + t + SPLIT, 0, 0)
                else:
                    gain_y(3, 2)
                out_add(2, AT_REC_OUT, t, (r_half, REC_HEADS + 1) if t == 31 else None)
                if t in (27, 29):
                    gain_y(3, (t - 27) // 2)

            mlp(1, AT_FF1)
            root_y(4)
            for c in range(COLS):
                renew(4, c)


def _tiles_by_head(w, groups, parts, heads):
    a = w.reshape(KC // KK, KK, P, groups, parts, heads, P)
    a = a.transpose(5, 3, 0, 2, 1, 4, 6)
    return np.ascontiguousarray(a).reshape(heads * groups * (KC // KK), P, KK * parts * P)


def _tiles_up(w):
    a = w.reshape(2, KC // KK, KK, P, FF_BLOCKS, NB).transpose(0, 4, 1, 3, 2, 5)
    return np.ascontiguousarray(a).reshape(-1, P, KK * NB)


def _tiles_down(w):
    a = w.reshape(-1, 2, KK, P, COLS, NB).transpose(0, 4, 1, 3, 2, 5)
    return np.ascontiguousarray(a).reshape(-1, P, KK * NB)


def kernel(**inputs):
    import concourse.bacc as _bacc
    from concourse.bass_utils import run_bass_kernel_spmd as _run

    a = {k: np.asarray(v) for k, v in inputs.items()}
    arrays = {
        "x": a["x"][0],
        "positions": np.ascontiguousarray(a["positions"].reshape(HALVES, P).T),
        "norm_gains": a["norm_gains"],
        "lower_bound": np.ascontiguousarray(a["rec_lower_bounds"].reshape(REC_HEADS, P).T),
        "rec_gain": np.ascontiguousarray(a["rec_out_norm"].reshape(P, 1)),
        "s_att_in": _tiles_by_head(a["w_att_in"][0], GROUPS, 3, ATT_HEADS),
        "s_att_out": _tiles_down(a["w_att_out"]),
        "s_rec_in": _tiles_by_head(a["w_rec_in"][0], 1, 4, REC_HEADS),
        "s_rec_out": _tiles_down(a["w_rec_out"]),
        "s_up": _tiles_up(a["w_ff1"]),
        "s_down": _tiles_down(a["w_ff2"]),
    }
    nc = _bacc.Bacc("TRN2", target_bir_lowering=False, num_devices=1)
    args = [nc.dram_tensor("in_" + k, v.shape, mybir.dt.from_np(v.dtype), kind="ExternalInput").ap()
            for k, v in arrays.items()]
    out = nc.dram_tensor("out_h", (TOK, D), F32, kind="ExternalOutput").ap()
    hybrid_trunk(nc, *args, out)
    r = _run(nc, [{"in_" + k: np.ascontiguousarray(v) for k, v in arrays.items()}], core_ids=[0])
    return r.results[0]["out_h"].reshape(1, TOK, D)
```

```python
from contextlib import ExitStack

import numpy as np

import concourse.bass as bass
from concourse import mybir

F32 = mybir.dt.float32
F32R = mybir.dt.float32r
I32 = mybir.dt.int32
ALU = mybir.AluOpType
ACT = mybir.ActivationFunctionType
AX = mybir.AxisListType

P = 128
TOK = 256
HALVES = TOK // P
D = 2048
KC = D // P
NB = 512
KK = 2
RAW = 8
START_WARM = 10
WARM = 20
SPLIT = 4
COLS = D // NB

ATT_HEADS = 8
GROUPS = 3
DILATION = (1, 4, 16)
WINDOW = (128, 512, 2048)
ATT_W = 3 * P
ATT_BLOCK_TILES = KC // KK
ATT_TILES = GROUPS * ATT_BLOCK_TILES
HALF_ROPE = 16
ROPE_THETA = 500000.0
MASKED = -1e30

REC_HEADS = 16
REC_TILES = KC // KK
LEVELS = 8
MASK_LEVELS = 5
SCORES = MASK_LEVELS * P // 2 + P
LB_FLOOR = 1e-30

FF_BLOCKS = 16
FF_TILES = 8
EPS = 1e-6

AT_ATT = 0
AT_ATT_OUT = AT_ATT + ATT_HEADS * ATT_TILES
AT_FF0 = AT_ATT_OUT + ATT_HEADS // 4 * COLS * 2
AT_REC = AT_FF0 + FF_BLOCKS * 2 * FF_TILES
AT_REC_OUT = AT_REC + REC_HEADS * REC_TILES
AT_FF1 = AT_REC_OUT + REC_HEADS // 4 * COLS * 2
TILES = AT_FF1 + FF_BLOCKS * 2 * FF_TILES


class Steps:

    def __init__(self, eng, sem, base=0):
        self.eng, self.sem, self.base, self.count = eng, sem, base, 0

    def note(self, ins):
        ins.then_inc(self.sem, 1)
        self.count += 1
        return self.base + self.count

    def last(self):
        self.eng.wait_ge(self.sem, self.base + self.count)

    def reach(self, count):
        self.eng.wait_ge(self.sem, self.base + count)

    def link(self, ins):
        self.note(ins)
        self.last()


def hybrid_trunk(nc, x, positions, norm_gains, pre_gains, lower_bound, rec_gain, s_att_in, s_att_out,
                 s_rec_in, s_rec_out, s_up, s_down, out):
    with ExitStack() as ctx:
        def sb(name, shape, dt=F32):
            return ctx.enter_context(nc.sbuf_tensor(name, shape, dt))

        def psum(name, shape):
            return ctx.enter_context(nc.psum_tensor(name, shape, F32))

        def sem(name):
            return ctx.enter_context(nc.semaphore(name))

        raw = sb("raw", [P, RAW, KK * NB])
        w_hi = sb("w_hi", [P, SPLIT, KK * NB], F32R)
        w_lo = sb("w_lo", [P, SPLIT, KK * NB], F32R)
        u_hi = sb("u_hi", [P, KC, TOK], F32R)
        u_lo = sb("u_lo", [P, KC, TOK], F32R)
        c_hi = sb("c_hi", [P, REC_HEADS, TOK], F32R)
        c_lo = sb("c_lo", [P, REC_HEADS, TOK], F32R)
        h = sb("h", [P, HALVES, D])
        y = sb("y", [P, HALVES, D])
        gain_post = sb("gain_post", [P, D])
        gain_pre = sb("gain_pre", [P, 4, KC])
        ident = sb("ident", [P, P])
        junk = sb("junk", [P, NB], mybir.dt.bfloat16)
        stat = sb("stat", [P, 64])
        mix = sb("mix", [P, 7168])
        rope = sb("rope", [P, 2, HALVES, HALF_ROPE])
        pos_i = sb("pos_i", [P, HALVES], I32)
        bounds = sb("bounds", [P, 5, REC_HEADS])
        rgain = sb("rgain", [P, 1])

        def carve(at, *shape):
            n = int(np.prod(shape))
            v = mix[:, at:at + n]
            if len(shape) == 2:
                v = v.rearrange("p (a b) -> p a b", a=shape[0])
            if len(shape) == 3:
                v = v.rearrange("p (a b c) -> p a b c", a=shape[0], b=shape[1])
            return v

        ssq_y = stat[:, 0:8].rearrange("p (m c) -> p m c", m=HALVES)
        ssq_h = stat[:, 8:16].rearrange("p (m c) -> p m c", m=HALVES)
        mean_y = stat[:, 16:18]
        rstd_y = stat[:, 18:20]
        mean_h = stat[:, 20:22]
        rstd_u = stat[:, 22:24]
        eps_col = stat[:, 24:25]

        az = carve(0, HALVES, 9, P)
        a_qkT = carve(2304, GROUPS, NB)
        a_v = carve(3840, HALVES, GROUPS, P)
        a_p = carve(4608, 768)
        a_pT = carve(5376, 768)
        a_o = carve(6144, HALVES, P)
        a_cosx = carve(4608, 9 * 32)
        a_sinx = carve(4896, 9 * 32)
        amask = carve(6400, GROUPS, TOK)
        a_max = stat[:, 26:28]
        a_sum = stat[:, 28:30]
        a_rsum = stat[:, 30:32]

        rz = carve(0, HALVES, NB)
        r_Rq = carve(1024, HALVES, P // 2 + P)
        r_q = r_Rq[:, :, P // 2:]
        r_neg = carve(1408, TOK)
        r_sig = carve(1664, TOK)
        r_f = carve(1920, TOK)
        r_R = [r_Rq[:, :, 0:P // 2]] + [carve(2176 + (j - 1) * P, HALVES, P // 2) for j in range(1, LEVELS)]
        r_K = carve(3072, LEVELS, TOK)
        r_tot = carve(5120, 2 * TOK)
        r_A = carve(5632, GROUPS * P)
        r_sgate = carve(6016, HALVES, P)
        r_G = carve(6272, HALVES, P)
        r_o = carve(6528, HALVES, P)
        r_v = carve(6784, HALVES, P)
        rmask = sb("rmask", [P, SCORES], mybir.dt.bfloat16)
        r_prod = carve(2176, HALVES, SCORES)
        at_level = [0] + [P // 2 + P + (j - 1) * P // 2 for j in range(1, MASK_LEVELS)]
        at_diagonal = P // 2
        r_ms = stat[:, 32:34]
        r_rs = stat[:, 36:38]
        r_x = stat[:, 38:40]
        r_t = stat[:, 40:42]

        m_h = carve(0, HALVES, NB)
        hid_hi, hid_lo = c_hi[:, 0:8, :], c_lo[:, 0:8, :]

        pairA = psum("pairA", [P, HALVES, NB])
        pairB = psum("pairB", [P, HALVES, NB])
        pairS = psum("pairS", [P, HALVES, NB])
        bankX = psum("bankX", [P, NB])
        bankO = psum("bankO", [P, NB])
        turn_bank = [bankX[:], bankO[:], pairS[:, 0], pairS[:, 1]]

        def out_pair(b, n):
            if b == 0:
                return pairA if n % 2 else pairB
            if n < 4:
                return pairS if n == 1 else pairA
            return pairA if n % 2 else pairB

        FIRST_SPLITS = [[3], [4, 5]]

        landed = [sem(f"landed{s}") for s in range(RAW)]
        hi_made, lo_made, tiles_used = sem("hi_made"), sem("lo_made"), sem("tiles_used")
        x_in = [sem(f"x_in{c}") for c in range(COLS)]
        pos_in, bound_in, rgain_in = sem("pos_in"), sem("bound_in"), sem("rgain_in")
        pre_in, post_in = sem("pre_in"), sem("post_in")
        out_sent = sem("out_sent")
        ident_ready, masks_ready, pool_steps = sem("ident_ready"), sem("masks_ready"), sem("pool_steps")
        v_setup, act_setup = sem("v_setup"), sem("act_setup")
        amask_ready, angle_ready, sines_ready, rope_ready = (
            sem("amask_ready"), sem("angle_ready"), sem("sines_ready"), sem("rope_ready"))
        bexp_in, bexp_out = sem("bexp_in"), sem("bexp_out")
        zmem = sem("zmem")

        def norm_sems(b):
            names = ["steps"]
            if b > 0:
                names += ["ssq_y_made", "gained", "mean_y_made", "root_y_made", "h_new"]
            if b < 4:
                names += ["turned", "u_hi_made", "u_lo_made", "ssq_h_made", "mean_h_made",
                          "root_h_made", "rstd_u_made"]
            return {n: sem(f"n{b}_{n}") for n in names}

        NORM = [norm_sems(b) for b in range(5)]

        a_half = sem("a_half")
        a_evac = sem("a_evac")
        a_rot = sem("a_rot")
        a_vcopied = sem("a_vcopied")
        a_turned = sem("a_turned")
        a_qk = sem("a_qk")
        a_scored = sem("a_scored")
        a_maxed = sem("a_maxed")
        a_probs = sem("a_probs")
        a_rs = sem("a_rs")
        a_pturned = sem("a_pturned")
        a_pt = sem("a_pt")
        a_pv = sem("a_pv")
        a_out = sem("a_out")
        a_oturned = sem("a_oturned")
        a_ohi = sem("a_ohi")
        a_olo = sem("a_olo")
        a_steps = sem("a_steps")

        r_half, r_evac, r_qfT, r_sigs, r_qcopied, r_sgated, r_vcopied = (
            sem("r_half"), sem("r_evac"), sem("r_qfT"), sem("r_sigs"), sem("r_qcopied"), sem("r_sgated"),
            sem("r_vcopied"))
        r_levels, r_scored, r_att, r_across = sem("r_levels"), sem("r_scored"), sem("r_att"), sem("r_across")
        r_pv, r_ssq, r_out, r_gate = sem("r_pv"), sem("r_ssq"), sem("r_out"), sem("r_gate")
        r_oturned, r_ohi, r_olo = sem("r_oturned"), sem("r_ohi"), sem("r_olo")
        r_front_steps, r_back_steps = sem("r_front_steps"), sem("r_back_steps")

        y_add = [sem(f"y_add{b}") for b in range(4)]
        f_half = [sem(f"f_half{b}") for b in range(2)]
        f_relu = [sem(f"f_relu{b}") for b in range(2)]
        f_hid = [sem(f"f_hid{b}") for b in range(2)]
        f_turned = [sem(f"f_turned{b}") for b in range(2)]
        f_hi = [sem(f"f_hi{b}") for b in range(2)]
        f_lo = [sem(f"f_lo{b}") for b in range(2)]

        block = ctx.enter_context(nc.Block())

        @block.sync
        def _(sp):
            def load(stream, width, index, base, i, per, t):
                slot = (base + t) % RAW
                at = index if isinstance(index, int) else sp.snap(index)
                if base + t >= RAW or not isinstance(i, int) or i:
                    sp.wait_ge(lo_made, i * per + (base + t - RAW + 1))
                src = stream[at] if isinstance(at, int) else stream[bass.ds(at, 1)].squeeze(0)
                sp.dma_start(raw[:, slot, 0:width], src).then_inc(landed[slot], 16)

            def mlp_loads(layer, base):
                for t in range(FF_TILES):
                    load(s_up, KK * NB, layer * P + t, base, 0, 0, t)
                with sp.Fori(0, FF_BLOCKS - 1) as i:
                    for t in range(FF_TILES):
                        load(s_up, KK * NB, i * FF_TILES + (layer * P + FF_TILES + t),
                             base + FF_TILES, i, 2 * FF_TILES, t)
                    for t in range(FF_TILES):
                        load(s_down, KK * NB, i * FF_TILES + (layer * P + t),
                             base + 2 * FF_TILES, i, 2 * FF_TILES, t)
                for t in range(FF_TILES):
                    load(s_down, KK * NB, layer * P + (FF_BLOCKS - 1) * FF_TILES + t,
                         base + (2 * FF_BLOCKS - 1) * FF_TILES, 0, 0, t)

            sp.dma_start(gain_pre[:], pre_gains).then_inc(pre_in, 16)
            for c in range(COLS):
                cols = slice(c * NB, (c + 1) * NB)
                sp.dma_start(h[:, :, cols],
                             x.rearrange("(m p) d -> p m d", p=P)[:, :, cols]).then_inc(x_in[c], 16)
                for t in ([0], [1, 2], [3, 4], [5, 6, 7])[c]:
                    load(s_att_in, KK * ATT_W, t, AT_ATT, 0, 0, t)
            sp.dma_start(pos_i[:], positions).then_inc(pos_in, 16)
            sp.dma_start(bounds[:, 0, :], lower_bound).then_inc(bound_in, 16)
            sp.dma_start(rgain[:], rec_gain).then_inc(rgain_in, 16)
            for t in range(RAW, ATT_TILES):
                load(s_att_in, KK * ATT_W, t, AT_ATT, 0, 0, t)
            with sp.Fori(1, ATT_HEADS) as hd:
                for t in range(ATT_TILES):
                    load(s_att_in, KK * ATT_W, hd * ATT_TILES + t, AT_ATT, hd, ATT_TILES, t)
            for t in range(AT_FF0 - AT_ATT_OUT):
                load(s_att_out, KK * NB, t, AT_ATT_OUT, 0, 0, t)
            mlp_loads(0, AT_FF0)
            for t in range(REC_TILES):
                load(s_rec_in, KK * NB, t, AT_REC, 0, 0, t)
            with sp.Fori(1, REC_HEADS) as hd:
                for t in range(REC_TILES):
                    load(s_rec_in, KK * NB, hd * REC_TILES + t, AT_REC, hd, REC_TILES, t)
            for t in range(AT_FF1 - AT_REC_OUT):
                load(s_rec_out, KK * NB, t, AT_REC_OUT, 0, 0, t)
            mlp_loads(1, AT_FF1)
            out_rows = out.rearrange("(m p) d -> p m d", p=P)
            for c in range(COLS):
                for m in range(HALVES):
                    sp.wait_ge(NORM[4]["h_new"], HALVES * c + m + 1)
                    sp.dma_start(out_rows[:, m, c * NB:(c + 1) * NB],
                                 h[:, m, c * NB:(c + 1) * NB]).then_inc(out_sent, 16)
            sp.wait_ge(out_sent, 16 * COLS * HALVES)

        @block.gpsimd
        def _(pool):
            pool_s = Steps(pool, pool_steps)
            pool_s.note(nc.gpsimd.memset(ident[:], 0.0))
            pool_s.note(nc.gpsimd.memset(amask, 0.0))
            pool_s.note(nc.gpsimd.memset(rmask[:], 1.0))
            pool_s.last()
            nc.gpsimd.affine_select(out=ident[:], in_=ident[:], compare_op=ALU.not_equal, fill=1.0, base=0,
                                    pattern=[[-1, P]], channel_multiplier=1).then_inc(ident_ready, 1)
            pool_s.link(nc.gpsimd.affine_select(out=amask, in_=amask, compare_op=ALU.is_ge, fill=MASKED,
                                                base=P, pattern=[[0, GROUPS], [-1, TOK]], channel_multiplier=1))
            for g in range(GROUPS):
                if WINDOW[g] < TOK:
                    pool_s.link(nc.gpsimd.affine_select(
                        out=amask[:, g, :], in_=amask[:, g, :], compare_op=ALU.is_ge, fill=MASKED,
                        base=WINDOW[g] - P, pattern=[[1, TOK]], channel_multiplier=-1))
            for j in range(MASK_LEVELS):
                w = 1 << j
                view = rmask[:, at_level[j]:at_level[j] + P // 2].rearrange("p (b w) -> p b w", w=w)
                pool_s.link(nc.gpsimd.affine_select(out=view, in_=view, compare_op=ALU.is_ge, fill=0.0, base=0,
                                                    pattern=[[-2 * w, P // 2 // w], [0, w]], channel_multiplier=1))
                pool_s.link(nc.gpsimd.affine_select(out=view, in_=view, compare_op=ALU.is_ge, fill=0.0, base=w - 1,
                                                    pattern=[[2 * w, P // 2 // w], [0, w]], channel_multiplier=-1))
            diagonal = rmask[:, at_diagonal:at_diagonal + P]
            pool_s.link(nc.gpsimd.affine_select(out=diagonal, in_=diagonal,
                                                compare_op=ALU.is_equal, fill=0.0, base=0,
                                                pattern=[[-1, P]], channel_multiplier=1))
            nc.gpsimd.memset(eps_col, EPS).then_inc(masks_ready, 1)
            for layer in range(2):
                pool.wait_ge(NORM[1 + 2 * layer]["h_new"], COLS * HALVES)
                for m in range(HALVES):
                    nc.gpsimd.memset(y[:, m, :], 0.0).then_inc(y_add[1 + 2 * layer], 1)

        @block.tensor
        def _(pe):
            def three_pass(dst, s_hi, s_lo, slot, kk, width, first, last):
                wh = w_hi[:, slot, kk * width:(kk + 1) * width]
                wl = w_lo[:, slot, kk * width:(kk + 1) * width]
                pe.matmul(dst, s_hi, wh, start=first, stop=False)
                pe.matmul(dst, s_hi, wl, start=False, stop=False)
                return pe.matmul(dst, s_lo, wh, start=False, stop=last)

            def tile(pair, s_hi, s_lo, chunk0, at, i, per, width, first, last, half_sem=None, free=None,
                     ready=None):
                slot = at % SPLIT
                pe.wait_ge(lo_made, i * per + (at + 1))
                for m in range(HALVES):
                    if first and free is not None:
                        free(m)
                    if ready is not None:
                        ready(m)
                    for kk in range(KK):
                        k = chunk0 + kk
                        mm = three_pass(pair[:, m, 0:width], s_hi[:, k, m * P:(m + 1) * P],
                                        s_lo[:, k, m * P:(m + 1) * P], slot, kk, width,
                                        first and kk == 0, last and kk == KK - 1)
                    if m == 0 and last and half_sem is not None:
                        mm.then_inc(half_sem, 1)
                mm.then_inc(tiles_used, 1)

            def turn_chunks(b, t):
                n = NORM[b]
                c = t // 2
                for m in range(HALVES):
                    u = HALVES * t + m
                    if b:
                        pe.wait_ge(n["h_new"], HALVES * c + m + 1)
                    else:
                        pe.wait_ge(x_in[c], 16)
                    if u >= 4:
                        pe.wait_ge(n["u_lo_made"], u - 3)
                    for j in range(KK):
                        k = KK * t + j
                        ins = pe.transpose(turn_bank[u % 4][:, j * P:(j + 1) * P],
                                           h[:, m, k * P:(k + 1) * P], ident[:])
                    ins.then_inc(n["turned"], 1)

            def keep_warm(count):
                for _ in range(count):
                    pe.matmul(bankX[:], u_hi[:, 0, 0:P], u_hi[:, 0:2, :].rearrange("p k t -> p (k t)"),
                              start=True, stop=True)

            def wait_u(b, t, m):
                pe.wait_ge(NORM[b]["u_lo_made"], HALVES * t + m + 1)

            def turn_next(b, t):
                if t + 2 < KC // KK:
                    turn_chunks(b, t + 2)

            def att_turn(hp, g):
                if g == 0:
                    pe.wait_ge(a_rot, hp + 1)
                if g == 2:
                    pe.wait_ge(a_qk, hp * 3 + 1)
                bank = bankO if g == 1 else bankX
                for j in range(4):
                    src = az[:, j % 2, 3 * g + j // 2, :]
                    t = pe.transpose(bank[:, j * P:(j + 1) * P], src, ident[:])
                t.then_inc(a_turned, 1)

            def att_scores(hp, m):
                if m == 1:
                    pe.wait_ge(a_qk, hp * 3 + 3)
                keys = (m + 1) * P
                flat = pairS[:].rearrange("p m n -> p (m n)")
                for g in range(GROUPS):
                    mm = pe.matmul(flat[:, g * keys:(g + 1) * keys], a_qkT[:, g, m * P:(m + 1) * P],
                                   a_qkT[:, g, TOK:TOK + keys], start=True, stop=True)
                mm.then_inc(a_scored, 1)

            def att_turn_probs(hp, m):
                pe.wait_ge(a_probs, hp * 2 + (2 - m))
                flat = pairS[:].rearrange("p m n -> p (m n)")
                for j in range(GROUPS * (m + 1)):
                    t = pe.transpose(flat[:, j * P:(j + 1) * P], a_p[:, j * P:(j + 1) * P], ident[:])
                t.then_inc(a_pturned, 1)

            def att_pv(hp, m):
                pe.wait_ge(a_pt, hp * 2 + (2 - m))
                pe.wait_ge(a_vcopied, hp + 1)
                if m == 0:
                    pe.wait_ge(a_out, hp * 2 + 1)
                n = GROUPS * (m + 1)
                for j in range(n):
                    mm = pe.matmul(bankO[:, m * P:(m + 1) * P], a_pT[:, j * P:(j + 1) * P],
                                   a_v[:, j % (m + 1), j // (m + 1), :], start=(j == 0), stop=(j == n - 1))
                mm.then_inc(a_pv, 1)

            def att_turn_out(hp):
                pe.wait_ge(a_out, hp * 2 + 2)
                for m in range(HALVES):
                    t = pe.transpose(bankX[:, m * P:(m + 1) * P], a_o[:, m, :], ident[:])
                t.then_inc(a_oturned, 1)

            def att_block_free(hd, g):
                def free(m):
                    back = {0: 1, 1: 3, 2: 2}[g]
                    if not isinstance(hd, int) or hd * 3 + g - back >= 0:
                        pe.wait_ge(a_evac, hd * 6 + ((g - back) * 2 + 1 + m))
                return free

            def att_project(hd, prev):
                for t in range(ATT_TILES):
                    g, tb = divmod(t, ATT_BLOCK_TILES)
                    first_block = isinstance(hd, int) and hd == 0 and g == 0
                    tile(pairB if g == 1 else pairA, u_hi, u_lo, tb * KK, AT_ATT + t, hd, ATT_TILES, ATT_W,
                         tb == 0, tb == ATT_BLOCK_TILES - 1, a_half, att_block_free(hd, g),
                         (lambda m: wait_u(0, tb, m)) if first_block else None)
                    if first_block:
                        turn_next(0, tb)
                    if prev is None:
                        continue
                    if t == 2:
                        att_turn(prev, 0)
                        att_turn(prev, 1)
                    if t == 3:
                        att_turn(prev, 2)
                    if t == 5:
                        att_scores(prev, 1)
                    if t == 7:
                        att_turn_probs(prev, 1)
                    if t == 9:
                        att_pv(prev, 1)
                        att_scores(prev, 0)
                    if t == 12:
                        att_turn_probs(prev, 0)
                    if t == 14:
                        att_pv(prev, 0)
                    if t == 16:
                        att_turn_out(prev)

            def out_tile(t, base, b, evac_sem, half_sem):
                kq, c, pr = t // 8, t // 2 % 4, t % 2
                n = t // 2

                def free(m):
                    if b == 0 and n < 2:
                        pe.wait_ge(evac_sem, 6 * ATT_HEADS - 3 + 2 * n + m)
                    elif b == 0:
                        pe.wait_ge(y_add[b], n - 1)
                    elif n == 0:
                        pe.wait_ge(evac_sem, 2 * REC_HEADS - 1 + m)
                    elif n == 4:
                        pe.wait_ge(r_att, REC_HEADS)
                    elif n != 1:
                        pe.wait_ge(y_add[b], {2: 1, 3: 3, 5: 4}.get(n, n - 1))

                tile(out_pair(b, n), c_hi, c_lo, kq * 4 + pr * KK, base + t, 0, 0, NB, pr == 0, pr == 1,
                     half_sem, free)

            pe.wait_ge(ident_ready, 1)
            for _ in range(START_WARM):
                pe.transpose(bankX[:, 0:P], ident[:], ident[:])
            for t in range(2):
                turn_chunks(0, t)
            att_project(0, None)
            with pe.Fori(1, ATT_HEADS) as hd:
                att_project(hd, hd - 1)
            hp = ATT_HEADS - 1
            for t in range(16):
                if t == 0:
                    pe.wait_ge(a_olo, 4)
                if t == 8:
                    pe.wait_ge(a_olo, 6)
                if t == 9:
                    pe.wait_ge(a_olo, ATT_HEADS)
                out_tile(t, AT_ATT_OUT, 0, a_evac, a_half if t == 15 else None)
                if t == 1:
                    att_turn(hp, 0)
                    att_turn(hp, 1)
                if t == 2:
                    att_turn(hp, 2)
                    att_scores(hp, 1)
                if t == 4:
                    att_turn_probs(hp, 1)
                if t == 5:
                    att_pv(hp, 1)
                    att_scores(hp, 0)
                if t == 6:
                    att_turn_probs(hp, 0)
                if t == 7:
                    att_pv(hp, 0)
                if t == 8:
                    att_turn_out(hp)

            def up(layer, base, i, t, first_block):
                def free(m):
                    if not first_block:
                        pe.wait_ge(f_relu[layer], i * 2 + (1 + m))

                tile(pairA, u_hi, u_lo, t * KK, base + t, 0 if isinstance(i, int) else i, 2 * FF_TILES, NB,
                     t == 0, t == FF_TILES - 1, f_half[layer], free,
                     (lambda m: wait_u(1 + 2 * layer, t, m)) if first_block else None)
                if first_block:
                    turn_next(1 + 2 * layer, t)

            def turn_hidden(layer, i):
                for m in range(HALVES):
                    pe.wait_ge(f_hid[layer], i * 2 + (1 + m))
                    bank = bankO if m else bankX
                    for j in range(4):
                        t = pe.transpose(bank[:, j * P:(j + 1) * P], m_h[:, m, j * P:(j + 1) * P], ident[:])
                    t.then_inc(f_turned[layer], 1)

            def down(layer, base, i, t):
                c, pr = divmod(t, 2)
                if t == 0:
                    pe.wait_ge(f_lo[layer], i * 2 + 2)

                def free(m):
                    pe.wait_ge(y_add[1 + 2 * layer], i * 4 + (c + 1))

                last = isinstance(i, int) and i == FF_BLOCKS - 1
                tile(pairS if c % 2 else pairB, hid_hi, hid_lo, 4 * last + pr * KK, base + t,
                     0 if isinstance(i, int) else i, 2 * FF_TILES, NB, pr == 0, pr == 1,
                     f_half[layer] if last and t == FF_TILES - 1 else None, free)

            def mlp(layer, base):
                keep_warm(WARM)
                for t in range(2):
                    turn_chunks(1 + 2 * layer, t)
                for t in range(FF_TILES):
                    up(layer, base, 0, t, True)
                with pe.Fori(0, FF_BLOCKS - 2) as i:
                    for t in range(FF_TILES):
                        up(layer, base + FF_TILES, i, t, False)
                        if t == 1:
                            turn_hidden(layer, i)
                    for t in range(FF_TILES):
                        down(layer, base + 2 * FF_TILES, i, t)
                last = FF_BLOCKS - 1
                at = base + (2 * last - 1) * FF_TILES
                for t in range(FF_TILES):
                    up(layer, at, last - 1, t, False)
                    if t == 1:
                        turn_hidden(layer, last - 1)
                for t in range(FF_TILES):
                    down(layer, at + FF_TILES, last - 1, t)
                    if t == 3:
                        turn_hidden(layer, last)
                for t in range(FF_TILES):
                    down(layer, at + 2 * FF_TILES, last, t)

            mlp(0, AT_FF0)

            def rec_turn(hp):
                pe.wait_ge(r_evac, hp * 2 + 2)
                if not isinstance(hp, int) or hp > 0:
                    pe.wait_ge(r_olo, hp)
                for j in range(4):
                    t = pe.transpose(bankX[:, j * P:(j + 1) * P], rz[:, j % 2, (j // 2) * P:(j // 2 + 1) * P],
                                     ident[:])
                t.then_inc(r_qfT, 1)

            def rec_scores(hp):
                pe.wait_ge(r_levels, hp + 1)
                for m in range(HALVES):
                    half = m * P
                    pe.matmul(pairS[:, m, 0:P // 2 + P], r_K[:, 0, half:half + P], r_Rq[:, m, :],
                              start=True, stop=True)
                    for j in range(1, MASK_LEVELS):
                        pe.matmul(pairS[:, m, at_level[j]:at_level[j] + P // 2], r_K[:, j, half:half + P],
                                  r_R[j][:, m, :], start=True, stop=True)
                    for b in range(2):
                        pe.matmul(pairB[64 * b:64 * b + 32, 0, half + 64 * b + 32:half + 64 * b + 64],
                                  r_K[:, 5, half + 64 * b:half + 64 * b + 32],
                                  r_R[5][:, m, 32 * b:32 * b + 32], start=True, stop=True)
                    pe.matmul(pairB[0:64, 0, half + 64:half + P], r_K[:, 6, half:half + 64],
                              r_R[6][:, m, :], start=True, stop=True)
                pe.matmul(pairB[:, 0, 2 * P:3 * P], r_K[:, 7, 0:P], r_R[7].rearrange("p m t -> p (m t)"),
                          start=True, stop=True).then_inc(r_scored, 1)

            def rec_pv(hp):
                pe.wait_ge(r_att, hp + 1)
                pe.wait_ge(r_across, hp + 1)
                pe.wait_ge(r_vcopied, hp + 1)
                v = [r_v[:, m, :] for m in range(HALVES)]
                pe.matmul(bankO[:, 0:P], r_A[:, 0:P], v[0], start=True, stop=True)
                pe.matmul(bankO[:, P:2 * P], r_A[:, P:2 * P], v[1], start=True, stop=False)
                pe.matmul(bankO[:, P:2 * P], r_A[:, 2 * P:3 * P], v[0], start=False, stop=True).then_inc(r_pv, 1)

            def rec_turn_out(hp, last=False):
                pe.wait_ge(r_out, hp + 1)
                pe.wait_ge(r_qcopied, hp + 1 if last else hp + 2)
                for m in range(HALVES):
                    t = pe.transpose(bankX[:, m * P:(m + 1) * P], r_o[:, m, :], ident[:])
                t.then_inc(r_oturned, 1)

            def rec_mix(t, front, back):
                if t == 0 and front is not None:
                    rec_turn(front)
                if t == 0 and back is not None:
                    rec_pv(back)
                if t == 3 and back is not None:
                    rec_turn_out(back, last=front is None)
                if t == 5 and front is not None:
                    rec_scores(front)

            keep_warm(WARM)
            for t in range(2):
                turn_chunks(2, t)
            for t in range(REC_TILES):
                tile(pairA, u_hi, u_lo, t * KK, AT_REC + t, 0, 0, NB, t == 0, t == REC_TILES - 1, r_half, None,
                     lambda m: wait_u(2, t, m))
                turn_next(2, t)

            def rec_project(hd, front, back):
                for t in range(REC_TILES):
                    tile(pairA, u_hi, u_lo, t * KK, AT_REC + t, hd, REC_TILES, NB, t == 0, t == REC_TILES - 1,
                         r_half, lambda m: pe.wait_ge(r_evac, hd * 2 + (m - 1)))
                    rec_mix(t, front, back)

            rec_project(1, 0, None)
            with pe.Fori(2, REC_HEADS) as hd:
                rec_project(hd, hd - 1, hd - 2)
            for t in range(32):
                if t == 0:
                    pe.wait_ge(r_olo, 5)
                if t == 24:
                    pe.wait_ge(r_olo, REC_HEADS + 1)
                out_tile(t, AT_REC_OUT, 2, r_evac, r_half if t == 31 else None)
                if t == 5:
                    pe.wait_ge(y_add[2], 2)
                if t < 8:
                    rec_mix(t, REC_HEADS - 1, REC_HEADS - 2)
                elif t < 16:
                    rec_mix(t - 8, None, REC_HEADS - 1)

            mlp(1, AT_FF1)

        @block.scalar
        def _(act):
            def high(at, i, per, width=KK * NB):
                if isinstance(i, int) and i * per + at >= TILES:
                    return
                slot, rounds = at % RAW, per // RAW
                act.wait_ge(landed[slot], i * (16 * rounds) + 16 * (at // RAW + 1))
                if at >= SPLIT or not isinstance(i, int):
                    act.wait_ge(tiles_used, i * per + (at - SPLIT + 1))
                nc.scalar.activation(w_hi[:, at % SPLIT, 0:width], raw[:, slot, 0:width],
                                     ACT.Copy).then_inc(hi_made, 1)

            def square_y(b, c, count):
                n = NORM[b]
                if c == 0:
                    nc.scalar.activation(stat[:, 44 + b:45 + b], eps_col, ACT.Sqrt)
                act.wait_ge(y_add[b - 1], count)
                for m in range(HALVES):
                    if c == COLS - 1 and m:
                        act.wait_ge(y_add[b - 1], count + 1)
                    if c or m:
                        act.wait_ge(n["ssq_y_made"], c * HALVES + m)
                    nc.scalar.activation(junk[:], y[:, m, c * NB:(c + 1) * NB], ACT.Square,
                                         accum_out=ssq_y[:, m, c:c + 1]).then_inc(n["ssq_y_made"], 1)

            def out_first(b, base, t):
                n = t // 2
                if t % 2 and n < 4:
                    act.wait_ge(tiles_used, base + t + 1)
                    nc.scalar.activation(y[:, :, n * NB:(n + 1) * NB], out_pair(b, n)[:],
                                         ACT.Copy).then_inc(y_add[b], 1)

            def root_y(b):
                act.wait_ge(NORM[b]["mean_y_made"], 1)
                nc.scalar.activation(rstd_y, mean_y, ACT.Sqrt).then_inc(NORM[b]["root_y_made"], 1)

            def high_u(b, t):
                n = NORM[b]
                if b == 0 and t == 0:
                    act.wait_ge(pre_in, 16)
                for m in range(HALVES):
                    u = HALVES * t + m
                    act.wait_ge(n["turned"], u + 1)
                    for j in range(KK):
                        k = KK * t + j
                        ins = nc.scalar.activation(u_hi[:, k, m * P:(m + 1) * P],
                                                   turn_bank[u % 4][:, j * P:(j + 1) * P], ACT.Copy,
                                                   scale=gain_pre[:, b, k:k + 1])
                    ins.then_inc(n["u_hi_made"], 1)

            def square_h(b, c):
                n = NORM[b]
                for m in range(HALVES):
                    q = c * HALVES + m
                    if b:
                        act.wait_ge(n["h_new"], q + 1)
                    else:
                        act.wait_ge(x_in[c], 16)
                    if q:
                        act.wait_ge(n["ssq_h_made"], q)
                    elif b:
                        act.wait_ge(n["ssq_y_made"], COLS * HALVES)
                    nc.scalar.activation(junk[:], h[:, m, c * NB:(c + 1) * NB], ACT.Square,
                                         accum_out=ssq_h[:, m, c:c + 1]).then_inc(n["ssq_h_made"], 1)

            def first_before(b, t):
                if t + 2 < KC // KK:
                    high_u(b, t + 2)
                if t == 7:
                    act.wait_ge(NORM[b]["rstd_u_made"], 1)

            def first_after(b, t, post):
                if t in (0, 1, 3, 5):
                    square_h(b, (t + 1) // 2)
                if t == 6:
                    act.wait_ge(NORM[b]["mean_h_made"], 1)
                    nc.scalar.activation(rstd_u, mean_h, ACT.Sqrt).then_inc(NORM[b]["root_h_made"], 1)
                    if b:
                        act.wait_ge(NORM[b]["gained"], COLS * HALVES)
                    act.dma_start(gain_post[:], post.partition_broadcast(P)).then_inc(post_in, 16)

            def att_evacuate(hd, g):
                pair = pairB if g == 1 else pairA
                for m in range(HALVES):
                    if m == 0:
                        act.wait_ge(a_half, hd * 3 + (g + 1))
                    else:
                        act.wait_ge(tiles_used, hd * ATT_TILES + (AT_ATT + (g + 1) * ATT_BLOCK_TILES))
                    nc.scalar.activation(az[:, m, 3 * g:3 * g + 3, :],
                                         pair[:, m, 0:ATT_W].rearrange("p (s n) -> p s n", s=3), ACT.Copy,
                                         scale=rstd_u[:, m:m + 1]).then_inc(a_evac, 1)

            def att_copy_v(hp):
                act.wait_ge(a_evac, hp * 6 + 6)
                for m in range(HALVES):
                    ins = nc.scalar.activation(a_v[:, m, :, :], az[:, m, 2:9:3, :], ACT.Copy)
                ins.then_inc(a_vcopied, 1)

            def att_copy_qk(hp, g):
                act.wait_ge(a_turned, hp * 3 + (g + 1))
                bank = bankO if g == 1 else bankX
                nc.scalar.activation(a_qkT[:, g, :], bank[:], ACT.Copy).then_inc(a_qk, 1)

            def att_exp(hp, m):
                act.wait_ge(a_maxed, hp * 2 + (2 - m))
                n = GROUPS * (m + 1) * P
                nc.scalar.activation(a_p[:, 0:n], a_p[:, 0:n], ACT.Exp, bias=a_max[:, m:m + 1],
                                     accum_out=a_sum[:, m:m + 1]).then_inc(a_probs, 1)

            def att_copy_pt(hp, m):
                act.wait_ge(a_pturned, hp * 2 + (2 - m))
                n = GROUPS * (m + 1) * P
                flat = pairS[:].rearrange("p m n -> p (m n)")
                nc.scalar.activation(a_pT[:, 0:n], flat[:, 0:n], ACT.Copy).then_inc(a_pt, 1)

            def att_output(hp, m):
                act.wait_ge(a_pv, hp * 2 + (2 - m))
                act.wait_ge(a_rs, hp * 2 + (2 - m))
                nc.scalar.activation(a_o[:, m, :], bankO[:, m * P:(m + 1) * P], ACT.Copy,
                                     scale=a_rsum[:, m:m + 1]).then_inc(a_out, 1)

            def att_high(hp):
                act.wait_ge(a_oturned, hp + 1)
                dst = c_hi[:, hp, :] if isinstance(hp, int) else c_hi[:, bass.ds(hp, 1), :].squeeze(1)
                nc.scalar.activation(dst, bankX[:, 0:TOK], ACT.Copy).then_inc(a_ohi, 1)

            def att_head(hd, prev, last=False):
                for t in range(ATT_TILES):
                    if prev is not None:
                        if t == 0:
                            att_copy_v(prev)
                        if t == 2:
                            att_copy_qk(prev, 0)
                            att_copy_qk(prev, 1)
                        if t == 3:
                            att_copy_qk(prev, 2)
                        if t == 6:
                            att_exp(prev, 1)
                        if t == 8:
                            att_copy_pt(prev, 1)
                        if t == 10:
                            att_output(prev, 1)
                        if t == 11:
                            att_exp(prev, 0)
                        if t == 13:
                            att_copy_pt(prev, 0)
                        if t == 15:
                            att_output(prev, 0)
                        if t == 17:
                            att_high(prev)
                    first_block = prev is None and t < ATT_BLOCK_TILES
                    if first_block:
                        first_before(0, t)
                    if prev is None and t == 13:
                        act.wait_ge(angle_ready, 1)
                        nc.scalar.activation(rope[:, 0, :, :], rope[:, 0, :, :], ACT.Sin)
                        nc.scalar.activation(rope[:, 1, :, :], rope[:, 1, :, :], ACT.Sin).then_inc(sines_ready, 1)
                    if prev is None and t == 14:
                        act.wait_ge(bexp_in, 1)
                        nc.scalar.activation(bounds[:, 1, :], bounds[:, 1, :], ACT.Exp).then_inc(bexp_out, 1)
                    if t % ATT_BLOCK_TILES == ATT_BLOCK_TILES - 1:
                        att_evacuate(hd, t // ATT_BLOCK_TILES)
                    into_next = last and t + SPLIT >= ATT_TILES
                    if first_block and t < 2:
                        for at in FIRST_SPLITS[t]:
                            high(at, 0, 0, KK * ATT_W)
                    else:
                        high(AT_ATT + t + SPLIT, hd, ATT_TILES, KK * (NB if into_next else ATT_W))
                    if first_block:
                        first_after(0, t, norm_gains[0, 1])

            high(0, 0, 0, KK * ATT_W)
            for t in range(2):
                high_u(0, t)
            high(1, 0, 0, KK * ATT_W)
            high(2, 0, 0, KK * ATT_W)
            att_head(0, None)
            with act.Fori(1, ATT_HEADS - 1) as hd:
                att_head(hd, hd - 1)
            att_head(ATT_HEADS - 1, ATT_HEADS - 2, last=True)
            hp = ATT_HEADS - 1
            for t in range(16):
                if t == 0:
                    att_copy_v(hp)
                if t == 1:
                    att_copy_qk(hp, 0)
                    att_copy_qk(hp, 1)
                if t == 2:
                    att_copy_qk(hp, 2)
                if t == 3:
                    att_exp(hp, 1)
                if t == 4:
                    att_copy_pt(hp, 1)
                if t == 5:
                    att_output(hp, 1)
                if t == 6:
                    att_exp(hp, 0)
                    att_copy_pt(hp, 0)
                if t == 7:
                    att_output(hp, 0)
                if t == 8:
                    att_high(hp)
                out_first(0, AT_ATT_OUT, t)
                if t < 15:
                    high(AT_ATT_OUT + t + SPLIT, 0, 0)
                if t in (9, 11, 13):
                    square_y(1, (t - 9) // 2, 5 + (t - 9) // 2)
            square_y(1, COLS - 1, 8)

            def hidden(layer, i, used):
                for m in range(HALVES):
                    if m == 0:
                        act.wait_ge(f_half[layer], i + 1)
                    else:
                        act.wait_ge(tiles_used, used)
                    nc.scalar.activation(m_h[:, m, :], pairA[:, m, :], ACT.Relu,
                                         scale=rstd_u[:, m:m + 1]).then_inc(f_relu[layer], 1)
                for m in range(HALVES):
                    act.wait_ge(f_relu[layer], i * 2 + (1 + m))
                    nc.scalar.activation(m_h[:, m, :], m_h[:, m, :], ACT.Square).then_inc(f_hid[layer], 1)

            def hidden_high(layer, i):
                for m in range(HALVES):
                    act.wait_ge(f_turned[layer], i * 2 + (1 + m))
                    bank = bankO if m else bankX
                    at = 4 * (isinstance(i, int) and i == FF_BLOCKS - 1)
                    nc.scalar.activation(hid_hi[:, at:at + 4, m * P:(m + 1) * P],
                                         bank[:].rearrange("p (k t) -> p k t", k=4),
                                         ACT.Copy).then_inc(f_hi[layer], 1)

            def mlp(layer, base):
                b = 1 + 2 * layer
                root_y(b)
                for t in range(2):
                    high_u(b, t)
                high(base + SPLIT - 1, 0, 0)
                for t in range(FF_TILES):
                    first_before(b, t)
                    if t == FF_TILES - 1:
                        hidden(layer, 0, base + FF_TILES)
                    high(base + t + SPLIT, 0, 0)
                    first_after(b, t, norm_gains[layer, 3])
                with act.Fori(0, FF_BLOCKS - 2) as i:
                    for t in range(2 * FF_TILES):
                        if t == 1:
                            hidden_high(layer, i)
                        if t == FF_TILES - 1:
                            hidden(layer, i + 1, i * (2 * FF_TILES) + (base + 2 * FF_TILES))
                        high(base + FF_TILES + t + SPLIT, i, 2 * FF_TILES)
                last = FF_BLOCKS - 1
                at = base + (2 * last - 1) * FF_TILES
                for t in range(2 * FF_TILES):
                    if t == 1:
                        hidden_high(layer, last - 1)
                    if t == FF_TILES - 1:
                        hidden(layer, last, at + FF_TILES)
                    if t == FF_TILES + 4:
                        hidden_high(layer, last)
                    high(at + t + SPLIT, 0, 0)
                for t in range(FF_TILES):
                    if t < FF_TILES - 1:
                        high(at + 2 * FF_TILES + t + SPLIT, 0, 0)
                        if t % 2:
                            square_y(b + 1, t // 2, 3 + 4 * last + t // 2)
                square_y(b + 1, COLS - 1, 2 + 4 * FF_BLOCKS)

            mlp(0, AT_FF0)

            def rec_evacuate(hd):
                for m in range(HALVES):
                    if m == 0:
                        act.wait_ge(r_half, hd + 1)
                        if not isinstance(hd, int) or hd > 0:
                            act.wait_ge(r_gate, hd)
                    else:
                        act.wait_ge(tiles_used, hd * REC_TILES + (AT_REC + REC_TILES))
                    nc.scalar.activation(rz[:, m, :], pairA[:, m, :], ACT.Copy,
                                         scale=rstd_u[:, m:m + 1]).then_inc(r_evac, 1)

            def rec_sigmoids(hp):
                act.wait_ge(r_qfT, hp + 1)
                nc.scalar.activation(r_sig, bankX[:, TOK:2 * TOK], ACT.Sigmoid).then_inc(r_sigs, 1)
                nc.scalar.activation(r_neg, bankX[:, TOK:2 * TOK], ACT.Sigmoid, scale=-1.0).then_inc(r_sigs, 1)
                nc.scalar.activation(r_q, bankX[:, 0:TOK].rearrange("p (m t) -> p m t", m=HALVES),
                                     ACT.Copy).then_inc(r_qcopied, 1)

            def rec_values(hp):
                act.wait_ge(r_evac, hp * 2 + 2)
                if not isinstance(hp, int) or hp > 0:
                    act.wait_ge(r_pv, hp)
                nc.scalar.activation(r_v, rz[:, :, 2 * P:3 * P], ACT.Copy).then_inc(r_vcopied, 1)
                nc.scalar.activation(r_sgate, rz[:, :, 3 * P:4 * P], ACT.Sigmoid).then_inc(r_sgated, 1)

            def rec_across(hp):
                act.wait_ge(r_scored, hp + 1)
                nc.scalar.activation(r_A[:, TOK:3 * P], pairB[:, 0, TOK:3 * P], ACT.Copy).then_inc(r_across, 1)

            def rec_squares(hp):
                act.wait_ge(r_pv, hp + 1)
                for m in range(HALVES):
                    if m or not isinstance(hp, int) or hp > 0:
                        act.wait_ge(r_ssq, hp * 2 + m)
                    nc.scalar.activation(junk[:, 0:P], bankO[:, m * P:(m + 1) * P], ACT.Square,
                                         accum_out=r_ms[:, m:m + 1]).then_inc(r_ssq, 1)

            def rec_high(hp):
                act.wait_ge(r_oturned, hp + 1)
                dst = c_hi[:, hp, :] if isinstance(hp, int) else c_hi[:, bass.ds(hp, 1), :].squeeze(1)
                nc.scalar.activation(dst, bankX[:, 0:TOK], ACT.Copy, scale=rgain[:, 0:1]).then_inc(r_ohi, 1)

            def rec_mix(t, front, back):
                if t == 0 and front is not None:
                    rec_sigmoids(front)
                if t == 1 and back is not None:
                    rec_squares(back)
                if t == 3 and front is not None:
                    rec_values(front)
                if t == 4 and back is not None:
                    rec_high(back)
                if t == 6 and front is not None:
                    rec_across(front)

            def rec_head(hd, front, back):
                for t in range(REC_TILES):
                    first_block = isinstance(hd, int) and hd == 0
                    if first_block:
                        first_before(2, t)
                    rec_mix(t, front, back)
                    if t == REC_TILES - 1:
                        rec_evacuate(hd)
                    high(AT_REC + t + SPLIT, hd, REC_TILES)
                    if first_block:
                        first_after(2, t, norm_gains[1, 1])

            root_y(2)
            for t in range(2):
                high_u(2, t)
            high(AT_REC + SPLIT - 1, 0, 0)
            act.wait_ge(rgain_in, 16)
            rec_head(0, None, None)
            rec_head(1, 0, None)
            with act.Fori(2, REC_HEADS) as hd:
                rec_head(hd, hd - 1, hd - 2)
            for t in range(32):
                if t < 8:
                    rec_mix(t, REC_HEADS - 1, REC_HEADS - 2)
                elif t < 16:
                    rec_mix(t - 8, None, REC_HEADS - 1)
                out_first(2, AT_REC_OUT, t)
                if t < 31:
                    high(AT_REC_OUT + t + SPLIT, 0, 0)
                if t in (25, 27, 29):
                    square_y(3, (t - 25) // 2, 13 + (t - 25) // 2)
            square_y(3, COLS - 1, 16)

            mlp(1, AT_FF1)
            root_y(4)

        @block.vector
        def _(dve):
            V = nc.vector

            def low(at, i, per, width=KK * NB):
                if isinstance(i, int) and i * per + at >= TILES:
                    return
                dve.wait_ge(hi_made, i * per + (at + 1))
                V.tensor_tensor(w_lo[:, at % SPLIT, 0:width], raw[:, at % RAW, 0:width],
                                w_hi[:, at % SPLIT, 0:width].bitcast(F32), ALU.subtract).then_inc(lo_made, 1)

            def gain_y(b, c, halves=range(HALVES)):
                n = NORM[b]
                cols = slice(c * NB, (c + 1) * NB)
                if c == 0:
                    dve.wait_ge(post_in, 16 * b)
                for m in halves:
                    dve.wait_ge(n["ssq_y_made"], HALVES * c + m + 1)
                    V.tensor_tensor(y[:, m, cols], y[:, m, cols], gain_post[:, cols],
                                    ALU.mult).then_inc(n["gained"], 1)

            def root_y(b):
                n = NORM[b]
                s = Steps(dve, n["steps"])
                gain_y(b, COLS - 1, [0])
                dve.wait_ge(n["ssq_y_made"], COLS * HALVES)
                s.link(V.tensor_reduce(mean_y, ssq_y, AX.X, ALU.add))
                V.tensor_scalar(mean_y, mean_y, 1.0 / D, EPS, ALU.mult, ALU.add).then_inc(n["mean_y_made"], 1)
                dve.wait_ge(n["root_y_made"], 1)
                s.link(V.reciprocal(rstd_y, rstd_y))

            def renew(b, c, halves=range(HALVES)):
                n = NORM[b]
                cols = slice(c * NB, (c + 1) * NB)
                for m in halves:
                    dve.wait_ge(n["gained"], HALVES * c + m + 1)
                    V.scalar_tensor_tensor(out=h[:, m, cols], in0=y[:, m, cols],
                                           scalar=rstd_y[:, m:m + 1], in1=h[:, m, cols],
                                           op0=ALU.mult, op1=ALU.add).then_inc(n["h_new"], 1)

            def low_u(b, t):
                n = NORM[b]
                if b == 0 and t == 0:
                    dve.wait_ge(pre_in, 16)
                for m in range(HALVES):
                    u = HALVES * t + m
                    dve.wait_ge(n["u_hi_made"], u + 1)
                    for j in range(KK):
                        k = KK * t + j
                        ins = V.scalar_tensor_tensor(out=u_lo[:, k, m * P:(m + 1) * P],
                                                     in0=turn_bank[u % 4][:, j * P:(j + 1) * P],
                                                     scalar=gain_pre[:, b, k:k + 1],
                                                     in1=u_hi[:, k, m * P:(m + 1) * P].bitcast(F32),
                                                     op0=ALU.mult, op1=ALU.subtract)
                    ins.then_inc(n["u_lo_made"], 1)

            def first_before(b, t):
                n = NORM[b]
                if t + 2 < KC // KK:
                    low_u(b, t + 2)
                if b and t in (1, 3):
                    renew(b, (t + 3) // 2)
                if t == 6:
                    s = Steps(dve, n["steps"], 2 if b else 0)
                    dve.wait_ge(n["ssq_h_made"], COLS * HALVES)
                    s.link(V.tensor_reduce(mean_h, ssq_h, AX.X, ALU.add))
                    V.tensor_scalar(mean_h, mean_h, 1.0 / D, EPS, ALU.mult, ALU.add).then_inc(n["mean_h_made"], 1)
                if t == 7:
                    dve.wait_ge(n["root_h_made"], 1)
                    V.reciprocal(rstd_u, rstd_u).then_inc(n["rstd_u_made"], 1)

            def first_blocks(b, at):
                renew(b, 0)
                gain_y(b, COLS - 1, [1])
                renew(b, 1, [0])
                for t in range(2):
                    low_u(b, t)
                renew(b, 1, [1])
                for t in range(2):
                    low(at + t, 0, 0)

            def setup_masks(s):
                dve.wait_ge(masks_ready, 1)
                dve.wait_ge(ident_ready, 1)
                onehot = carve(4608, 32)
                for g in range(GROUPS):
                    d = DILATION[g]
                    if d == 1:
                        continue
                    s.link(V.tensor_reduce(onehot[:, 0:d], ident[:].rearrange("p (b r) -> p r b", r=d),
                                           AX.X, ALU.add))
                    s.link(V.tensor_scalar(onehot[:, 0:d], onehot[:, 0:d], 1.0, -MASKED, ALU.subtract, ALU.mult))
                    view = amask[:, g, :].rearrange("p (b r) -> p b r", r=d)
                    s.link(V.tensor_tensor(view, view, onehot[:, None, 0:d].broadcast_to([P, TOK // d, d]),
                                           ALU.add))

            inv = carve(4640, HALF_ROPE)
            posf = carve(4672, HALVES)
            ang = carve(4704, HALVES, HALF_ROPE)
            turns = carve(4736, HALVES, HALF_ROPE)

            def setup_angles(s):
                half = HALF_ROPE
                freq = np.float32(ROPE_THETA) ** (-np.arange(half, dtype=np.float32) / np.float32(half))
                dve.wait_ge(pos_in, 16)
                s.note(V.tensor_copy(posf, pos_i[:]))
                for j in range(half):
                    s.note(V.memset(inv[:, j:j + 1], float(freq[j])))
                s.last()
                for m in range(HALVES):
                    s.note(V.tensor_scalar(ang[:, m, :], inv, posf[:, m:m + 1], None, ALU.mult))
                s.last()

            def setup_range(s):
                two_pi = 2 * np.pi
                part1 = 6.28125
                part2 = float(np.float32(np.round((two_pi - part1) * 2 ** 21) / 2 ** 21))
                part3 = float(np.float32(two_pi - part1 - part2))
                magic = 1.5 * 2 ** 23
                s.link(V.tensor_scalar(turns, ang, float(np.float32(1 / two_pi)), None, ALU.mult))
                s.link(V.tensor_scalar(turns, turns, magic, None, ALU.add))
                s.link(V.tensor_scalar(turns, turns, magic, None, ALU.subtract))
                for part in (part1, part2, part3):
                    s.link(V.scalar_tensor_tensor(out=ang, in0=turns, scalar=-part, in1=ang,
                                                  op0=ALU.mult, op1=ALU.add))
                pi = 3.1415925
                s.link(V.tensor_scalar(ang, ang, pi, -pi, ALU.min, ALU.max))
                s.note(V.tensor_scalar(rope[:, 0, :, :], ang, 0.5, None, ALU.mult))
                V.tensor_copy(rope[:, 1, :, :], ang).then_inc(angle_ready, 1)
                dve.wait_ge(bound_in, 16)
                V.tensor_tensor(bounds[:, 1, :], bounds[:, 0, :], bounds[:, 0, :],
                                ALU.subtract).then_inc(bexp_in, 1)

            def setup_cosines(s):
                dve.wait_ge(sines_ready, 1)
                s.link(V.tensor_tensor(rope[:, 0, :, :], rope[:, 0, :, :], rope[:, 0, :, :], ALU.mult))
                V.tensor_scalar(rope[:, 0, :, :], rope[:, 0, :, :], -2.0, 1.0, ALU.mult,
                                ALU.add).then_inc(rope_ready, 1)
                dve.wait_ge(rope_ready, 1)

            def setup_bounds(s):
                dve.wait_ge(bexp_out, 1)
                s.link(V.reciprocal(bounds[:, 2, :], bounds[:, 1, :]))
                s.link(V.tensor_tensor(bounds[:, 1, :], bounds[:, 1, :], bounds[:, 2, :], ALU.mult))
                s.link(V.tensor_tensor(bounds[:, 1, :], bounds[:, 1, :], bounds[:, 1, :], ALU.subtract))
                s.note(V.tensor_scalar(bounds[:, 2, :], bounds[:, 1, :], LB_FLOOR, None, ALU.max))
                s.link(V.tensor_scalar(bounds[:, 3, :], bounds[:, 1, :], -1.0, 1.0, ALU.mult, ALU.add))
                s.link(V.tensor_tensor(bounds[:, 4, :], bounds[:, 2, :], bounds[:, 1, :], ALU.subtract))

            def att_rotate(hp, s):
                dve.wait_ge(a_evac, hp * 6 + 6)
                cosx = a_cosx.rearrange("p (s j i) -> p s j i", s=9, j=2)
                sinx = a_sinx.rearrange("p (s j i) -> p s j i", s=9, j=2)
                for m in range(HALVES):
                    src = az[:, m, :, 0:32].rearrange("p s (j i) -> p s j i", j=2)
                    cos = rope[:, 0, m, :][:, None, None, :].broadcast_to([P, 9, 2, HALF_ROPE])
                    sin = rope[:, 1, m, :][:, None, None, :].broadcast_to([P, 9, 2, HALF_ROPE])
                    s.note(V.tensor_tensor(cosx, src, cos, ALU.mult))
                    s.note(V.tensor_tensor(sinx, src, sin, ALU.mult))
                    s.last()

                    def qk(view):
                        return view.rearrange("p (g s) i -> p g s i", g=GROUPS)[:, :, 0:2, :]

                    s.note(V.tensor_tensor(qk(az[:, m, :, 0:16]), qk(cosx[:, :, 0, :]), qk(sinx[:, :, 1, :]),
                                           ALU.subtract))
                    ins = V.tensor_tensor(qk(az[:, m, :, 16:32]), qk(cosx[:, :, 1, :]), qk(sinx[:, :, 0, :]),
                                          ALU.add)
                    if m == 0:
                        s.link(ins)
                    else:
                        ins.then_inc(a_rot, 1)

            def att_mask(hp, m, s):
                dve.wait_ge(a_scored, hp * 2 + (2 - m))
                n = (m + 1) * P
                flat = pairS[:].rearrange("p m n -> p (m n)")[:, 0:GROUPS * n]
                s.link(V.scalar_tensor_tensor(
                    out=a_p[:, 0:GROUPS * n].rearrange("p (g n) -> p g n", g=GROUPS),
                    in0=flat.rearrange("p (g n) -> p g n", g=GROUPS), scalar=float(P) ** -0.5,
                    in1=amask[:, :, TOK - n:TOK], op0=ALU.mult, op1=ALU.add))
                s.link(V.tensor_reduce(a_max[:, m:m + 1], a_p[:, 0:GROUPS * n], AX.X, ALU.max))
                V.tensor_scalar(a_max[:, m:m + 1], a_max[:, m:m + 1], -1.0, None,
                                ALU.mult).then_inc(a_maxed, 1)

            def att_rsum(hp, m):
                dve.wait_ge(a_probs, hp * 2 + (2 - m))
                V.reciprocal(a_rsum[:, m:m + 1], a_sum[:, m:m + 1]).then_inc(a_rs, 1)

            def att_low(hp):
                dve.wait_ge(a_ohi, hp + 1)
                if isinstance(hp, int):
                    hi, lo = c_hi[:, hp, :], c_lo[:, hp, :]
                else:
                    hi, lo = c_hi[:, bass.ds(hp, 1), :].squeeze(1), c_lo[:, bass.ds(hp, 1), :].squeeze(1)
                V.tensor_tensor(lo, bankX[:, 0:TOK], hi.bitcast(F32), ALU.subtract).then_inc(a_olo, 1)

            ATT_STEPS = 11

            def att_head(hd, prev, last=False):
                s = Steps(dve, a_steps, None if prev is None else prev * ATT_STEPS)
                setup = Steps(dve, v_setup)
                for t in range(ATT_TILES):
                    if prev is None and t < ATT_BLOCK_TILES:
                        first_before(0, t)
                    if prev is None and 9 <= t < 17 and t != 12 and t != 13 and t != 14:
                        {9: setup_masks, 10: setup_angles, 11: setup_range, 15: setup_cosines,
                         16: setup_bounds}[t](setup)
                    if prev is not None:
                        if t == 0:
                            att_rotate(prev, s)
                        if t == 5:
                            att_mask(prev, 1, s)
                        if t == 7:
                            att_rsum(prev, 1)
                        if t == 10:
                            att_mask(prev, 0, s)
                        if t == 12:
                            att_rsum(prev, 0)
                        if t == 17:
                            att_low(prev)
                    into_next = last and t + SPLIT >= ATT_TILES
                    if prev is None and t < 2:
                        for at in FIRST_SPLITS[t]:
                            low(at, 0, 0, KK * ATT_W)
                    else:
                        low(AT_ATT + t + SPLIT, hd, ATT_TILES, KK * (NB if into_next else ATT_W))
                assert prev is None or s.count == ATT_STEPS, s.count

            def add_y(b, c, pair, used, before, half=None, between=None):
                dst = y[:, :, c * NB:(c + 1) * NB]
                if before is not None:
                    dve.wait_ge(y_add[b], before)
                if half is not None:
                    dve.wait_ge(*half)
                    V.tensor_tensor(dst[:, 0, :], dst[:, 0, :], pair[:, 0, :], ALU.add).then_inc(y_add[b], 1)
                    between()
                    dve.wait_ge(tiles_used, used)
                    V.tensor_tensor(dst[:, 1, :], dst[:, 1, :], pair[:, 1, :], ALU.add).then_inc(y_add[b], 1)
                    return
                dve.wait_ge(tiles_used, used)
                V.tensor_tensor(dst, dst, pair[:], ALU.add).then_inc(y_add[b], 1)

            def out_add(b, base, t, half=None, between=None):
                n = t // 2
                if t % 2 and n >= 4:
                    add_y(b, n % 4, out_pair(b, n), base + t + 1, n, half,
                          between)

            low(0, 0, 0, KK * ATT_W)
            for t in range(2):
                low_u(0, t)
            low(1, 0, 0, KK * ATT_W)
            low(2, 0, 0, KK * ATT_W)
            att_head(0, None)
            with dve.Fori(1, ATT_HEADS - 1) as hd:
                att_head(hd, hd - 1)
            att_head(ATT_HEADS - 1, ATT_HEADS - 2, last=True)
            hp = ATT_HEADS - 1
            s = Steps(dve, a_steps, hp * ATT_STEPS)
            for t in range(16):
                if t == 0:
                    att_rotate(hp, s)
                if t == 2:
                    att_mask(hp, 1, s)
                if t == 4:
                    att_rsum(hp, 1)
                if t == 5:
                    att_mask(hp, 0, s)
                if t == 6:
                    att_rsum(hp, 0)
                if t == 8:
                    att_low(hp)
                if t < 14:
                    out_add(0, AT_ATT_OUT, t)
                    low(AT_ATT_OUT + t + SPLIT, 0, 0)
                if t == 11:
                    gain_y(1, 0)
                if t == 14:
                    gain_y(1, 1)
                    gain_y(1, 2, [0])
                if t == 15:
                    out_add(0, AT_ATT_OUT, t, (a_half, 3 * ATT_HEADS + 1), lambda: gain_y(1, 2, [1]))

            def hidden_low(layer, i):
                for m in range(HALVES):
                    dve.wait_ge(f_hi[layer], i * 2 + (1 + m))
                    bank = bankO if m else bankX
                    at = 4 * (isinstance(i, int) and i == FF_BLOCKS - 1)
                    V.tensor_tensor(hid_lo[:, at:at + 4, m * P:(m + 1) * P],
                                    bank[:].rearrange("p (k t) -> p k t", k=4),
                                    hid_hi[:, at:at + 4, m * P:(m + 1) * P].bitcast(F32),
                                    ALU.subtract).then_inc(f_lo[layer], 1)

            def mlp(layer, base):
                b = 1 + 2 * layer
                root_y(b)
                first_blocks(b, base + SPLIT - 2)
                for t in range(FF_TILES):
                    first_before(b, t)
                    low(base + t + SPLIT, 0, 0)
                with dve.Fori(0, FF_BLOCKS - 2) as i:
                    for t in range(2 * FF_TILES):
                        if t == 1:
                            hidden_low(layer, i)
                        if t >= FF_TILES and t % 2:
                            c = (t - FF_TILES) // 2
                            add_y(b, c, pairS if c % 2 else pairB,
                                  i * (2 * FF_TILES) + (base + FF_TILES + t + 1), i * 4 + (c + 2))
                        low(base + FF_TILES + t + SPLIT, i, 2 * FF_TILES)
                last = FF_BLOCKS - 1
                at = base + (2 * last - 1) * FF_TILES
                for t in range(2 * FF_TILES):
                    if t == 1:
                        hidden_low(layer, last - 1)
                    if t == FF_TILES + 4:
                        hidden_low(layer, last)
                    if t >= FF_TILES and t % 2:
                        c = (t - FF_TILES) // 2
                        add_y(b, c, pairS if c % 2 else pairB, at + t + 1, (last - 1) * 4 + c + 2)
                    low(at + t + SPLIT, 0, 0)
                at += 2 * FF_TILES
                for t in range(FF_TILES):
                    if t % 2:
                        c = t // 2
                        add_y(b, c, pairS if c % 2 else pairB, at + t + 1, 4 * last + c + 2,
                              (f_half[layer], FF_BLOCKS + 1) if t == FF_TILES - 1 else None,
                              lambda: gain_y(b + 1, 2, [1]))
                    if t < FF_TILES - 2:
                        low(at + t + SPLIT, 0, 0)
                    if t == 3:
                        gain_y(b + 1, 0)
                    if t == 6:
                        gain_y(b + 1, 1)
                        gain_y(b + 1, 2, [0])

            mlp(0, AT_FF0)

            REC_FRONT_STEPS = 2 + 5 * (LEVELS - 1) + 2 + MASK_LEVELS - 1
            ROOT_OPS = 3 + 3 * 3
            REC_BACK_STEPS = ROOT_OPS

            def rec_gates(hp, s):
                def col(row):
                    return bounds[:, row, hp:hp + 1] if isinstance(hp, int) else bounds[:, row, bass.ds(hp, 1)]
                dve.wait_ge(r_sigs, hp * 2 + 1)
                s.note(V.tensor_scalar(r_f, r_sig, col(3), col(2), ALU.mult, ALU.add))
                dve.wait_ge(r_sigs, hp * 2 + 2)
                s.note(V.tensor_scalar(r_K[:, 0, :], r_neg, col(3), col(4), ALU.mult, ALU.subtract))

            def rec_level(hp, s, j, root_op):
                if j == 0:
                    s.last()
                else:
                    s.reach(s.count - 2)
                w, nb = 1 << j, TOK >> (j + 1)

                def halves(v):
                    return v.rearrange("p (b two w) -> p b two w", two=2, w=w)

                def decayed_queries():
                    if j == LEVELS - 1:
                        return V.tensor_tensor(r_R[j].rearrange("p m t -> p (m t)"), r_q[:, 1, :], r_f[:, P:],
                                               ALU.mult)

                    def right(v):
                        return v.rearrange("p m (b two w) -> p m b two w", two=2, w=w)[:, :, :, 1, :]

                    return V.tensor_tensor(r_R[j].rearrange("p m (b w) -> p m b w", w=w), right(r_q),
                                           right(r_f.rearrange("p (m t) -> p m t", m=HALVES)), ALU.mult)

                f, k = halves(r_f), halves(r_K[:, j, :])
                if j == LEVELS - 1:
                    s.last()
                    decayed_queries().then_inc(r_levels, 1)
                    return
                at = 0 if j == 0 else TOK - (TOK >> (j - 1))
                tot = (r_f if j == 0 else r_tot[:, at:at + 2 * nb]).rearrange("p (b two) -> p b two", two=2)
                k_next = halves(r_K[:, j + 1, :])
                root_op(0)
                s.note(V.tensor_tensor(k_next[:, :, 0, :], k[:, :, 0, :],
                                       tot[:, :, 1:2].broadcast_to([P, nb, w]), ALU.mult))
                root_op(1)
                s.note(V.tensor_copy(k_next[:, :, 1, :], k[:, :, 1, :]))
                root_op(2)
                at_next = TOK - (TOK >> j)
                s.note(V.tensor_tensor(r_tot[:, at_next:at_next + nb], tot[:, :, 0], tot[:, :, 1], ALU.mult))
                root_op(3)
                if j == 0:
                    dve.wait_ge(r_qcopied, hp + 1)
                else:
                    s.reach(s.count - 3)
                s.note(decayed_queries())
                root_op(4)
                s.note(V.tensor_tensor(f[:, :, 1, :], f[:, :, 1, :],
                                       tot[:, :, 0:1].broadcast_to([P, nb, w]), ALU.mult))
                root_op(5)

            def rec_assemble(hp, s):
                dve.wait_ge(r_scored, hp + 1)
                s.link(V.tensor_tensor(r_prod, pairS[:, :, 0:SCORES],
                                       rmask[:, None, :].broadcast_to([P, HALVES, SCORES]), ALU.mult))
                rows = r_A[:, 0:TOK]
                dve.wait_ge(r_across, hp + 1)
                s.link(V.tensor_tensor(rows.rearrange("p (m t) -> p m t", m=HALVES),
                                       pairB[:, 0, 0:TOK].rearrange("p (m t) -> p m t", m=HALVES),
                                       r_prod[:, :, at_diagonal:at_diagonal + P], ALU.add))
                for j in range(MASK_LEVELS):
                    w = 1 << j
                    dst = rows.rearrange("p (m b two w) -> p m b two w", m=HALVES, two=2, w=w)[:, :, :, 1, :]
                    ins = V.tensor_tensor(dst, dst, r_prod[:, :, at_level[j]:at_level[j] + P // 2].rearrange(
                        "p m (b w) -> p m b w", w=w), ALU.add)
                    if j < MASK_LEVELS - 1:
                        s.link(ins)
                ins.then_inc(r_att, 1)

            def rec_gate_out(hp):
                dve.wait_ge(r_sgated, hp + 1)
                V.tensor_tensor(r_G, r_sgate, rz[:, :, 3 * P:4 * P], ALU.mult).then_inc(r_gate, 1)

            def rec_root(hp, s, op):
                if op == 0:
                    dve.wait_ge(r_ssq, hp * 2 + 2)
                    s.note(V.tensor_scalar(r_x, r_ms, 1.0 / P, EPS, ALU.mult, ALU.add))
                    return
                s.last()
                if op == 1:
                    s.note(V.tensor_scalar(r_t.bitcast(I32), r_x.bitcast(I32), 1, None, ALU.logical_shift_right))
                elif op == 2:
                    s.note(V.tensor_scalar(r_rs.bitcast(I32), r_t.bitcast(I32), -1.0, float(0x5F3759DF),
                                           ALU.mult, ALU.add))
                elif op % 3 == 0:
                    s.note(V.scalar_tensor_tensor(out=r_t, in0=r_rs, scalar=-0.5, in1=r_x,
                                                  op0=ALU.mult, op1=ALU.mult))
                elif op % 3 == 1:
                    s.note(V.tensor_tensor(r_t, r_t, r_rs, ALU.mult))
                else:
                    s.note(V.scalar_tensor_tensor(out=r_rs, in0=r_t, scalar=1.5, in1=r_rs,
                                                  op0=ALU.add, op1=ALU.mult))

            def rec_output(hp, s):
                s.last()
                dve.wait_ge(r_gate, hp + 1)
                for m in range(HALVES):
                    ins = V.scalar_tensor_tensor(out=r_o[:, m, :], in0=bankO[:, m * P:(m + 1) * P],
                                                 scalar=r_rs[:, m:m + 1], in1=r_G[:, m, :],
                                                 op0=ALU.mult, op1=ALU.mult)
                ins.then_inc(r_out, 1)

            def rec_low(hp):
                dve.wait_ge(r_ohi, hp + 1)
                if isinstance(hp, int):
                    hi, lo = c_hi[:, hp, :], c_lo[:, hp, :]
                else:
                    hi, lo = c_hi[:, bass.ds(hp, 1), :].squeeze(1), c_lo[:, bass.ds(hp, 1), :].squeeze(1)
                V.scalar_tensor_tensor(out=lo, in0=bankX[:, 0:TOK], scalar=rgain[:, 0:1], in1=hi.bitcast(F32),
                                       op0=ALU.mult, op1=ALU.subtract).then_inc(r_olo, 1)

            def rec_mix(t, front, back, sf, sb_):
                if t == 0 and front is not None:
                    rec_gates(front, sf)
                if 1 <= t <= 4 and front is not None:
                    for j in (2 * t - 2, 2 * t - 1):
                        rec_level(front, sf, j, lambda k: rec_root(back, sb_, 6 * j + k)
                                  if t == 1 and back is not None else None)
                elif t == 1 and back is not None:
                    for op in range(ROOT_OPS):
                        rec_root(back, sb_, op)
                if t == 1 and back is not None:
                    rec_output(back, sb_)
                if t == 5 and front is not None:
                    rec_gate_out(front)
                if t == 5 and back is not None:
                    rec_low(back)
                if t == 6 and front is not None:
                    rec_assemble(front, sf)

            def rec_head(hd, front, back):
                sf = Steps(dve, r_front_steps, None if front is None else front * REC_FRONT_STEPS)
                sb_ = Steps(dve, r_back_steps, None if back is None else back * REC_BACK_STEPS)
                for t in range(REC_TILES):
                    if isinstance(hd, int) and hd == 0:
                        first_before(2, t)
                    if isinstance(hd, int) and hd == 0 and t == 7:
                        V.memset(pairB[:, 0, :], 0.0).then_inc(zmem, 1)
                        dve.wait_ge(zmem, 1)
                        V.memset(r_A, 0.0).then_inc(r_olo, 1)
                    rec_mix(t, front, back, sf, sb_)
                    if t != 3:
                        for at in ([3, 4] if t == 4 else [t]):
                            low(AT_REC + at + SPLIT, hd, REC_TILES)
                assert front is None or sf.count == REC_FRONT_STEPS, sf.count
                assert back is None or sb_.count == REC_BACK_STEPS, sb_.count

            root_y(2)
            first_blocks(2, AT_REC + SPLIT - 2)
            dve.wait_ge(rgain_in, 16)
            rec_head(0, None, None)
            rec_head(1, 0, None)
            with dve.Fori(2, REC_HEADS) as hd:
                rec_head(hd, hd - 1, hd - 2)
            last_head = REC_HEADS - 1
            sf = Steps(dve, r_front_steps, last_head * REC_FRONT_STEPS)
            for t in range(32):
                if t == 0:
                    sb_ = Steps(dve, r_back_steps, (last_head - 1) * REC_BACK_STEPS)
                if t == 8:
                    sb_ = Steps(dve, r_back_steps, last_head * REC_BACK_STEPS)
                if t < 8:
                    rec_mix(t, last_head, last_head - 1, sf, sb_)
                elif t < 16:
                    rec_mix(t - 8, None, last_head, None, sb_)
                if t < 31:
                    out_add(2, AT_REC_OUT, t)
                if t < 30:
                    low(AT_REC_OUT + t + SPLIT, 0, 0)
                if t == 27:
                    gain_y(3, 0)
                if t == 30:
                    gain_y(3, 1)
                    gain_y(3, 2, [0])
                if t == 31:
                    out_add(2, AT_REC_OUT, t, (r_half, REC_HEADS + 1), lambda: gain_y(3, 2, [1]))

            mlp(1, AT_FF1)
            root_y(4)
            for c in range(COLS):
                if c == COLS - 1:
                    gain_y(4, c, [1])
                renew(4, c)


def _tiles_by_head(w, groups, parts, heads):
    a = w.reshape(KC // KK, KK, P, groups, parts, heads, P)
    a = a.transpose(5, 3, 0, 2, 1, 4, 6)
    return np.ascontiguousarray(a).reshape(heads * groups * (KC // KK), P, KK * parts * P)


def _tiles_up(w):
    a = w.reshape(2, KC // KK, KK, P, FF_BLOCKS, NB).transpose(0, 4, 1, 3, 2, 5)
    return np.ascontiguousarray(a).reshape(-1, P, KK * NB)


def _tiles_down(w):
    a = w.reshape(-1, 2, KK, P, COLS, NB).transpose(0, 4, 1, 3, 2, 5)
    return np.ascontiguousarray(a).reshape(-1, P, KK * NB)


def kernel(**inputs):
    import concourse.bacc as _bacc
    from concourse.bass_utils import run_bass_kernel_spmd as _run

    a = {k: np.asarray(v) for k, v in inputs.items()}
    arrays = {
        "x": a["x"][0],
        "positions": np.ascontiguousarray(a["positions"].reshape(HALVES, P).T),
        "norm_gains": a["norm_gains"],
        "pre_gains": np.ascontiguousarray(a["norm_gains"][:, ::2].reshape(4, KC, P).transpose(2, 0, 1)),
        "lower_bound": np.ascontiguousarray(a["rec_lower_bounds"].reshape(REC_HEADS, P).T),
        "rec_gain": np.ascontiguousarray(a["rec_out_norm"].reshape(P, 1)),
        "s_att_in": _tiles_by_head(a["w_att_in"][0], GROUPS, 3, ATT_HEADS),
        "s_att_out": _tiles_down(a["w_att_out"]),
        "s_rec_in": _tiles_by_head(a["w_rec_in"][0], 1, 4, REC_HEADS),
        "s_rec_out": _tiles_down(a["w_rec_out"]),
        "s_up": _tiles_up(a["w_ff1"]),
        "s_down": _tiles_down(a["w_ff2"]),
    }
    nc = _bacc.Bacc("TRN2", target_bir_lowering=False, num_devices=1)
    args = [nc.dram_tensor("in_" + k, v.shape, mybir.dt.from_np(v.dtype), kind="ExternalInput").ap()
            for k, v in arrays.items()]
    out = nc.dram_tensor("out_h", (TOK, D), F32, kind="ExternalOutput").ap()
    hybrid_trunk(nc, *args, out)
    r = _run(nc, [{"in_" + k: np.ascontiguousarray(v) for k, v in arrays.items()}], core_ids=[0])
    return r.results[0]["out_h"].reshape(1, TOK, D)
```
